# Optimizing a Trainium2 kernel written in Bass

```python
import math
import jax, jax.numpy as jnp
from jax import lax
import numpy as np

D_MODEL = 1024
BATCH = 1
SEQ = 256
DEPTH = 1

HEAD_DIM = 64
RWKV_HEADS = 12
RWKV_WIDTH = RWKV_HEADS * HEAD_DIM
DECAY_LORA = 64
ICLR_LORA = 64
GATE_LORA = 128
ATTN_GROUPS = ((128, 1), (512, 4), (2048, 16))
HEADS_PER_GROUP = 4
ATTN_HEADS = HEADS_PER_GROUP * len(ATTN_GROUPS)
ATTN_WIDTH = ATTN_HEADS * HEAD_DIM
ATTN_OUT_WIDTH = HEADS_PER_GROUP * HEAD_DIM
ATTN_BLOCK = 128
ROPE_THETA = 10000.0
D_FF = -(-8 * D_MODEL // (3 * 256)) * 256
SHIFT_WIDTH = 3 * RWKV_WIDTH + DECAY_LORA + ICLR_LORA + GATE_LORA
IN_WIDTH = SHIFT_WIDTH + 3 * ATTN_WIDTH + 2 * D_MODEL
NORM_EPS = 1e-6
GN_EPS = 64e-5


def _split(t, sizes):
    idx = np.cumsum(sizes)[:-1].tolist()
    return jnp.split(t, idx, axis=-1)

def rms_norm(x, g):
    xf = x.astype(jnp.float32)
    y = xf * lax.rsqrt(jnp.mean(xf * xf, axis=-1, keepdims=True) + NORM_EPS)
    return (y * g.astype(jnp.float32)).astype(x.dtype)

def modulate(h, shift, scale):
    return h * (1.0 + scale[:, None, :]) + shift[:, None, :]

def token_shift(p):
    return jnp.pad(p, ((0, 0), (1, 0), (0, 0)))[:, :-1]

def apply_rope(t, pos):
    half = t.shape[-1] // 2
    inv_freq = ROPE_THETA ** (-jnp.arange(half, dtype=jnp.float32) / half)
    ang = pos.astype(jnp.float32)[:, None] * inv_freq[None, :]
    cos, sin = jnp.cos(ang), jnp.sin(ang)
    tf = t.astype(jnp.float32)
    t1, t2 = tf[..., :half], tf[..., half:]
    return jnp.concatenate([t1 * cos - t2 * sin, t2 * cos + t1 * sin], axis=-1).astype(t.dtype)

def rwkv7_recurrence(r, w, k, v, kk, a):
    B, S, H, N = r.shape

    def step(state, inp):
        r_t, w_t, k_t, v_t, kk_t, a_t = inp
        sa = -jnp.einsum('bhvk,bhk->bhv', state, kk_t)
        state = (state * w_t[:, :, None, :]
                 + sa[..., None] * (kk_t * a_t)[:, :, None, :]
                 + v_t[..., None] * k_t[:, :, None, :])
        y = jnp.einsum('bhvk,bhk->bhv', state, r_t)
        return state, y

    xs = tuple(jnp.moveaxis(t.astype(jnp.float32), 1, 0) for t in (r, w, k, v, kk, a))
    init = jnp.zeros((B, H, N, N), jnp.float32)
    _, ys = lax.scan(step, init, xs)
    return jnp.moveaxis(ys, 0, 1)

def rwkv7_mix(pr, pk, pv, pw, pa, pg, w0, w2, a0, a2, g2, k_k, k_a, r_k, lnx_w, lnx_b, w_a):
    B, S, _ = pr.shape
    f32 = jnp.float32
    heads = lambda t: t.reshape(B, S, RWKV_HEADS, HEAD_DIM)
    wf = (w0 + jnp.tanh(pw) @ w2).astype(f32)
    decay = jnp.exp(-jnp.exp(-jax.nn.softplus(-wf) - 0.5))
    a = jax.nn.sigmoid((a0 + pa @ a2).astype(f32))
    gate = (jax.nn.sigmoid(pg) @ g2).astype(f32)
    kk = heads((pk * k_k).astype(f32))
    kk = kk / jnp.maximum(jnp.linalg.norm(kk, axis=-1, keepdims=True), 1e-12)
    k = pk.astype(f32) * (1.0 + (a - 1.0) * k_a.astype(f32))
    rf, vf = heads(pr.astype(f32)), heads(pv.astype(f32))
    y = rwkv7_recurrence(rf, heads(decay), heads(k), vf, kk, heads(a))
    mean = jnp.mean(y, axis=-1, keepdims=True)
    var = jnp.mean(jnp.square(y - mean), axis=-1, keepdims=True)
    yn = ((y - mean) * lax.rsqrt(var + GN_EPS)).reshape(B, S, RWKV_WIDTH)
    yn = yn * lnx_w.astype(f32) + lnx_b.astype(f32)
    bonus = (jnp.sum(rf * heads(k) * r_k.astype(f32), axis=-1, keepdims=True) * vf).reshape(B, S, RWKV_WIDTH)
    return ((yn + bonus) * gate).astype(pr.dtype) @ w_a

def dilated_window_attn(q, k, v, window, dilation):
    B, H, S, hd = q.shape
    span = window // dilation
    n_prev = -(-span // ATTN_BLOCK)
    chunk = dilation * ATTN_BLOCK
    s_pad = -(-S // chunk) * chunk
    L = s_pad // dilation
    nb = L // ATTN_BLOCK

    def to_blocks(t):
        t = jnp.pad(t, ((0, 0), (0, 0), (0, s_pad - S), (0, 0)))
        t = t.reshape(B, H, L, dilation, hd).transpose(0, 1, 3, 2, 4)
        return t.reshape(B, H, dilation, nb, ATTN_BLOCK, hd)

    def with_prev(t):
        padded = jnp.pad(t, ((0, 0), (0, 0), (0, 0), (n_prev, 0), (0, 0), (0, 0)))
        return jnp.concatenate([padded[:, :, :, i:i + nb] for i in range(n_prev + 1)], axis=4)

    qb, kb, vb = to_blocks(q), to_blocks(k), to_blocks(v)
    kc, vc = with_prev(kb), with_prev(vb)
    s = jnp.einsum('bhrnqd,bhrnkd->bhrnqk', qb, kc, preferred_element_type=jnp.float32)
    s = s * (HEAD_DIM ** -0.5)
    n_keys = (n_prev + 1) * ATTN_BLOCK
    qi = jnp.arange(ATTN_BLOCK)[:, None]
    kj = jnp.arange(n_keys)[None, :]
    dist = qi + n_prev * ATTN_BLOCK - kj
    key_pos = jnp.arange(nb)[:, None, None] * ATTN_BLOCK + kj[None] - n_prev * ATTN_BLOCK
    valid = (dist >= 0) & (dist <= span) & (key_pos >= 0)
    s = jnp.where(valid, s, -jnp.inf)
    lse = jax.nn.logsumexp(s, axis=-1)
    p = jnp.exp(s - lse[..., None])
    o = jnp.einsum('bhrnqk,bhrnkd->bhrnqd', p, vc.astype(jnp.float32))
    o = o.reshape(B, H, dilation, L, hd).transpose(0, 1, 3, 2, 4).reshape(B, H, s_pad, hd)[:, :, :S]
    lse = lse.reshape(B, H, dilation, L).transpose(0, 1, 3, 2).reshape(B, H, s_pad)[:, :, :S]
    return o, lse

def dilated_attention_mix(pq, pk, pv, w_b):
    B, S, _ = pq.shape
    heads = lambda t: t.reshape(B, S, ATTN_HEADS, HEAD_DIM).transpose(0, 2, 1, 3)
    pos = jnp.arange(S)
    q, k, v = apply_rope(heads(pq), pos), apply_rope(heads(pk), pos), heads(pv)
    outs, lses = [], []
    for g, (window, dilation) in enumerate(ATTN_GROUPS):
        sl = slice(g * HEADS_PER_GROUP, (g + 1) * HEADS_PER_GROUP)
        o, l = dilated_window_attn(q[:, sl], k[:, sl], v[:, sl], window, dilation)
        outs.append(o)
        lses.append(l)
    outs = jnp.stack(outs)
    wts = jax.nn.softmax(jnp.stack(lses), axis=0)
    o = jnp.sum(wts[..., None] * outs, axis=0)
    o = o.transpose(0, 2, 1, 3).reshape(B, S, ATTN_OUT_WIDTH).astype(pq.dtype)
    return o @ w_b

def first_inputs(seed: int = 0) -> dict:
    key = jax.random.key(seed)
    ks = iter(jax.random.split(key, 32))
    f32 = jnp.float32
    nrm = lambda shape, sc: jax.random.normal(next(ks), shape, f32) * sc
    L, D, RW = DEPTH, D_MODEL, RWKV_WIDTH
    return {
        "x": nrm((BATCH, SEQ, D), 1.0),
        "c": nrm((BATCH, D), 1.0),
        "w_ada": nrm((L, D, 6 * D), 0.5 * D ** -0.5),
        "b_ada": nrm((L, 6 * D), 0.02),
        "g_pre_mix": 1.0 + nrm((L, D), 0.05),
        "g_post_mix": 1.0 + nrm((L, D), 0.05),
        "w_in": nrm((L, D, IN_WIDTH), D ** -0.5),
        "mu_shift": jax.random.uniform(next(ks), (L, SHIFT_WIDTH), f32, 0.0, 1.0),
        "w0": jax.random.uniform(next(ks), (L, RW), f32, -5.0, -0.5),
        "w2": nrm((L, DECAY_LORA, RW), 0.1 * DECAY_LORA ** -0.5),
        "a0": nrm((L, RW), 0.5),
        "a2": nrm((L, ICLR_LORA, RW), 0.5 * ICLR_LORA ** -0.5),
        "g2": nrm((L, GATE_LORA, RW), GATE_LORA ** -0.5),
        "k_k": 0.85 + nrm((L, RW), 0.05),
        "k_a": 1.0 + nrm((L, RW), 0.05),
        "r_k": nrm((L, RWKV_HEADS, HEAD_DIM), 0.1),
        "lnx_w": 1.0 + nrm((L, RW), 0.05),
        "lnx_b": nrm((L, RW), 0.02),
        "w_a": nrm((L, RW, D), RW ** -0.5),
        "w_b": nrm((L, ATTN_OUT_WIDTH, D), ATTN_OUT_WIDTH ** -0.5),
        "w_out": nrm((L, D, D), D ** -0.5),
        "g_pre_ffn": 1.0 + nrm((L, D), 0.05),
        "g_post_ffn": 1.0 + nrm((L, D), 0.05),
        "w_ffn_in": nrm((L, D, 2 * D_FF), D ** -0.5),
        "w_ffn_out": nrm((L, D_FF, D), D_FF ** -0.5),
    }

def first_block(x, c, w_ada, b_ada, g_pre_mix, g_post_mix, w_in, mu_shift, w0, w2, a0, a2, g2,
              k_k, k_a, r_k, lnx_w, lnx_b, w_a, w_b, w_out, g_pre_ffn, g_post_ffn,
              w_ffn_in, w_ffn_out):
    for i in range(DEPTH):
        mod = jax.nn.silu(c) @ w_ada[i] + b_ada[i]
        shift_m, scale_m, gate_m, shift_f, scale_f, gate_f = jnp.split(mod, 6, axis=-1)

        h = modulate(rms_norm(x, g_pre_mix[i]), shift_m, scale_m)
        p = h @ w_in[i]
        p_shift, pq, pk_att, pv_att, p_ga, p_gb = _split(
            p, [SHIFT_WIDTH, ATTN_WIDTH, ATTN_WIDTH, ATTN_WIDTH, D_MODEL, D_MODEL])
        p_shift = p_shift + mu_shift[i] * (token_shift(p_shift) - p_shift)
        pr, pk, pv, pw, pa, pg = _split(
            p_shift, [RWKV_WIDTH, RWKV_WIDTH, RWKV_WIDTH, DECAY_LORA, ICLR_LORA, GATE_LORA])
        y_a = rwkv7_mix(pr, pk, pv, pw, pa, pg, w0[i], w2[i], a0[i], a2[i], g2[i],
                        k_k[i], k_a[i], r_k[i], lnx_w[i], lnx_b[i], w_a[i])
        y_b = dilated_attention_mix(pq, pk_att, pv_att, w_b[i])
        merged = jax.nn.sigmoid(p_ga) * y_a + jax.nn.sigmoid(p_gb) * y_b
        x = x + gate_m[:, None, :] * rms_norm(merged @ w_out[i], g_post_mix[i])

        h = modulate(rms_norm(x, g_pre_ffn[i]), shift_f, scale_f)
        u, gt = jnp.split(h @ w_ffn_in[i], 2, axis=-1)
        f = (jax.nn.silu(u) * gt) @ w_ffn_out[i]
        x = x + gate_f[:, None, :] * rms_norm(f, g_post_ffn[i])
    return x


DEPTH_2 = 2

HEAD_DIM_2 = D_MODEL // 16
NSA_HEADS = 8
NSA_KV_GROUPS = 2
FOX_HEADS = 4
MOBA_HEADS = 4
MIX_WIDTH = (NSA_HEADS + FOX_HEADS + MOBA_HEADS) * HEAD_DIM_2
ROPE_DIM = HEAD_DIM_2 // 4
ROPE_THETA_2 = 500000.0
CMP_LEN = 32
CMP_STRIDE = 16
CMP_HIDDEN = 4 * HEAD_DIM_2
SLC_LEN = 64
SLC_TOPN = 8
WIN = 512
MOBA_BLOCK = 256
MOBA_TOPK = 3
QBLOCK = 128
GATHER_CHUNK = 32
D_FF_2 = 256 * ((8 * D_MODEL // 3 + 255) // 256)
FOX_FGATE_BIAS = 3.0
MAX_POS_OFFSET = 4096
EPS = 1e-6

_NSA_KV = NSA_KV_GROUPS * HEAD_DIM_2
IN_SPLITS = (
    ("nsa_q", NSA_HEADS * HEAD_DIM_2),
    ("nsa_kc", _NSA_KV), ("nsa_vc", _NSA_KV),
    ("nsa_ks", _NSA_KV), ("nsa_vs", _NSA_KV),
    ("nsa_kw", _NSA_KV), ("nsa_vw", _NSA_KV),
    ("nsa_gate", 3 * NSA_HEADS),
    ("fox_q", FOX_HEADS * HEAD_DIM_2), ("fox_k", FOX_HEADS * HEAD_DIM_2),
    ("fox_v", FOX_HEADS * HEAD_DIM_2), ("fox_f", FOX_HEADS),
    ("moba_q", MOBA_HEADS * HEAD_DIM_2), ("moba_k", MOBA_HEADS * HEAD_DIM_2),
    ("moba_v", MOBA_HEADS * HEAD_DIM_2),
)
IN_COLS = sum(w for _, w in IN_SPLITS)


def rms_norm_2(x, g):
    xf = x.astype(jnp.float32)
    y = xf * lax.rsqrt(jnp.mean(xf * xf, axis=-1, keepdims=True) + EPS)
    return (y * g.astype(jnp.float32)).astype(x.dtype)

def ada_norm(x, g, shift, scale):
    return rms_norm_2(x, g) * (1 + scale[:, None, :]) + shift[:, None, :]

def swiglu(h, w13, w2):
    a, b = jnp.split(h @ w13, 2, axis=-1)
    return (jax.nn.silu(a) * b) @ w2

def masked_softmax(s, mask):
    s = jnp.where(mask, s.astype(jnp.float32), -jnp.inf)
    m = jnp.max(s, axis=-1, keepdims=True)
    m = jnp.where(jnp.isfinite(m), m, 0.0)
    e = jnp.exp(s - m)
    return e / jnp.maximum(jnp.sum(e, axis=-1, keepdims=True), 1e-30)

def rope_tables(positions):
    inv = ROPE_THETA_2 ** (-jnp.arange(0, ROPE_DIM, 2, dtype=jnp.float32) / ROPE_DIM)
    ang = positions.astype(jnp.float32)[..., None] * inv
    return jnp.cos(ang), jnp.sin(ang)

def apply_rope_2(x, cos, sin):
    r, rest = x[..., :ROPE_DIM], x[..., ROPE_DIM:]
    r1, r2 = r[..., :ROPE_DIM // 2], r[..., ROPE_DIM // 2:]
    c, s = cos[:, :, None, :], sin[:, :, None, :]
    rot = jnp.concatenate([r1 * c - r2 * s, r2 * c + r1 * s], axis=-1).astype(x.dtype)
    return jnp.concatenate([rot, rest], axis=-1)

def split_blocks(a, axis, size):
    n = a.shape[axis] // size
    a = a.reshape(a.shape[:axis] + (n, size) + a.shape[axis + 1:])
    return jnp.moveaxis(a, axis, 0)

def merge_blocks(a, axis):
    a = jnp.moveaxis(a, 0, axis)
    return a.reshape(a.shape[:axis] + (a.shape[axis] * a.shape[axis + 1],) + a.shape[axis + 2:])

def nsa_mixer(q, kc, vc, ks, vs, kw, vw, gates, cmp_pos, cmp_w1, cmp_w2):
    B, S = q.shape[0], q.shape[1]
    G, R, D = NSA_KV_GROUPS, NSA_HEADS // NSA_KV_GROUPS, HEAD_DIM_2
    scale = D ** -0.5
    qg = q.reshape(B, S, G, R, D).transpose(0, 2, 3, 1, 4)
    t = np.arange(S)

    n_c = (S - CMP_LEN) // CMP_STRIDE + 1
    win_idx = np.arange(n_c)[:, None] * CMP_STRIDE + np.arange(CMP_LEN)[None, :]

    def compress(z, pos, w1, w2):
        zb = z[:, win_idx] + pos[None, None, :, None, :]
        zb = zb.transpose(0, 3, 1, 2, 4).reshape(B, G, n_c, CMP_LEN * D)
        return jax.nn.gelu(zb @ w1) @ w2

    kcmp = compress(kc, cmp_pos[0], cmp_w1[0], cmp_w2[0])
    vcmp = compress(vc, cmp_pos[1], cmp_w1[1], cmp_w2[1])
    cmp_end = np.arange(n_c) * CMP_STRIDE + CMP_LEN - 1
    cmp_mask = cmp_end[None, :] <= t[:, None]
    s_cmp = jnp.einsum('bgrsd,bgcd->bgrsc', qg, kcmp) * scale
    p_cmp = masked_softmax(s_cmp, cmp_mask)
    o_cmp = jnp.einsum('bgrsc,bgcd->bgrsd', p_cmp.astype(vcmp.dtype), vcmp)

    n_s = S // SLC_LEN
    c0 = np.arange(n_c)[:, None] * CMP_STRIDE
    j0 = np.arange(n_s)[None, :] * SLC_LEN
    overlap = ((c0 < j0 + SLC_LEN) & (c0 + CMP_LEN > j0)).astype(np.float32)
    imp = jnp.einsum('bgrsc,cj->bgsj', p_cmp, jnp.asarray(overlap))
    tb = (t // SLC_LEN)[:, None]
    jj = np.arange(n_s)[None, :]
    valid = jj <= tb
    forced = (jj == 0) | (jj == tb) | (jj == tb - 1)
    imp = jnp.where(valid, jnp.where(forced, jnp.inf, imp), -jnp.inf)
    n_top = min(SLC_TOPN, n_s)
    top_val, top_idx = lax.top_k(imp, n_top)
    top_ok = top_val > -jnp.inf

    ks_blk = ks.reshape(B, n_s, SLC_LEN, G, D).transpose(0, 3, 1, 2, 4)
    vs_blk = vs.reshape(B, n_s, SLC_LEN, G, D).transpose(0, 3, 1, 2, 4)
    C = GATHER_CHUNK
    bi = jnp.arange(B)[:, None, None]
    gi = jnp.arange(G)[None, :, None]
    k_sel = n_top * SLC_LEN

    def slc_chunk(args):
        qc, idx, ok, q0 = args
        flat = idx.reshape(B, G, C * n_top)
        kg = ks_blk[bi, gi, flat].reshape(B, G, C, k_sel, D)
        vg = vs_blk[bi, gi, flat].reshape(B, G, C, k_sel, D)
        kpos = (idx[..., None] * SLC_LEN + jnp.arange(SLC_LEN)).reshape(B, G, C, k_sel)
        qpos = q0 + jnp.arange(C)
        mask = jnp.repeat(ok, SLC_LEN, axis=-1) & (kpos <= qpos[:, None])
        s = jnp.einsum('bgrcd,bgckd->bgrck', qc, kg) * scale
        p = masked_softmax(s, mask[:, :, None])
        return jnp.einsum('bgrck,bgckd->bgrcd', p.astype(vg.dtype), vg)

    o_slc = lax.map(slc_chunk, (split_blocks(qg, 3, C), split_blocks(top_idx, 2, C),
                                split_blocks(top_ok, 2, C), jnp.arange(S // C) * C))
    o_slc = merge_blocks(o_slc, 3)

    kw_p = jnp.pad(kw.transpose(0, 2, 1, 3), ((0, 0), (0, 0), (WIN, 0), (0, 0)))
    vw_p = jnp.pad(vw.transpose(0, 2, 1, 3), ((0, 0), (0, 0), (WIN, 0), (0, 0)))
    span = WIN + QBLOCK

    def win_block(args):
        qb, q0 = args
        kb = lax.dynamic_slice_in_dim(kw_p, q0, span, axis=2)
        vb = lax.dynamic_slice_in_dim(vw_p, q0, span, axis=2)
        qpos = q0 + jnp.arange(QBLOCK)
        kpos = q0 - WIN + jnp.arange(span)
        d = qpos[:, None] - kpos[None, :]
        mask = (kpos[None, :] >= 0) & (d >= 0) & (d < WIN)
        s = jnp.einsum('bgrqd,bgkd->bgrqk', qb, kb) * scale
        p = masked_softmax(s, mask)
        return jnp.einsum('bgrqk,bgkd->bgrqd', p.astype(vb.dtype), vb)

    o_win = lax.map(win_block, (split_blocks(qg, 3, QBLOCK), jnp.arange(S // QBLOCK) * QBLOCK))
    o_win = merge_blocks(o_win, 3)

    g = gates.reshape(B, S, G, R, 3).transpose(0, 2, 3, 1, 4)
    o = g[..., 0:1] * o_cmp + g[..., 1:2] * o_slc + g[..., 2:3] * o_win
    return o.transpose(0, 3, 1, 2, 4).reshape(B, S, NSA_HEADS * D)

def fox_mixer(q, k, v, f_logit, f_bias):
    B, S, H, D = q.shape
    scale = D ** -0.5
    logf = jax.nn.log_sigmoid((f_logit + f_bias).astype(jnp.float32))
    F = jnp.cumsum(logf, axis=1).transpose(0, 2, 1)
    qt, kt, vt = (a.transpose(0, 2, 1, 3) for a in (q, k, v))
    kpos = jnp.arange(S)

    def blk(args):
        qb, Fq, q0 = args
        s = (jnp.einsum('bhqd,bhkd->bhqk', qb, kt).astype(jnp.float32) * scale
             + Fq[..., None] - F[:, :, None, :])
        qpos = q0 + jnp.arange(QBLOCK)
        p = masked_softmax(s, kpos[None, :] <= qpos[:, None])
        return jnp.einsum('bhqk,bhkd->bhqd', p.astype(vt.dtype), vt)

    o = lax.map(blk, (split_blocks(qt, 2, QBLOCK), split_blocks(F, 2, QBLOCK),
                      jnp.arange(S // QBLOCK) * QBLOCK))
    o = merge_blocks(o, 2)
    return o.transpose(0, 2, 1, 3).reshape(B, S, H * D)

def moba_mixer(q, k, v):
    B, S, H, D = q.shape
    scale = D ** -0.5
    qt, kt, vt = (a.transpose(0, 2, 1, 3) for a in (q, k, v))
    NB = -(-S // MOBA_BLOCK)
    Sp = NB * MOBA_BLOCK
    kp = jnp.pad(kt, ((0, 0), (0, 0), (0, Sp - S), (0, 0)))
    vp = jnp.pad(vt, ((0, 0), (0, 0), (0, Sp - S), (0, 0)))
    kb = kp.reshape(B, H, NB, MOBA_BLOCK, D)
    vb = vp.reshape(B, H, NB, MOBA_BLOCK, D)
    n_sel = min(MOBA_TOPK, NB - 1)
    C = GATHER_CHUNK
    t = np.arange(S)
    xs = (split_blocks(qt, 2, C), jnp.arange(S // C) * C)
    if n_sel > 0:
        kmean = jnp.mean(kb.astype(jnp.float32), axis=3)
        gate = jnp.einsum('bhsd,bhnd->bhsn', qt.astype(jnp.float32), kmean)
        past = np.arange(NB)[None, :] < (t // MOBA_BLOCK)[:, None]
        gate = jnp.where(past, gate, -jnp.inf)
        top_val, top_idx = lax.top_k(gate, n_sel)
        xs = xs + (split_blocks(top_idx, 2, C), split_blocks(top_val > -jnp.inf, 2, C))
    bi = jnp.arange(B)[:, None, None]
    hi = jnp.arange(H)[None, :, None]
    k_sel = n_sel * MOBA_BLOCK

    def chunk(args):
        qc, q0 = args[0], args[1]
        own = q0 // MOBA_BLOCK
        k_own = lax.dynamic_slice_in_dim(kp, own * MOBA_BLOCK, MOBA_BLOCK, axis=2)
        v_own = lax.dynamic_slice_in_dim(vp, own * MOBA_BLOCK, MOBA_BLOCK, axis=2)
        qpos = q0 + jnp.arange(C)
        own_pos = own * MOBA_BLOCK + jnp.arange(MOBA_BLOCK)
        s_own = jnp.einsum('bhcd,bhkd->bhck', qc, k_own) * scale
        m_own = jnp.broadcast_to(own_pos[None, :] <= qpos[:, None], s_own.shape)
        if n_sel == 0:
            p = masked_softmax(s_own, m_own)
            return jnp.einsum('bhck,bhkd->bhcd', p.astype(v_own.dtype), v_own)
        idx, ok = args[2], args[3]
        flat = idx.reshape(B, H, C * n_sel)
        kg = kb[bi, hi, flat].reshape(B, H, C, k_sel, D)
        vg = vb[bi, hi, flat].reshape(B, H, C, k_sel, D)
        s_sel = jnp.einsum('bhcd,bhckd->bhck', qc, kg) * scale
        m_sel = jnp.repeat(ok, MOBA_BLOCK, axis=-1)
        p = masked_softmax(jnp.concatenate([s_sel, s_own], axis=-1),
                           jnp.concatenate([m_sel, m_own], axis=-1))
        p = p.astype(vg.dtype)
        return (jnp.einsum('bhck,bhckd->bhcd', p[..., :k_sel], vg)
                + jnp.einsum('bhck,bhkd->bhcd', p[..., k_sel:], v_own))

    o = merge_blocks(lax.map(chunk, xs), 2)
    return o.transpose(0, 2, 1, 3).reshape(B, S, H * D)

def token_mixer(h, w_in, f_bias, cmp_pos, cmp_w1, cmp_w2, w_out, cos, sin):
    B, S, _ = h.shape
    proj = h @ w_in
    parts = {}
    off = 0
    for name, width in IN_SPLITS:
        parts[name] = proj[..., off:off + width]
        off += width

    def heads(a, n):
        return a.reshape(B, S, n, HEAD_DIM_2)

    o_nsa = nsa_mixer(
        apply_rope_2(heads(parts['nsa_q'], NSA_HEADS), cos, sin),
        apply_rope_2(heads(parts['nsa_kc'], NSA_KV_GROUPS), cos, sin), heads(parts['nsa_vc'], NSA_KV_GROUPS),
        apply_rope_2(heads(parts['nsa_ks'], NSA_KV_GROUPS), cos, sin), heads(parts['nsa_vs'], NSA_KV_GROUPS),
        apply_rope_2(heads(parts['nsa_kw'], NSA_KV_GROUPS), cos, sin), heads(parts['nsa_vw'], NSA_KV_GROUPS),
        jax.nn.sigmoid(parts['nsa_gate']).reshape(B, S, NSA_HEADS, 3),
        cmp_pos, cmp_w1, cmp_w2)
    o_fox = fox_mixer(heads(parts['fox_q'], FOX_HEADS), heads(parts['fox_k'], FOX_HEADS),
                      heads(parts['fox_v'], FOX_HEADS), parts['fox_f'], f_bias)
    o_moba = moba_mixer(apply_rope_2(heads(parts['moba_q'], MOBA_HEADS), cos, sin),
                        apply_rope_2(heads(parts['moba_k'], MOBA_HEADS), cos, sin),
                        heads(parts['moba_v'], MOBA_HEADS))
    return jnp.concatenate([o_nsa, o_fox, o_moba], axis=-1) @ w_out

def second_inputs(seed: int = 0) -> dict:
    key = jax.random.key(seed)
    ks = jax.random.split(key, 16)
    D = D_MODEL

    def nrm(k, shape, s):
        return jax.random.normal(k, shape, jnp.float32) * s

    x = nrm(ks[0], (BATCH, SEQ, D), 1.0)
    c = nrm(ks[1], (BATCH, D), 1.0)
    offset = jax.random.randint(ks[2], (BATCH, 1), 0, MAX_POS_OFFSET, dtype=jnp.int32)
    positions = offset + jnp.arange(SEQ, dtype=jnp.int32)[None, :]
    return {
        "x": x,
        "c": c,
        "positions": positions,
        "norm_g": 1.0 + nrm(ks[3], (DEPTH_2, 3, D), 0.05),
        "w_ada": nrm(ks[4], (DEPTH_2, D, 9 * D), 0.5 * D ** -0.5),
        "b_ada": nrm(ks[5], (DEPTH_2, 9 * D), 0.01),
        "w_in": nrm(ks[6], (DEPTH_2, D, IN_COLS), D ** -0.5),
        "fox_fbias": FOX_FGATE_BIAS + nrm(ks[7], (DEPTH_2, FOX_HEADS), 0.1),
        "cmp_pos": nrm(ks[8], (DEPTH_2, 2, CMP_LEN, HEAD_DIM_2), 0.1),
        "cmp_w1": nrm(ks[9], (DEPTH_2, 2, CMP_LEN * HEAD_DIM_2, CMP_HIDDEN), (CMP_LEN * HEAD_DIM_2) ** -0.5),
        "cmp_w2": nrm(ks[10], (DEPTH_2, 2, CMP_HIDDEN, HEAD_DIM_2), CMP_HIDDEN ** -0.5),
        "w_out": nrm(ks[11], (DEPTH_2, MIX_WIDTH, D), MIX_WIDTH ** -0.5),
        "ffn_w13": nrm(ks[12], (DEPTH_2, 2, D, 2 * D_FF_2), D ** -0.5),
        "ffn_w2": nrm(ks[13], (DEPTH_2, 2, D_FF_2, D), D_FF_2 ** -0.5),
        "final_g": 1.0 + nrm(ks[14], (D,), 0.05),
    }

def second_block(x, c, positions, norm_g, w_ada, b_ada, w_in, fox_fbias, cmp_pos, cmp_w1, cmp_w2,
              w_out, ffn_w13, ffn_w2, final_g):
    cos, sin = rope_tables(positions)
    c_act = jax.nn.silu(c)
    B = x.shape[0]
    for l in range(DEPTH_2):
        mod = (c_act @ w_ada[l] + b_ada[l]).reshape(B, 3, 3, D_MODEL)
        h = ada_norm(x, norm_g[l, 0], mod[:, 0, 0], mod[:, 0, 1])
        x = x + 0.5 * mod[:, 0, 2][:, None, :] * swiglu(h, ffn_w13[l, 0], ffn_w2[l, 0])
        h = ada_norm(x, norm_g[l, 1], mod[:, 1, 0], mod[:, 1, 1])
        x = x + mod[:, 1, 2][:, None, :] * token_mixer(h, w_in[l], fox_fbias[l], cmp_pos[l], cmp_w1[l],
                                                        cmp_w2[l], w_out[l], cos, sin)
        h = ada_norm(x, norm_g[l, 2], mod[:, 2, 0], mod[:, 2, 1])
        x = x + 0.5 * mod[:, 2, 2][:, None, :] * swiglu(h, ffn_w13[l, 1], ffn_w2[l, 1])
    return rms_norm_2(x, final_g)


def setup_inputs(seed=0):
    out = dict(first_inputs(seed))
    for name, value in second_inputs(seed + 1).items():
        if name != "x":
            out[name + "_2"] = value
    return out


def reference(
    x, c, w_ada, b_ada, g_pre_mix, g_post_mix, w_in, mu_shift, w0, w2, a0, a2, g2, k_k, k_a,
    r_k, lnx_w, lnx_b, w_a, w_b, w_out, g_pre_ffn, g_post_ffn, w_ffn_in, w_ffn_out, c_2,
    positions_2, norm_g_2, w_ada_2, b_ada_2, w_in_2, fox_fbias_2, cmp_pos_2, cmp_w1_2, cmp_w2_2,
    w_out_2, ffn_w13_2, ffn_w2_2, final_g_2,
):
    x = first_block(
        x, c, w_ada, b_ada, g_pre_mix, g_post_mix, w_in, mu_shift, w0, w2, a0, a2, g2, k_k, k_a,
        r_k, lnx_w, lnx_b, w_a, w_b, w_out, g_pre_ffn, g_post_ffn, w_ffn_in, w_ffn_out,
    )
    return second_block(
        x, c_2, positions_2, norm_g_2, w_ada_2, b_ada_2, w_in_2, fox_fbias_2, cmp_pos_2,
        cmp_w1_2, cmp_w2_2, w_out_2, ffn_w13_2, ffn_w2_2, final_g_2,
    )


_drawn_inputs = setup_inputs


def setup_inputs(seed=0):
    import zlib

    import numpy as np

    out = dict(_drawn_inputs(seed))
    spreads = {}
    factors = {'g_post_mix': 3.297,
     'w2': 8.0,
     'k_k': 3.583,
     'k_a': 2.856,
     'lnx_w': 4.956,
     'lnx_b': 8.0,
     'g_pre_ffn': 2.757,
     'g_post_ffn': 4.017,
     'norm_g_2': 3.259,
     'b_ada_2': 5.547,
     'fox_fbias_2': 64.0,
     'cmp_pos_2': 6.478}
    for name, (base, spread) in spreads.items():
        noise = np.random.default_rng([zlib.crc32(name.encode()), seed]).standard_normal(out[name].shape)
        drawn = base * np.exp(spread * noise) if base else spread * noise
        out[name] = __import__('jax').numpy.asarray(drawn.astype(out[name].dtype))
    for name, factor in factors.items():
        out[name] = (out[name] * factor).astype(out[name].dtype)
    return out
```

```python
import math
from contextlib import ExitStack

import numpy as np

import concourse.bass as bass
from concourse import mybir

F32 = mybir.dt.float32
I32 = mybir.dt.int32
ACT = mybir.ActivationFunctionType
ALU = mybir.AluOpType
AX = mybir.AxisListType

P = 128
D = 1024
S = 256
NT = S // P
KD = D // P
FF = 2816
FC = FF // 256
LAYERS = 2
HD = 64
SCALE = HD ** -0.5
RW = 768
PAIRS = RW // P
EPS = 1e-6
GN_EPS = 64e-5
DECAY = math.exp(-0.5)
NEG = -1e30
SLOT = 4096
SHIFT_TILES = 20
C = 64
LEVELS = (2, 4, 8, 16, 32)
DVE_STEPS_PER_LAYER = 102

CONST_WIDTHS = (
    ("ident", P), ("rope1", P), ("rope2", P), ("swap", P), ("blockones", P), ("ident_stack", HD),
    ("tri", P), ("ones", P), ("causal", S),
    ("cos1", S), ("sin1", S), ("inv_freq2", 1), ("cmp_add", 32), ("cmp_keep", 32), ("cmp_block", 8), ("fox_row", 4),
)
EARLY_WIDTHS = (("lora", 2 * RW), ("dilated", 3 * 384), ("score_mask", 512),
                ("level1", P), ("level1_t", P), ("levels_t", len(LEVELS) * P))
PARAM_WIDTHS = (
    ("c", 2 * KD), ("b_ada1", 48), ("g_norm", 2 * KD), ("g_post", 2 * KD),
    ("final_g", KD), ("mu", SHIFT_TILES), ("w0", 6), ("a0", 6), ("k_k", 6),
    ("k_a", 6), ("r_k", 6), ("lnx_w", 6), ("lnx_b", 6),
)
LAYER_WIDTHS = (("b_ada", 72), ("norm_g", 3 * KD), ("fox_bias", 4), ("cmp_pos", 32), ("cmp_w2", 2 * 2 * HD))


def columns(widths):
    at, out = 0, {}
    for name, w in widths:
        out[name] = (at, w)
        at += w
    return out, at


CONST_AT, CONST_N = columns(CONST_WIDTHS)
EARLY_AT, EARLY_N = columns(EARLY_WIDTHS)
PARAM_AT, PARAM_N = columns(PARAM_WIDTHS)
LAYER_AT, LAYER_N = columns(LAYER_WIDTHS)

IN2_WIDTHS = (512, 512, 512, 512, 512, 284)
IN2_AT = tuple(8 * sum(IN2_WIDTHS[:i]) for i in range(len(IN2_WIDTHS)))


def constants():
    a, early = np.zeros((P, CONST_N), np.float32), np.zeros((P, EARLY_N - 2 * RW), np.float32)

    def put(name, value):
        at, w = CONST_AT[name] if name in CONST_AT else EARLY_AT[name]
        if name in EARLY_AT:
            early[:, at - 2 * RW:at - 2 * RW + w] = np.asarray(value, np.float32).reshape(P, w)
            return
        a[:, at:at + w] = np.asarray(value, np.float32).reshape(P, w)

    i = np.arange(P)
    row, col = i[:, None], i[None, :]
    put("ident", row == col)
    for name, half in (("rope1", 32), ("rope2", 8)):
        r = np.zeros((P, P))
        for m in range(P):
            d = m % HD
            if d < half:
                r[m + half, m] = -1
            elif d < 2 * half:
                r[m - half, m] = 1
        put(name, r)
    put("swap", row == (col + 64) % P)
    put("blockones", row // 64 == col // 64)
    put("ident_stack", (row % 64) == np.arange(64)[None, :])
    put("tri", row <= col)
    put("ones", np.ones((P, P)))
    q1 = P + i[:, None]
    k = np.arange(S)[None, :]
    put("causal", np.where(q1 >= k, 0, NEG))
    dil = []
    for dilation in (1, 4, 16):
        for q, keys in ((i[:, None], np.arange(P)[None, :]), (q1, k)):
            ok = (q >= keys) & (q - keys <= 128 * dilation) & ((q - keys) % dilation == 0)
            dil.append(np.where(ok, 0, NEG))
    put("dilated", np.concatenate(dil, 1))
    same = row // C == col // C
    strict, incl = same & (row < col), same & (row <= col)
    put("score_mask", np.concatenate([strict, incl, strict, incl], 1))

    def level(b):
        return (row // (2 * b) == col // (2 * b)) & (row % (2 * b) >= b) & (col % (2 * b) < b)

    put("level1", -1.0 * level(1))
    put("level1_t", -1.0 * level(1).T)
    put("levels_t", np.concatenate([level(b).T for b in LEVELS], 1))
    half = HD // 2
    inv = (10000.0 ** (-np.arange(half) / half)).astype(np.float32)
    ang = (np.arange(S, dtype=np.float32)[None, :] * inv[i % half][:, None]).astype(np.float32)
    put("cos1", np.cos(ang.astype(np.float64)))
    put("sin1", np.sin(ang.astype(np.float64)))
    inv2 = (500000.0 ** (-np.arange(0, 16, 2) / 16)).astype(np.float32)
    put("inv_freq2", np.where(i % HD < 16, inv2[i % 8], 0.0))
    cmp_ok = [(q >= 16 * np.arange(16)[None, :] + 31) & (np.arange(16)[None, :] < 15) for q in (i[:, None], q1)]
    put("cmp_add", np.concatenate([np.where(m, 0, NEG) for m in cmp_ok], 1))
    put("cmp_keep", np.concatenate(cmp_ok, 1))
    put("cmp_block", row // 16 == np.arange(8)[None, :])
    put("fox_row", row % 64 == np.arange(4)[None, :])
    return a, early


def cols(v):
    return np.asarray(v).reshape(-1, P).T


def k_tiles(w):
    kdim, n = w.shape
    return np.ascontiguousarray(np.asarray(w).reshape(kdim // P, P, n).transpose(1, 0, 2).reshape(P, -1))


def chunked(w, width=512):
    return np.stack([k_tiles(w[:, j:j + width]) for j in range(0, w.shape[1], width)])


def layout(inp):
    g = {k: np.asarray(v) for k, v in inp.items()}
    params = np.concatenate([
        cols(g["c"][0]), cols(g["c_2"][0]), cols(g["b_ada"][0]),
        cols(g["g_pre_mix"][0]), cols(g["g_pre_ffn"][0]), cols(g["g_post_mix"][0]), cols(g["g_post_ffn"][0]),
        cols(g["final_g_2"]), cols(g["mu_shift"][0]), cols(g["w0"][0]),
        cols(g["a0"][0]), cols(g["k_k"][0]), cols(g["k_a"][0]), cols(g["r_k"][0].reshape(-1)),
        cols(g["lnx_w"][0]), cols(g["lnx_b"][0]),
    ], axis=1)
    assert params.shape == (P, PARAM_N)
    layers = np.stack([np.concatenate([
        cols(g["b_ada_2"][l]), cols(g["norm_g_2"][l].reshape(-1)), np.broadcast_to(g["fox_fbias_2"][l][None], (P, 4)),
        g["cmp_pos_2"][l].reshape(2, 16, 2, HD).transpose(2, 3, 0, 1).reshape(P, 32),
        k_tiles(g["cmp_w2_2"][l, 0]), k_tiles(g["cmp_w2_2"][l, 1])], 1) for l in range(LAYERS)])
    const, early = constants()
    w_in = g["w_in"][0]
    at = np.cumsum([0, 2560, 768, 768, 768, 1024, 1024])
    shift, q, k, v, ga, gb = (w_in[:, at[n]:at[n + 1]] for n in range(6))
    first = np.concatenate([shift, q, k, v[:, :512]], 1)
    in2 = []
    for l in range(LAYERS):
        w = g["w_in_2"][l]
        nq = w[:, :512].reshape(D, 2, 4, HD).transpose(0, 2, 1, 3).reshape(D, 512)
        part = lambda a, b: w[:, a:b]
        chunks = [
            np.concatenate([part(512, 640), part(640, 768), part(768, 896), part(1024, 1152)], 1),
            nq,
            part(1304, 1816),
            part(2076, 2588),
            np.concatenate([part(896, 1024), part(1152, 1280), part(1816, 2072)], 1),
            np.concatenate([part(2588, 2844), part(1280, 1304), part(2072, 2076)], 1),
        ]
        in2.append(np.concatenate([k_tiles(c) for c in chunks], 1))
    w_out2 = g["w_out_2"].copy()
    w_out2[:, :512] = g["w_out_2"][:, :512].reshape(LAYERS, 2, 4, HD, D).transpose(0, 2, 1, 3, 4).reshape(LAYERS, 512, D)
    up = [g["w_ffn_in"][0]] + [g["ffn_w13_2"][l, f] for l in range(LAYERS) for f in range(2)]
    down = [g["w_ffn_out"][0]] + [g["ffn_w2_2"][l, f] for l in range(LAYERS) for f in range(2)]
    up = [w.reshape(D, 2, FC, 256).transpose(2, 0, 1, 3).reshape(FC, KD, P, 512).transpose(0, 2, 1, 3).reshape(FC, P, SLOT) for w in up]
    down = [w.reshape(FC, 2, P, D).transpose(0, 2, 1, 3).reshape(FC, P, 2 * D) for w in down]
    return {
        "const": const, "params": params, "layers": layers, 
        "early": np.concatenate([np.concatenate([g["w2"][0], g["a2"][0]], 0), g["g2"][0], early], 1),
        "x": g["x"][0].reshape(NT, P, D).transpose(1, 0, 2).reshape(P, NT * D),
        "pos": g["positions_2"],
        "ada": np.concatenate([chunked(g["w_ada"][0])] + [chunked(g["w_ada_2"][l]) for l in range(LAYERS)]),
        "in1": chunked(first), "in1_v": k_tiles(v[:, 512:]), "gates1": chunked(np.concatenate([ga, gb], 1)),
        "w_a": chunked(g["w_a"][0]), "w_b": k_tiles(g["w_b"][0]), "w_out": chunked(g["w_out"][0]),
        "up": np.concatenate(up), "down": np.concatenate(down),
        "in2": np.stack(in2),
        "cmp1": np.stack([k_tiles(g["cmp_w1_2"][l, i]) for l in range(LAYERS) for i in range(2)]),
        "w_out2": np.concatenate([chunked(w_out2[l]) for l in range(LAYERS)]),
    }


ADA1_CHUNKS, ADA2_CHUNKS = 12, 18
G_MIX1 = ADA1_CHUNKS
G_FFN1 = G_MIX1 + 19
G_LAYER = G_FFN1 + FC
MIX2_CHUNKS = 10
PER_LAYER = ADA2_CHUNKS + 2 * FC + MIX2_CHUNKS
assert G_LAYER % 2 == 0 and PER_LAYER % 2 == 0


class Steps:

    def __init__(self, engine, sem):
        self.engine, self.sem, self.base, self.n = engine, sem, 0, 0

    def __call__(self, instruction):
        instruction.then_inc(self.sem, 1)
        self.n += 1

    def settle(self):
        self.engine.wait_ge(self.sem, self.base + self.n)

    def enter(self, turn, per_turn):
        self.outer, self.base, self.n, self.per = self.base + self.n, self.base + self.n + turn * per_turn, 0, per_turn

    def leave(self, turns):
        assert self.n == self.per, f"{self.sem}: {self.n} steps in a turn"
        self.base, self.n = self.outer + turns * self.per, 0


def wait(engine, sem, value):
    if isinstance(value, int) and value <= 0:
        return
    engine.wait_ge(sem, value)


def build(nc, T, out):
    with ExitStack() as ctx:
        def sb(name, shape, dt=F32):
            return ctx.enter_context(nc.sbuf_tensor(name, shape, dt))

        def sem(name):
            return ctx.enter_context(nc.semaphore(name))

        const = sb("const", [P, CONST_N])
        params = sb("params", [P, PARAM_N])
        x = sb("x_res", [P, NT, D])
        xn = sb("xn", [P, NT, D])
        hT = sb("hT", [P, KD, S])
        ring = sb("ring", [P, 2, SLOT])
        ring_down = sb("ring_down", [P, 2, 2 * D])
        scratch = sb("scratch", [P, 3072])
        act_t = scratch[:, 0:1024].rearrange("p (b k n) -> p b k n", b=2, k=2)
        silu = scratch[:, 1024:2048].rearrange("p (b n) -> p b n", b=2)
        fin = scratch[:, 2048:3072].rearrange("p (t n) -> p t n", t=2)
        row = sb("row", [P, D])
        silu_c = sb("silu_c", [P, 2 * KD])
        mod = sb("mod", [P, 72])
        mod_raw = sb("mod_raw", [P, 72])
        mod_scale = sb("mod_scale", [P, 3, KD])
        mod_gate = sb("mod_gate", [P, 3, KD])
        stat = sb("stat", [P, 48])
        cos2 = sb("cos2", [P, S])
        sin2 = sb("sin2", [P, S])
        raw = sb("raw", [P, 3, S + 2])
        pre = sb("pre", [P, 3, S])
        rot = sb("rot", [P, 2, S])
        pos_i = hT[:, 7].bitcast(I32)
        now = sb("layer_now", [P, LAYER_N])
        mx, nb, rs, ri = (sb(n, [P, 24]) for n in ("mx", "neg_max", "row_sum", "row_scale"))
        ARENA = 24200
        arena = sb("arena", [P, ARENA])
        psum = ctx.enter_context(nc.psum_tensor("psum", [P, 8, 512], F32))
        bank = [psum[:, b, :] for b in range(8)]

        early = ring_down[:].rearrange("p b n -> p (b n)")
        lora = early[:, 0:2 * RW]

        def K(name, a=0, b=None):
            if name in EARLY_AT:
                at, w = EARLY_AT[name]
                return early[:, at + a:at + (w if b is None else b)]
            at, w = CONST_AT[name]
            return const[:, at + a:at + (w if b is None else b)]

        def PR(name, a=0, b=None):
            at, w = PARAM_AT[name]
            return params[:, at + a:at + (w if b is None else b)]

        def NOW(name, a=0, b=None):
            at, w = LAYER_AT[name]
            return now[:, at + a:at + (w if b is None else b)]

        def places(start, *widths):
            out = []
            for w in widths:
                out.append(arena[:, start:start + w])
                start += w
            assert start <= ARENA, start
            return out

        shifted, sgw, iclr, gate1, o1 = places(0, 5120, 1536, 1536, 1536, 512)
        ymix = sgw
        r_t, k_t, v_t = shifted[:, 0:1536], shifted[:, 1536:3072], shifted[:, 3072:4608]
        Z2 = 10240
        qk1, v1, p1, pt1 = places(Z2, 3072, 1536, 2 * 1152, 1152)
        v1 = v1.rearrange("p (t n) -> p t n", t=NT)
        p1 = p1.rearrange("p (b g n) -> p b g n", b=2, g=3)
        pt1 = pt1.rearrange("p (g n) -> p g n", g=3)
        inv_x, inv_y, inv_w, inv_n, scores, avk, vkb, nw, kr, kt, bt = places(
            Z2, 1024, 1024, 1024, 1024, 4096, 1024, 1536, 1024, 1024, 512, 512)
        mats = lambda a: a.rearrange("p (m n) -> p m n", m=8)
        inv_x, inv_y, inv_w, inv_n, avk, nw = (mats(a) for a in (inv_x, inv_y, inv_w, inv_n, avk, nw))
        scores = scores.rearrange("p (m k n) -> p m k n", m=8, k=4)
        vkb = vkb.rearrange("p (m k n) -> p m k n", m=4, k=3)
        kr = kr.rearrange("p (w h k n) -> p w h k n", w=2, h=2, k=2)
        kt, bt = (a.rearrange("p (w n) -> p w n", w=2) for a in (kt, bt))
        norm_kk = arena[:, Z2:Z2 + 1536]
        dev, sq = places(Z2 + 6656, 1536, 1536)
        sig, merged = arena[:, Z2:Z2 + 4096], arena[:, Z2 + 4096:Z2 + 6144]
        ytmp = arena[:, Z2 + 6144:Z2 + 6656].rearrange("p (b n) -> p b n", b=2)
        xn_flat = xn[:].rearrange("p t n -> p (t n)")
        kk = xn_flat[:, 0:1536]
        z_s = xn_flat[:, 1536:1792].rearrange("p (w c n) -> p w c n", w=2, c=2)
        cs = scratch[:, 0:512].rearrange("p (w n) -> p w n", w=2)
        decay = scratch[:, 512:512 + 520].rearrange("p (w c n) -> p w c n", w=2, c=4)
        decay_inv = scratch[:, 1032:1544].rearrange("p (w n) -> p w n", w=2)
        kbuf = scratch[:, 1544:2056].rearrange("p (w n) -> p w n", w=2)
        bbuf = scratch[:, 2056:2568].rearrange("p (w n) -> p w n", w=2)
        state = pre[:].rearrange("p a n -> p (a n)").rearrange("p (w c n) -> p w c n", w=2, c=3)
        trans = rot[:].rearrange("p a n -> p (a n)").rearrange("p (w c n) -> p w c n", w=2, c=2)
        (cm2, v2, zb, gh, ghrep, kcmp, vblk, csm, cpt, lf8, f_pos, f_neg, pb, pt, o2, g2sig, ftmp, cst) = places(
            0, 4096, 1592, 1024, 128, 256, 16, 512, 256, 256, 256, 256, 256, 1536, 768, 2048, 48, 48, 64)
        v2 = v2.rearrange("p (t n) -> p t n", t=NT)
        zb = zb.rearrange("p (i j g c) -> p i j g c", i=2, j=16, g=2)
        gh = gh.rearrange("p (i h n) -> p i h n", i=2, h=2)
        ghrep = ghrep.rearrange("p (h n) -> p h n", h=2)
        vblk = vblk.rearrange("p (h n) -> p h n", h=8)
        lf8 = lf8.rearrange("p (t n) -> p t n", t=2)
        pb = pb.rearrange("p (b n) -> p b n", b=4)
        pt = pt.rearrange("p (b n) -> p b n", b=2)
        g2sig = g2sig.rearrange("p (t n) -> p t n", t=2)
        ident = K("ident")

        s_params, s_const, s_x, s_pos, s_lora, s_layers = (sem(n + "_loaded") for n in ("params", "const", "x", "pos", "lora", "layers"))
        slot_full = [sem("slot0_full"), sem("slot1_full")]
        down_full = [sem("down0_full"), sem("down1_full")]
        ada_used = sem("ada_used")
        up_full = sem("up_full")
        down_done = sem("down_done")
        cm_full = sem("cm_full")
        cm_evac = sem("cm_evac")
        cm_out = sem("cm_out")
        cm_pre = sem("cm_pre")
        rope_full = sem("rope_full")
        rope_used = sem("rope_used")
        tm_full = sem("tm_full")
        tm_ready = sem("tm_ready")
        c_ready = sem("c_ready")
        mod_ready = sem("mod_ready")
        mod_part = sem("mod_part")
        mod_col = sem("mod_col")
        ss_ready = sem("ss_ready")
        ms_ready = sem("ms_ready")
        sd_ready = sem("sd_ready")
        xn_ready = sem("xn_ready")
        ht_full = sem("ht_full")
        ht_act = sem("ht_act")
        ht_dve = sem("ht_dve")
        row_full = sem("row_full")
        row_ready = sem("row_ready")
        silu_ready = sem("silu_ready")
        act_ready = sem("act_ready")
        out_full = sem("out_full")
        fin_read = sem("fin_read")
        x_ready = sem("x_ready")
        fss_ready = sem("fss_ready")
        fms_ready = sem("fms_ready")
        fsd_ready = sem("fsd_ready")
        y_ready = sem("y_ready")
        s_out = sem("s_out")
        dve_step = sem("dve_step")
        pool_step = sem("pool_step")
        raw_zero = sem("raw_zero")
        ang_ready = sem("ang_ready")
        trig_ready = sem("trig_ready")
        ym_full = sem("ym_full")
        ym_read = sem("ym_read")
        ym_ready = sem("ym_ready")
        s1_full = sem("s1_full")
        s1_max = sem("s1_max")
        s1_exp = sem("s1_exp")
        s1_scale = sem("s1_scale")
        s1_prob = sem("s1_prob")
        s1_t = sem("s1_t")
        s1_tr = sem("s1_tr")
        s1_pv = sem("s1_pv")
        s1_o = sem("s1_o")
        lr_in = sem("lr_in")
        lr_full = sem("lr_full")
        lr_ready = sem("lr_ready")
        kk0_ready = sem("kk0_ready")
        sq_ready = sem("sq_ready")
        kn_full = sem("kn_full")
        kn_clamped = sem("kn_clamped")
        kn_sqrt = sem("kn_sqrt")
        kn_rec = sem("kn_rec")
        kk_ready = sem("kk_ready")
        bd_zero = sem("bd_zero")
        cs_ready = sem("cs_ready")
        e_ready = sem("e_ready")
        pool_prep = sem("pool_prep")
        dve_prep = sem("dve_prep")
        bon_full = sem("bon_full")
        bon_ready = sem("bon_ready")
        tr_full = sem("tr_full")
        tr_ready = sem("tr_ready")
        sc_full = sem("sc_full")
        sc_ready = sem("sc_ready")
        y0_ready = sem("y0_ready")
        nl_ready = sem("nl_ready")
        w_full = sem("w_full")
        w_ready = sem("w_ready")
        p_full = sem("p_full")
        xy_ready = sem("xy_ready")
        av_full = sem("av_full")
        av_ready = sem("av_ready")
        nw_full = sem("nw_full")
        nw_ready = sem("nw_ready")
        hg_full = sem("hg_full")
        h_ready = sem("h_ready")
        g_ready = sem("g_ready")
        zt_full = sem("zt_full")
        zt_ready = sem("zt_ready")
        m_full = sem("m_full")
        m_ready = sem("m_ready")
        yc_full = sem("yc_full")
        pass_done = sem("pass_done")
        gn_mu = sem("gn_mu")
        gn_dev = sem("gn_dev")
        gn_sq = sem("gn_sq")
        gn_var = sem("gn_var")
        gn_ms = sem("gn_ms")
        gn_sd = sem("gn_sd")
        gn_rs = sem("gn_rs")
        gn_n = sem("gn_n")
        gn_ready = sem("gn_ready")
        swap_full = sem("swap_full")
        zb_ready = sem("zb_ready")
        cmp_full = sem("cmp_full")
        gelu_ready = sem("gelu_ready")
        ghrep_ready = sem("ghrep_ready")
        cmp2_full = sem("cmp2_full")
        cmp_ready = sem("cmp_ready")
        gate_exp = sem("gate_exp")
        fx_neg = sem("fx_neg")
        fx_exp = sem("fx_exp")
        fx_ln = sem("fx_ln")
        lf_ready = sem("lf_ready")
        f_full = sem("f_full")
        f_ready = sem("f_ready")
        cs_full = sem("cs_full")
        cs_sub = sem("cs_sub")
        cs_exp = sem("cs_exp")
        cs_prob = sem("cs_prob")
        cst_full = sem("cst_full")
        cpt_ready = sem("cpt_ready")
        s_full = sem("s_full")
        s_max = sem("s_max")
        p_raw = sem("p_raw")
        r_scale = sem("r_scale")
        p_ready = sem("p_ready")
        t_full = sem("t_full")
        t_ready = sem("t_ready")
        pv_full = sem("pv_full")
        o_ready = sem("o_ready")

        pool_zb = sem("pool_zb")

        def up_slot(g):
            return ring[:, g % 2, :]

        def full_count(g, more=0):
            return 16 * (g // 2 + 1) + 8 * more

        block = ctx.enter_context(nc.Block())

        def tiles(kinds, dests):
            out, q, r = [], 0, 0
            for kind, dest in zip(kinds, dests):
                out.append((kind, q if kind in ("shift", "rope1", "rope2") else None,
                            r if kind in ("rope1", "rope2") else None, dest))
                q += kind in ("shift", "rope1", "rope2")
                r += kind in ("rope1", "rope2")
            return out, q, r

        T1, Q1, R1 = tiles(["shift"] * SHIFT_TILES + ["rope1"] * 12,
                           [shifted[:, j * S:(j + 1) * S] for j in range(SHIFT_TILES)] + [qk1[:, j * S:(j + 1) * S] for j in range(12)])
        TG, _, _ = tiles(["sigmoid"] * 16, [sig[:, j * S:(j + 1) * S] for j in range(16)])
        T2, Q2, R2 = tiles(["rope2", "copy", "rope2", "rope2"] + ["rope2"] * 4 + ["copy"] * 4 + ["rope2"] * 4,
                           [cm2[:, j * S:(j + 1) * S] for j in range(16)])
        CM_G, CM_2 = len(T1), len(T1) + len(TG)

        def since(base, k):
            return base + max(k, 0)

        def behind(base, k):
            return base + k if k > 0 else 0

        UNITS = []
        for t in range(4):
            for branch, ktile, v0 in ((1, 2, 0), (2, 3, 128)):
                for e in range(2):
                    UNITS.append((t, e, 4 + t, ktile, v0 + e * HD, 3 * (t + 4 * e) + branch, None))
        for t in range(2):
            for e in range(2):
                UNITS.append((4 + t, e, 8 + t, 10 + t, 256 + (2 * t + e) * HD, None, 2 * t + e))
        for t in range(2):
            for e in range(2):
                UNITS.append((6 + t, e, 12 + t, 14 + t, 512 + (2 * t + e) * HD, None, None))
        NU = len(UNITS)
        LAST_OF_PAIR = {u[0]: i for i, u in enumerate(UNITS)}
        S_BANK, T_BANK, O_BANK = (4, 5, 6), (7, 2), (1, 3)

        def half(e):
            return slice(HD * e, HD * e + HD)


        @block.sync
        def _(sp):
            sp.dma_start(params[:], T["params"]).then_inc(s_params, 16)
            released = [None, None]

            def load(g, src, release):
                if released[0]:
                    wait(sp, *released[0])
                n = src.shape[-1]
                sp.dma_start(ring[:, g % 2, 0:n], src).then_inc(slot_full[g % 2], 16)
                released[:] = [released[1], release]

            def ada(g, half_first, chunks, used):
                two = T["ada"].rearrange("(c s) p n -> c s p n", s=2)
                for s in range(2):
                    load(g + s, two[half_first, s], (ada_used, used + s + 1))
                with sp.Fori(1, chunks // 2) as i:
                    for s in range(2):
                        sp.wait_ge(ada_used, used + 2 * i + s - 1)
                        sp.dma_start(ring[:, (g + s) % 2], two[half_first + i, s]).then_inc(slot_full[(g + s) % 2], 16)
                released[:] = [(ada_used, used + chunks - 1), (ada_used, used + chunks)]

            def ffn(g, f):
                def down(c, i=0):
                    wait(sp, down_done, FC * f + (c + i - 1 if c >= 2 else 0))
                    sp.dma_start(ring_down[:, c % 2], T["down"][FC * f + c + i]).then_inc(down_full[c % 2], 16)

                for c in range(2):
                    load(g + c, T["up"][FC * f + c], (up_full, FC * f + c + 1))
                    down(c)
                with sp.Fori(0, FC - 3, 2) as i:
                    for c in (2, 3):
                        sp.wait_ge(up_full, FC * f + c + i - 1)
                        sp.dma_start(ring[:, (g + c) % 2], T["up"][FC * f + c + i]).then_inc(slot_full[(g + c) % 2], 16)
                        down(c, i)
                c = FC - 1
                sp.wait_ge(up_full, FC * f + c - 1)
                sp.dma_start(ring[:, (g + c) % 2], T["up"][FC * f + c]).then_inc(slot_full[(g + c) % 2], 16)
                down(c)
                released[:] = [(up_full, FC * f + FC - 1), (up_full, FC * f + FC)]

            load(0, T["ada"][0], (ada_used, 1))
            sp.dma_start(const[:], T["const"]).then_inc(s_const, 16)
            sp.dma_start(x[:], T["x"].rearrange("p (t n) -> p t n", t=NT)).then_inc(s_x, 16)
            load(1, T["ada"][1], (ada_used, 2))
            sp.dma_start(early, T["early"]).then_inc(s_lora, 16)
            sp.dma_start(pos_i, T["pos"].broadcast_to([P, S])).then_inc(s_pos, 16)
            with sp.Fori(2, ADA1_CHUNKS, 2) as i:
                for s in range(2):
                    sp.wait_ge(ada_used, i + s - 1)
                    sp.dma_start(ring[:, s], T["ada"][i + s]).then_inc(slot_full[s], 16)
            released[:] = [(ada_used, ADA1_CHUNKS - 1), (ada_used, ADA1_CHUNKS)]

            g = G_MIX1
            for c in range(8):
                load(g + c, T["in1"][c], (cm_full, 4 * (c + 1)))
            load(g + 8, T["in1"][8], (tm_full, 2))
            load(g + 9, T["in1_v"], (tm_full, 4))
            for c in range(4):
                load(g + 10 + c, T["gates1"][c], (cm_full, 32 + 4 * (c + 1)))
            load(g + 14, T["w_b"], (ym_full, 8))
            for c in range(2):
                load(g + 15 + c, T["w_a"][c], (ym_full, 8 + 4 * (c + 1)))
            for c in range(2):
                load(g + 17 + c, T["w_out"][c], (out_full, c + 1))
            sp.wait_ge(pass_done, PAIRS // 2)
            ffn(G_FFN1, 0)
            with sp.Fori(0, LAYERS) as l:
                released[:] = [(up_full, FC * (1 + 2 * l) - 1), (up_full, FC * (1 + 2 * l))]
                ada(G_LAYER, ADA1_CHUNKS // 2 + ADA2_CHUNKS // 2 * l, ADA2_CHUNKS, ADA1_CHUNKS + ADA2_CHUNKS * l)
                sp.wait_ge(x_ready, 8 + 12 * l)
                sp.dma_start(now[:], T["layers"][l]).then_inc(s_layers, 16)
                ffn(G_LAYER + 18, 1 + 2 * l)
                g = G_LAYER + 18 + FC
                for c in range(4):
                    a, w = IN2_AT[c], 8 * IN2_WIDTHS[c]
                    load(g + c, T["in2"][l, :, a:a + w], (cm_full, 48 + 16 * l + 4 * (c + 1)))
                for c in range(2):
                    load(g + 4 + c, T["cmp1"][2 * l + c], (cmp_full, 2 * l + c + 1))
                for c in (4, 5):
                    a, w = IN2_AT[c], 8 * IN2_WIDTHS[c]
                    load(g + 2 + c, T["in2"][l, :, a:a + w], (tm_full, 4 + 4 * l + 2 * (c - 3)))
                for c in range(2):
                    load(g + 8 + c, T["w_out2"][2 * l + c], (out_full, 2 + 2 * l + c + 1))
                ffn(g + MIX2_CHUNKS, 2 + 2 * l)
            sp.wait_ge(y_ready, NT)
            sp.dma_start(out, xn[:]).then_inc(s_out, 16)
            sp.wait_ge(s_out, 16)
        @block.tensor
        def _(pe):
            mm = pe.matmul

            def chunk(g, more=0):
                pe.wait_ge(slot_full[g % 2], full_count(g, more))
                return up_slot(g)

            def ada(g, chunks, which, used, more=0):
                def one(c, i=0):
                    w = chunk(g + c, more + i)
                    wait(pe, mod_part, used + c + i - 1)
                    for k in range(KD):
                        last = mm(bank[6 + c % 2], silu_c[:, which + k:which + k + 1].broadcast_to([P, P]), w[:, k * 512:(k + 1) * 512],
                                  start=(k == 0), stop=(k == KD - 1))
                    last.then_inc(ada_used, 1)

                one(0)
                one(1)
                with pe.Fori(0, chunks - 2, 2) as i:
                    one(2, i)
                    one(3, i)

            def transposes(n):
                pe.wait_ge(xn_ready, 2 * n + 2)
                for b in range(4):
                    for k in range(2):
                        for t in range(NT):
                            last = pe.transpose(bank[4 + b][:, k * S + t * P:k * S + t * P + P],
                                                xn[:, t, (2 * b + k) * P:(2 * b + k + 1) * P], ident)
                    last.then_inc(ht_full, 1)

            def gate_row(n, column):
                wait(pe, fin_read, 4 * n)
                for k in range(KD):
                    last = mm(bank[k // 4][:, (k % 4) * P:(k % 4 + 1) * P], column[:, k:k + 1].broadcast_to([P, P]), ident,
                              start=True, stop=True)
                last.then_inc(row_full, 1)

            def wait_ht(n):
                pe.wait_ge(ht_act, n + 1)
                pe.wait_ge(ht_dve, n + 1)

            def ffn(g, f, n, more=0):
                def up(c, i=0):
                    w = chunk(g + c, more + i)
                    if c >= 2:
                        pe.wait_ge(act_ready, FC * f + c + i - 1)
                    for j in range(4):
                        dst = bank[4 + 2 * (c % 2) + j // 2][:, (j % 2) * S:(j % 2 + 1) * S]
                        for k in range(KD):
                            last = mm(dst, w[:, k * 512 + j * P:k * 512 + j * P + P], hT[:, k, :],
                                      start=(k == 0), stop=(k == KD - 1))
                    last.then_inc(up_full, 1)

                def down(c, i=0):
                    pe.wait_ge(act_ready, FC * f + c + i + 1)
                    pe.wait_ge(down_full[c % 2], 16 * ((6 - c % 2) * f + c // 2 + 1) + 8 * i)
                    for k in range(2):
                        for t in range(NT):
                            for h in range(2):
                                last = mm(bank[2 * t + h], act_t[:, c % 2, k, t * P:(t + 1) * P],
                                          ring_down[:, c % 2, k * D + h * 512:k * D + h * 512 + 512],
                                          start=(c == 0 and k == 0), stop=(c == FC - 1 and k == 1), skip_group_check=True)
                    last.then_inc(down_done, 1)

                wait_ht(n)
                up(0)
                up(1)
                pe.wait_ge(row_ready, n + 1)
                down(0)
                with pe.Fori(0, FC - 3, 2) as i:
                    up(2, i)
                    down(1, i)
                    up(3, i)
                    down(2, i)
                up(FC - 1)
                down(FC - 2)
                down(FC - 1)

            def channel_major(g, table, base, rbase, more=0):
                def rotate(j):
                    kind, q, r, _ = table[j]
                    if r is None:
                        return
                    pe.wait_ge(cm_evac, base + j + 1)
                    wait(pe, rope_used, since(rbase, r - 1))
                    mm(bank[6 + r % 2][:, 0:S], K(kind), raw[:, q % 3, 1:S + 1], start=True, stop=True).then_inc(rope_full, 1)

                for j in range(len(table)):
                    if j % 4 == 0:
                        w = chunk(g + j // 4, more)
                    wait(pe, cm_evac, since(base, j - 1))
                    n = j % 4
                    for k in range(KD):
                        last = mm(bank[4 + j % 2][:, 0:S], w[:, k * 512 + n * P:k * 512 + n * P + P], hT[:, k, :],
                                  start=(k == 0), stop=(k == KD - 1))
                    last.then_inc(cm_full, 1)
                    if j:
                        rotate(j - 1)
                rotate(len(table) - 1)

            def token_major(g, width, banks, more=0):
                w = chunk(g, more)
                for t in range(NT):
                    for k in range(KD):
                        last = mm(bank[banks[t]][:, 0:width], hT[:, k, t * P:(t + 1) * P], w[:, k * width:(k + 1) * width],
                                  start=(k == 0), stop=(k == KD - 1))
                    last.then_inc(tm_full, 1)

            def project(g, lhs, more=0):
                for h in range(2):
                    w = chunk(g + h, more)
                    for t in range(NT):
                        for k in range(KD):
                            last = mm(bank[2 * t + h], lhs(k, t), w[:, k * 512:(k + 1) * 512], start=(k == 0), stop=(k == KD - 1))
                    last.then_inc(out_full, 1)

            def attention1():
                def heads(i):
                    return [((4 * g + i) // 2, half(i % 2), (4 * g + i) * HD) for g in range(3)]

                def qk(i):
                    wait(pe, s1_max, i)
                    for g, (tile, h, _) in enumerate(heads(i)):
                        q, k = qk1[h, tile * S:(tile + 1) * S], qk1[h, (6 + tile) * S:(7 + tile) * S]
                        mm(bank[4 + g][:, 0:P], q[:, 0:P], k[:, 0:P], start=True, stop=True)
                        last = mm(bank[4 + g][:, P:P + S], q[:, P:S], k, start=True, stop=True)
                    last.then_inc(s1_full, 1)

                pe.wait_ge(cm_out, Q1)
                pe.wait_ge(tm_ready, 4)
                qk(0)
                for i in range(4):
                    if i < 3:
                        qk(i + 1)
                    pe.wait_ge(s1_prob, i + 1)
                    wait(pe, s1_tr, 3 * i)
                    for g in range(3):
                        b = bank[(7, 2, 1)[g]]
                        for n in range(3):
                            last = pe.transpose(b[:, n * P:(n + 1) * P], p1[:, i % 2, g, n * P:(n + 1) * P], ident)
                        last.then_inc(s1_t, 1)
                    pe.wait_ge(s1_tr, 3 * i + 3)
                    dst = bank[3][half(i % 2), (i // 2) * S:(i // 2 + 1) * S]
                    wait(pe, s1_o, i)
                    for g, (_, _, vc) in enumerate(heads(i)):
                        mm(dst, v1[:, 0, vc:vc + HD], pt1[:, g, 0:S], start=(g == 0), stop=False, skip_group_check=True)
                        last = mm(dst[:, P:S], v1[:, 1, vc:vc + HD], pt1[:, g, S:S + P], start=False, stop=(g == 2), skip_group_check=True)
                    last.then_inc(s1_pv, 1)

            def rwkv():
                pe.wait_ge(lr_in, 1)
                pe.wait_ge(s1_o, 4)
                pe.wait_ge(s_lora, 16)
                for w in range(PAIRS):
                    wait(pe, lr_ready, w - 1)
                    b0, b1 = bank[4 + 2 * (w % 2)], bank[5 + 2 * (w % 2)]
                    c = slice(w * P, (w + 1) * P)
                    mm(b0[:, 0:S], lora[0:64, c], shifted[0:64, 18 * S:19 * S], start=True, stop=True)
                    mm(b1[:, 0:S], lora[64:128, c], shifted[64:128, 18 * S:19 * S], start=True, stop=True)
                    mm(b0[:, S:2 * S], lora[:, RW + w * P:RW + (w + 1) * P], shifted[:, 19 * S:20 * S],
                       start=True, stop=True).then_inc(lr_full, 1)
                pe.wait_ge(sq_ready, 1)
                for n in range(3):
                    last = mm(bank[n], K("blockones"), norm_kk[:, n * 512:(n + 1) * 512], start=True, stop=True)
                last.then_inc(kn_full, 1)
                pe.wait_ge(lr_ready, PAIRS)
                pe.wait_ge(kn_clamped, 1)
                for ps in range(PAIRS // 2):
                    wait(pe, pass_done, ps)
                    for lp in range(2):
                        w = 2 * ps + lp
                        pe.wait_ge(pool_prep, w + 1)
                        pe.wait_ge(dve_prep, w + 1)
                        wait(pe, bon_ready, w)
                        mm(bank[3][:, 0:S], K("blockones"), cs[:, lp], start=True, stop=True).then_inc(bon_full, 1)
                        for h in range(2):
                            t = slice(h * P, (h + 1) * P)
                            n = 2 * w + h
                            wait(pe, tr_ready, n - 1)
                            b = bank[2 - h]
                            for j, src in enumerate((v_t[:, w * S:(w + 1) * S][:, t], kbuf[:, lp, t], bbuf[:, lp, t], kr[:, lp, h, 0])):
                                last = pe.transpose(b[:, j * P:(j + 1) * P], src, ident)
                            last.then_inc(tr_full, 1)
                            wait(pe, sc_ready, n)
                            for e in range(2):
                                hs = half(e)
                                both = kr[hs, lp, h].rearrange("p k n -> p (k n)")
                                mm(bank[4 + e][:, 0:S], bt[hs, lp, t], both, start=True, stop=True)
                                mm(bank[4 + e][:, S:2 * S], kt[hs, lp, t], both, start=True, stop=True)
                                last = mm(bank[6 + e][:, 0:P], kr[hs, lp, h, 0], bt[hs, lp, t], start=True, stop=True)
                            last.then_inc(sc_full, 1)
                    pe.wait_ge(sc_ready, 4 * (ps + 1))
                    pe.wait_ge(tr_ready, 4 * (ps + 1))
                    for m in range(8):
                        e = m % 2
                        last = mm(bank[6][:, m * HD:(m + 1) * HD], scores[:, m, 2], vkb[:, m // 2, 0, e * HD:(e + 1) * HD],
                                  start=True, stop=True)
                    last.then_inc(av_full, 1)
                    pe.wait_ge(y0_ready, 4 * (ps + 1))
                    pe.wait_ge(bon_ready, 2 * (ps + 1))
                    for j in range(len(LEVELS)):
                        q = (ps * len(LEVELS) + j) * 2
                        for lp in range(2):
                            pe.wait_ge(nl_ready, q + lp + 1)
                            if j:
                                pe.wait_ge(xy_ready, q + lp - 1)
                            wait(pe, w_ready, q + lp - 1)
                            for n in range(4):
                                m = 4 * lp + n
                                last = mm(bank[lp][:, n * P:(n + 1) * P], inv_n[:, m], inv_x[:, m], start=True, stop=True)
                            last.then_inc(w_full, 1)
                        for lp in range(2):
                            pe.wait_ge(w_ready, q + lp + 1)
                            for n in range(4):
                                m = 4 * lp + n
                                c = slice(n * P, (n + 1) * P)
                                if j < len(LEVELS) - 1:
                                    mm(bank[2 + lp][:, c], inv_y[:, m], inv_w[:, m], start=True, stop=True)
                                last = mm(bank[4 + lp][:, c], inv_w[:, m], inv_y[:, m], start=True, stop=True)
                            last.then_inc(p_full, 1)
                    pe.wait_ge(xy_ready, 10 * (ps + 1))
                    pe.wait_ge(av_ready, ps + 1)
                    for m in range(8):
                        last = mm(bank[m // 4][:, (m % 4) * P:(m % 4 + 1) * P], inv_y[:, m], avk[:, m], start=True, stop=True)
                    last.then_inc(nw_full, 1)
                    pe.wait_ge(nw_ready, ps + 1)
                    for m in range(8):
                        lp, h, e = m // 4, (m // 2) % 2, m % 2
                        c = slice(lp * S + h * P, lp * S + (h + 1) * P)
                        mm(bank[2][half(e), c], vkb[:, m // 2, 0, e * HD:(e + 1) * HD], scores[:, m, 3], start=True, stop=False, skip_group_check=True)
                        mm(bank[2][half(e), c], nw[:, m, 0:HD], scores[:, m, 1], start=False, stop=True, skip_group_check=True)
                        last = mm(bank[3][half(e), c], nw[:, m, HD:P], scores[:, m, 1], start=True, stop=True)
                    last.then_inc(hg_full, 1)
                    for lp in range(2):
                        for e in range(2):
                            ec = slice(e * HD, (e + 1) * HD)
                            for c, b, z, t in ((0, 6, 0, None), (2, 6, 64, 128), (1, 7, 0, 64)):
                                m = 4 * lp + 2 * (c // 2) + e
                                rows = slice(HD * (c % 2), HD * (c % 2) + HD)
                                v, kp, bp = (vkb[rows, m // 2, k, ec] for k in range(3))
                                dst = bank[b][half(e), lp * S + z:lp * S + z + HD]
                                mm(dst, kp, v, start=True, stop=False, skip_group_check=True)
                                last = mm(dst, bp, nw[rows, m, 0:HD], start=False, stop=True, skip_group_check=True)
                                if t is not None:
                                    last = mm(bank[b][half(e), lp * S + t:lp * S + t + HD], nw[rows, m, HD:P], bp, start=True, stop=True)
                    last.then_inc(zt_full, 1)
                    for step in range(2):
                        pe.wait_ge(zt_ready, ps + 1)
                        if step:
                            pe.wait_ge(m_ready, 2 * ps + 1)
                        for lp in range(2):
                            last = mm(bank[step][:, lp * P:(lp + 1) * P], trans[:, lp, step], state[:, lp, step], start=True, stop=True)
                        last.then_inc(m_full, 1)
                    pe.wait_ge(m_ready, 2 * ps + 2)
                    pe.wait_ge(g_ready, ps + 1)
                    for lp in range(2):
                        for c in range(1, 4):
                            last = mm(bank[4][:, lp * S + c * C:lp * S + (c + 1) * C], state[:, lp, c - 1],
                                      kr[:, lp, c // 2, 1, (c % 2) * C:(c % 2 + 1) * C], start=True, stop=True)
                    last.then_inc(yc_full, 1)
                pe.wait_ge(pass_done, PAIRS // 2)
                for n in range(3):
                    last = mm(bank[n], K("blockones"), ymix[:, n * 512:(n + 1) * 512], start=True, stop=True)
                last.then_inc(gn_mu, 1)
                pe.wait_ge(gn_sq, 1)
                for n in range(3):
                    last = mm(bank[5 + n], K("blockones"), sq[:, n * 512:(n + 1) * 512], start=True, stop=True)
                last.then_inc(gn_var, 1)

            def merge():
                w = chunk(G_MIX1 + 14)
                pe.wait_ge(cm_evac, CM_G + 16)
                for n in range(16):
                    if n >= 8 and n % 4 == 0:
                        w = chunk(G_MIX1 + 15 + (n - 8) // 4)
                    if n == 8:
                        pe.wait_ge(gn_ready, PAIRS)
                    wait(pe, ym_read, n - 1)
                    for k in range(2 if n < 8 else 6):
                        if n < 8:
                            lhs, rhs = w[:, k * D + n * P:k * D + n * P + P], o1[:, k * S:(k + 1) * S]
                        else:
                            lhs, rhs = w[:, k * 512 + (n % 4) * P:k * 512 + (n % 4) * P + P], ymix[:, k * S:(k + 1) * S]
                        last = mm(bank[4 + n % 2][:, 0:S], lhs, rhs, start=(k == 0), stop=(k == (1 if n < 8 else 5)))
                    last.then_inc(ym_full, 1)

            def mixer2(l):
                n = 3 + 3 * l
                more = PER_LAYER * l
                g = G_LAYER + 18 + FC
                base, qbase, rbase, U = CM_2 + 16 * l, Q1 + Q2 * l, R1 + R2 * l, NU * l
                wait_ht(n)
                channel_major(g, T2, base, rbase, more)
                pe.wait_ge(row_ready, n + 1)
                pe.wait_ge(cm_out, qbase + 1)
                for i in range(2):
                    last = mm(bank[i][:, 0:S], K("swap"), cm2[:, i * S:(i + 1) * S], start=True, stop=True)
                last.then_inc(swap_full, 1)
                for i in range(2):
                    w = chunk(g + 4 + i, more)
                    if i == 0:
                        pe.wait_ge(zb_ready, l + 1)
                    for h in range(2):
                        for j in range(16):
                            last = mm(bank[2][:, (2 * i + h) * 32:(2 * i + h + 1) * 32], w[:, j * S + h * P:j * S + h * P + P],
                                      zb[:, i, j].rearrange("p g c -> p (g c)"), start=(j == 0), stop=(j == 15))
                    last.then_inc(cmp_full, 1)
                pe.wait_ge(cm_evac, base + 16)
                pe.wait_ge(rope_used, rbase + R2)
                token_major(g + 6, 512, (4, 5), more)
                token_major(g + 7, IN2_WIDTHS[5], (6, 7), more)
                pe.wait_ge(gelu_ready, l + 1)
                for e in range(2):
                    for h in range(2):
                        mm(bank[3][half(e), 0:16], NOW("cmp_w2", h * HD, (h + 1) * HD), gh[:, 0, h, e * 16:(e + 1) * 16],
                           start=(h == 0), stop=(h == 1), skip_group_check=True)
                pe.wait_ge(ghrep_ready, l + 1)
                for h in range(2):
                    last = mm(bank[3][:, 64:128], ghrep[:, h], NOW("cmp_w2", (2 + h) * HD, (3 + h) * HD),
                              start=(h == 0), stop=(h == 1), skip_group_check=True)
                last.then_inc(cmp2_full, 1)
                pe.wait_ge(lf_ready, l + 1)
                mm(bank[2][:, 0:P], lf8[:, 0], K("tri"), start=True, stop=True)
                mm(bank[2][:, P:S], lf8[:, 0], K("ones"), start=True, stop=False, skip_group_check=True)
                mm(bank[2][:, P:S], lf8[:, 1], K("tri"), start=False, stop=True, skip_group_check=True).then_inc(f_full, 1)
                pe.wait_ge(cmp_ready, l + 1)
                pe.wait_ge(cm_out, qbase + Q2)
                for e in range(2):
                    for t in range(NT):
                        for j in range(4):
                            last = mm(bank[e][:, t * 64 + j * 16:t * 64 + (j + 1) * 16], cm2[half(e), (4 + j) * S + t * P:(4 + j) * S + (t + 1) * P],
                                      kcmp[half(e), 0:16], start=True, stop=True)
                last.then_inc(cs_full, 1)
                pe.wait_ge(cs_prob, l + 1)
                for t in range(NT):
                    last = pe.transpose(bank[0][:, t * P:(t + 1) * P], csm[:, t * P:(t + 1) * P], ident)
                last.then_inc(cst_full, 1)
                pe.wait_ge(tm_ready, 8 + 4 * l)
                pe.wait_ge(f_ready, l + 1)

                def qk(u):
                    _, e, qt, ktile, _, _, fox = UNITS[u]
                    wait(pe, s_max, behind(U, u - 2))
                    b = bank[S_BANK[u % 3]]
                    q, k = cm2[half(e), qt * S:(qt + 1) * S], cm2[half(e), ktile * S:(ktile + 1) * S]
                    for qs, ks, dst in ((slice(0, P), slice(0, P), b[:, 0:P]), (slice(P, S), slice(0, S), b[:, P:P + S])):
                        last = mm(dst, q[:, qs], k[:, ks], start=True, stop=(fox is None), skip_group_check=True)
                        if fox is not None:
                            pick = K("fox_row", fox, fox + 1)[half(e)]
                            width = ks.stop - ks.start
                            mm(dst, pick.broadcast_to([HD, P]), f_neg[half(e), ks], start=False, stop=False, skip_group_check=True)
                            last = mm(dst, f_pos[half(e), qs], pick.broadcast_to([HD, width]), start=False, stop=True, skip_group_check=True)
                    last.then_inc(s_full, 1)

                def turn(u):
                    pe.wait_ge(p_ready, U + u + 1)
                    wait(pe, t_ready, behind(U, u - 1))
                    b = bank[T_BANK[u % 2]]
                    for n in range(3):
                        last = pe.transpose(b[:, n * P:(n + 1) * P], pb[:, u % 4, n * P:(n + 1) * P], ident)
                    last.then_inc(t_full, 1)

                def pv(u):
                    pair, e, _, _, vc, gate, _ = UNITS[u]
                    first = not any(x[0] == pair and x[1] == e for x in UNITS[:u])
                    final = not any(x[0] == pair and x[1] == e for x in UNITS[u + 1:])
                    dst = bank[O_BANK[pair % 2]][half(e), 0:S]
                    if first:
                        wait(pe, o_ready, behind(8 * l, pair - 1))
                        if gate is not None:
                            pe.wait_ge(cpt_ready, l + 1)
                            mm(dst, vblk[:, pair + 4 * e], cpt, start=True, stop=False, skip_group_check=True)
                    pe.wait_ge(t_ready, U + u + 1)
                    mm(dst, v2[:, 0, vc:vc + HD], pt[:, u % 2, 0:S], start=(first and gate is None), stop=False, skip_group_check=True)
                    mm(dst[:, P:S], v2[:, 1, vc:vc + HD], pt[:, u % 2, S:S + P], start=False, stop=final,
                       skip_group_check=True).then_inc(pv_full, 1)

                for i in range(NU + 3):
                    if i < NU:
                        qk(i)
                    if 2 <= i < NU + 2:
                        turn(i - 2)
                    if i >= 3:
                        pv(i - 3)
                pe.wait_ge(o_ready, 8 * (l + 1))
                project(g + 8, lambda k, t: o2[:, k * S + t * P:k * S + (t + 1) * P], more)

            pe.wait_ge(s_const, 16)
            pe.wait_ge(c_ready, 1)
            ada(0, ADA1_CHUNKS, 0, 0)
            pe.wait_ge(mod_ready, 1)
            gate_row(0, mod_gate[:, 0])
            transposes(0)
            wait_ht(0)
            channel_major(G_MIX1, T1, 0, 0)
            pe.wait_ge(row_ready, 1)
            token_major(G_MIX1 + 8, 512, (0, 1))
            token_major(G_MIX1 + 9, 256, (2, 3))
            attention1()
            rwkv()
            pe.wait_ge(gn_ms, 1)
            channel_major(G_MIX1 + 10, TG, CM_G, 0)
            merge()
            pe.wait_ge(ym_ready, 8)
            project(G_MIX1 + 17, lambda k, t: merged[:, k * S + t * P:k * S + (t + 1) * P])
            gate_row(1, mod_gate[:, 1])
            transposes(1)
            ffn(G_FFN1, 0, 1)
            with pe.Fori(0, LAYERS) as l:
                more = PER_LAYER * l
                ada(G_LAYER, ADA2_CHUNKS, KD, ADA1_CHUNKS + ADA2_CHUNKS * l, more)
                pe.wait_ge(mod_ready, 2 + l)
                gate_row(2 + 3 * l, mod_gate[:, 0])
                transposes(2 + 3 * l)
                ffn(G_LAYER + 18, 1 + 2 * l, 2 + 3 * l, more)
                gate_row(3 + 3 * l, mod_gate[:, 1])
                transposes(3 + 3 * l)
                mixer2(l)
                gate_row(4 + 3 * l, mod_gate[:, 2])
                transposes(4 + 3 * l)
                ffn(G_LAYER + 18 + FC + MIX2_CHUNKS, 2 + 2 * l, 4 + 3 * l, more)
            gate_row(8, PR("final_g"))

        @block.scalar
        def _(act):
            f = act.activation

            def norm(n, sub, rows=True):
                for t in range(NT):
                    if isinstance(n, int) and n == 0:
                        act.wait_ge(s_x, 16)
                    else:
                        act.wait_ge(x_ready, 4 * n - 2 * (1 - t))
                    f(xn[:, t], x[:, t], ACT.Square, accum_out=stat[:, t:t + 1]).then_inc(ss_ready, 1)
                act.wait_ge(ms_ready, n + 1)
                f(stat[:, 4:6], stat[:, 2:4], ACT.Sqrt).then_inc(sd_ready, 1)
                act.wait_ge(row_full, n + 1)
                f(row[:], psum[:, 0:2, :].rearrange("p b n -> p (b n)"), ACT.Copy).then_inc(row_ready, 1)
                if not rows:
                    return
                for b in range(2):
                    act.wait_ge(ht_full, 4 * n + b + 1)
                    for k in (2 * b, 2 * b + 1):
                        last = f(hT[:, k], bank[4 + b][:, (k % 2) * S:(k % 2 + 1) * S], ACT.Identity,
                                 bias=mod[:, 24 * sub + k:24 * sub + k + 1], scale=mod_scale[:, sub, k:k + 1])
                last.then_inc(ht_act, 1)

            def channel_major(table, base, qbase):
                for j, (kind, q, _, dest) in enumerate(table):
                    act.wait_ge(cm_full, base + j + 1)
                    if q is not None:
                        wait(act, cm_out, since(qbase, q - 2))
                        dest = raw[:, q % 3, 1:S + 1]
                    f(dest, bank[4 + j % 2][:, 0:S], ACT.Sigmoid if kind == "sigmoid" else ACT.Copy).then_inc(cm_evac, 1)

            def ffn(fn):
                def one(c, i=0):
                    act.wait_ge(up_full, FC * fn + c + i + 1)
                    wait(act, act_ready, FC * fn + c + i - 1 if c >= 2 else FC * fn)
                    f(silu[:, c % 2], bank[4 + 2 * (c % 2)], ACT.Silu).then_inc(silu_ready, 1)
                one(0)
                one(1)
                with act.Fori(0, FC - 3, 2) as i:
                    one(2, i)
                    one(3, i)
                one(FC - 1)

            def rms_of_output(n, source, value):
                act.wait_ge(source, value)
                for j in range(4):
                    f(xn_flat[:, j * 512:(j + 1) * 512], bank[j], ACT.Square, accum_out=stat[:, 8 + j:9 + j]).then_inc(fss_ready, 1)
                act.wait_ge(fms_ready, n + 1)
                f(stat[:, 14:16], stat[:, 12:14], ACT.Sqrt).then_inc(fsd_ready, 1)

            def attention1():
                def exps(i):
                    act.wait_ge(s1_max, i + 1)
                    c = 2 * (i % 2)
                    for q, (a, b) in enumerate(((0, P), (P, 384))):
                        last = f(p1[:, i % 2, :, a:b], p1[:, i % 2, :, a:b], ACT.Exp, bias=nb[:, c + q:c + q + 1], scale=SCALE,
                                 accum_out=rs[:, c + q:c + q + 1])
                    last.then_inc(s1_exp, 1)
                exps(0)
                for i in range(4):
                    if i < 3:
                        exps(i + 1)
                    act.wait_ge(s1_pv, i + 1)
                    c = slice((i // 2) * S, (i // 2 + 1) * S)
                    f(o1[half(i % 2), c], bank[3][half(i % 2), c], ACT.Copy).then_inc(s1_o, 1)

            def rwkv():
                act.wait_ge(cm_out, SHIFT_TILES)
                f(shifted[0:64, 18 * S:19 * S], shifted[0:64, 18 * S:19 * S], ACT.Tanh)
                f(shifted[:, 19 * S:20 * S], shifted[:, 19 * S:20 * S], ACT.Sigmoid).then_inc(lr_in, 1)
                for w in range(PAIRS):
                    act.wait_ge(lr_full, w + 1)
                    b0, b1 = bank[4 + 2 * (w % 2)], bank[5 + 2 * (w % 2)]
                    c = slice(w * S, (w + 1) * S)
                    f(sgw[:, c], b0[:, 0:S], ACT.Sigmoid, bias=PR("w0", w, w + 1))
                    f(iclr[:, c], b1[:, 0:S], ACT.Sigmoid, bias=PR("a0", w, w + 1))
                    f(gate1[:, c], b0[:, S:2 * S], ACT.Copy).then_inc(lr_ready, 1)
                act.wait_ge(kn_clamped, 1)
                f(norm_kk, norm_kk, ACT.Sqrt).then_inc(kn_sqrt, 1)
                for ps in range(PAIRS // 2):
                    wait(act, pass_done, ps)
                    for lp in range(2):
                        act.wait_ge(cs_ready, 2 * ps + lp + 1)
                        act.wait_ge(bd_zero, 1)
                        c4 = cs[:, lp].rearrange("p (c n) -> p c n", c=4)
                        f(decay[:, lp, :, 1:C + 1], c4, ACT.Exp, scale=-DECAY)
                        f(decay_inv[:, lp], cs[:, lp], ACT.Exp, scale=DECAY).then_inc(e_ready, 1)
                    act.wait_ge(av_full, ps + 1)
                    f(avk[:, :, 0:HD], bank[6].rearrange("p (m n) -> p m n", m=8), ACT.Copy).then_inc(av_ready, 1)
                    for j in range(len(LEVELS)):
                        for lp in range(2):
                            q = (ps * len(LEVELS) + j) * 2 + lp
                            act.wait_ge(w_full, q + 1)
                            wait(act, p_full, q - 1)
                            f(inv_w[:, 4 * lp:4 * lp + 4].rearrange("p m n -> p (m n)"), bank[lp], ACT.Copy).then_inc(w_ready, 1)
                    act.wait_ge(nw_full, ps + 1)
                    f(nw.rearrange("p m n -> p (m n)"), psum[:, 0:2].rearrange("p b n -> p (b n)"), ACT.Copy, scale=-1.0).then_inc(nw_ready, 1)
                    act.wait_ge(hg_full, ps + 1)
                    f(ymix[:, ps * 512:(ps + 1) * 512], bank[2], ACT.Copy).then_inc(h_ready, 1)
                act.wait_ge(gn_ms, 1)
                f(sq, sq, ACT.Sqrt).then_inc(gn_sd, 1)

            def mixer2(l):
                base, qbase, U = CM_2 + 16 * l, Q1 + Q2 * l, NU * l
                channel_major(T2, base, qbase)
                act.wait_ge(cmp_full, 2 * l + 2)
                f(gh.rearrange("p i h n -> p (i h n)"), bank[2][:, 0:P], ACT.Gelu_apprx_tanh).then_inc(gelu_ready, 1)
                for i, (c0, c1) in enumerate(((0, 512), (512, 796))):
                    for t in range(NT):
                        act.wait_ge(tm_full, 4 + 4 * l + 2 * i + t + 1)
                        f(v2[:, t, c0:c1], bank[4 + 2 * i + t][:, 0:c1 - c0], ACT.Copy).then_inc(tm_ready, 1)
                act.wait_ge(tm_ready, 8 + 4 * l)
                f(g2sig, v2[:, :, 768:792], ACT.Exp, scale=-1.0).then_inc(gate_exp, 1)
                act.wait_ge(fx_neg, l + 1)
                f(ftmp[:, 16:24], ftmp[:, 8:16], ACT.Exp).then_inc(fx_exp, 1)
                act.wait_ge(fx_exp, l + 1)
                f(ftmp[:, 24:32], ftmp[:, 16:24], ACT.Ln, bias=1.0).then_inc(fx_ln, 1)
                act.wait_ge(cs_sub, l + 1)
                f(csm, csm, ACT.Exp, scale=SCALE).then_inc(cs_exp, 1)
                act.wait_ge(cst_full, l + 1)
                f(cpt, bank[0][:, 0:S], ACT.Copy).then_inc(cpt_ready, 1)
                for i in range(NU + 4):
                    if i < NU:
                        act.wait_ge(s_max, U + i + 1)
                        c = 2 * (i % 4)
                        for q, (a, b) in enumerate(((0, P), (P, 384))):
                            last = f(pb[:, i % 4, a:b], pb[:, i % 4, a:b], ACT.Exp, bias=nb[:, c + q:c + q + 1], scale=SCALE,
                                     accum_out=rs[:, c + q:c + q + 1])
                        last.then_inc(p_raw, 1)
                    for pair, u in LAST_OF_PAIR.items():
                        if u + 4 == i:
                            act.wait_ge(pv_full, U + u + 1)
                            f(o2[:, pair * S:(pair + 1) * S], bank[O_BANK[pair % 2]][:, 0:S], ACT.Copy).then_inc(o_ready, 1)

            act.wait_ge(s_params, 16)
            f(silu_c[:], PR("c"), ACT.Silu).then_inc(c_ready, 1)
            act.wait_ge(ang_ready, 1)
            f(sin2[:], sin2[:], ACT.Sin)
            f(cos2[:], cos2[:], ACT.Sin).then_inc(trig_ready, 1)
            act.wait_ge(mod_ready, 1)
            norm(0, 0)
            act.wait_ge(raw_zero, 1)
            channel_major(T1, 0, 0)
            for i in range(4):
                act.wait_ge(tm_full, i + 1)
                a, b = ((0, 512), (512, 768))[i // 2]
                f(v1[:, i % 2, a:b], bank[i][:, 0:b - a], ACT.Copy).then_inc(tm_ready, 1)
            attention1()
            rwkv()
            channel_major(TG, CM_G, 0)
            rms_of_output(0, out_full, 2)
            norm(1, 1)
            ffn(0)
            rms_of_output(1, down_done, FC)
            with act.Fori(0, LAYERS) as l:
                norm(2 + 3 * l, 0)
                ffn(1 + 2 * l)
                norm(3 + 3 * l, 1)
                mixer2(l)
                norm(4 + 3 * l, 2)
                ffn(2 + 2 * l)
            norm(8, 0, rows=False)

        @block.vector
        def _(dve):
            v = Steps(dve, dve_step)
            tt, ts, stt = dve.tensor_tensor, dve.tensor_scalar, dve.scalar_tensor_tensor
            mod3 = mod[:].rearrange("p (s j k) -> p s j k", s=3, j=3)

            def angles():
                turn_hi = 6.28125
                turn_lo = 2 * math.pi - turn_hi
                magic = 1.5 * 2.0 ** 23
                dve.wait_ge(s_pos, 16)
                dve.wait_ge(s_const, 16)
                posf, ang, m = hT[:, 0], hT[:, 1], hT[:, 2]
                v(dve.tensor_copy(posf, pos_i))
                v.settle()
                v(ts(ang, posf, K("inv_freq2"), None, ALU.mult))
                v.settle()
                for dst, quarter in ((sin2, 0.0), (cos2, 0.25)):
                    v(ts(m, ang, 1 / (2 * math.pi), quarter, ALU.mult, ALU.add))
                    v.settle()
                    v(ts(m, m, magic, None, ALU.add))
                    v.settle()
                    v(ts(m, m, magic, None, ALU.subtract))
                    v.settle()
                    v(stt(posf, m, -turn_hi, ang, ALU.mult, ALU.add))
                    v.settle()
                    v(stt(posf, m, -turn_lo, posf, ALU.mult, ALU.add))
                    v.settle()
                    v(ts(posf, posf, quarter * 2 * math.pi, None, ALU.add))
                    v.settle()
                    last = ts(dst[:], posf, math.pi, -math.pi, ALU.min, ALU.max)
                    v(last)
                    v.settle()
                dve.nop().then_inc(ang_ready, 1)

            def norm(n, sub, rows=True):
                dve.wait_ge(ss_ready, 2 * n + 2)
                ts(stat[:, 2:4], stat[:, 0:2], 1.0 / D, EPS, ALU.mult, ALU.add).then_inc(ms_ready, 1)
                dve.wait_ge(sd_ready, n + 1)
                v(dve.reciprocal(stat[:, 6:8], stat[:, 4:6]))
                v.settle()
                for t in range(NT):
                    ts(xn[:, t], x[:, t], stat[:, 6 + t:7 + t], None, ALU.mult).then_inc(xn_ready, 1)
                if not rows:
                    return
                for b in range(2, 4):
                    dve.wait_ge(ht_full, 4 * n + b + 1)
                    for k in (2 * b, 2 * b + 1):
                        last = ts(hT[:, k], bank[4 + b][:, (k % 2) * S:(k % 2 + 1) * S], mod_scale[:, sub, k:k + 1],
                                  mod[:, 24 * sub + k:24 * sub + k + 1], ALU.mult, ALU.add)
                last.then_inc(ht_dve, 1)

            def finish(n, source, value, rms):
                dve.wait_ge(source, value)
                dve.wait_ge(row_ready, n + 1)
                if rms:
                    dve.wait_ge(fss_ready, 4 * n + 4)
                    s4 = stat[:, 8:12].rearrange("p (t h) -> p t h", t=2)
                    v(tt(stat[:, 12:14], s4[:, :, 0], s4[:, :, 1], ALU.add))
                    v.settle()
                    ts(stat[:, 12:14], stat[:, 12:14], 1.0 / D, EPS, ALU.mult, ALU.add).then_inc(fms_ready, 1)
                    dve.wait_ge(fsd_ready, n + 1)
                    v(dve.reciprocal(stat[:, 16:18], stat[:, 14:16]))
                    v.settle()
                for j in range(4):
                    wait(dve, x_ready, 4 * n + j - 1)
                    r = row[:, (j % 2) * 512:(j % 2 + 1) * 512]
                    if rms:
                        last = stt(fin[:, j % 2], bank[j], stat[:, 16 + j // 2:17 + j // 2], r, ALU.mult, ALU.mult)
                    else:
                        last = tt(fin[:, j % 2], bank[j], r, ALU.mult)
                    last.then_inc(fin_read, 1)

            def channel_major(table, base, qbase, rbase):
                for j, (kind, q, r, dest) in enumerate(table):
                    if kind == "shift":
                        dve.wait_ge(cm_pre, q + 1)
                        stt(dest, pre[:, q % 3], PR("mu", j, j + 1), raw[:, q % 3, 1:S + 1], ALU.mult, ALU.add).then_inc(cm_out, 1)
                    elif r is not None:
                        sin = K("sin1") if kind == "rope1" else sin2[:]
                        dve.wait_ge(trig_ready, 1)
                        dve.wait_ge(rope_full, rbase + r + 1)
                        tt(rot[:, r % 2], bank[6 + r % 2][:, 0:S], sin, ALU.mult).then_inc(rope_used, 1)
                        dve.wait_ge(rope_used, rbase + r + 1)
                        dve.wait_ge(cm_pre, qbase + q + 1)
                        tt(dest, rot[:, r % 2], pre[:, q % 3], ALU.add).then_inc(cm_out, 1)

            def ffn(fn):
                def one(c, i=0):
                    dve.wait_ge(silu_ready, FC * fn + c + i + 1)
                    wait(dve, down_done, FC * fn + c + i - 1 if c >= 2 else FC * fn)
                    tt(act_t[:, c % 2].rearrange("p k n -> p (k n)"), silu[:, c % 2], bank[5 + 2 * (c % 2)], ALU.mult).then_inc(act_ready, 1)
                one(0)
                one(1)
                with dve.Fori(0, FC - 3, 2) as i:
                    one(2, i)
                    one(3, i)
                one(FC - 1)

            def masked_max(dst, scores, mask, out):
                return dve.tensor_tensor_reduce(out=dst, in0=scores, in1=mask, scale=1.0, scalar=-3e38, op0=ALU.add, op1=ALU.max, accum_out=out)

            def attention1():
                def maxima(i):
                    dve.wait_ge(s1_full, i + 1)
                    wait(dve, s1_t, 3 * (i - 1))
                    c = 8 * (i % 2)
                    for g in range(3):
                        for q, (a, b) in enumerate(((0, P), (P, 384))):
                            v(masked_max(p1[:, i % 2, g, a:b], bank[4 + g][:, a:b], K("dilated", 384 * g + a, 384 * g + b),
                                         mx[:, c + 3 * q + g:c + 3 * q + g + 1]))
                    v.settle()
                    v(dve.tensor_reduce(mx[:, c + 6:c + 8], mx[:, c:c + 6].rearrange("p (q g) -> p q g", q=2), AX.X, ALU.max))
                    v.settle()
                    ts(nb[:, 2 * (i % 2):2 * (i % 2) + 2], mx[:, c + 6:c + 8], -SCALE, None, ALU.mult).then_inc(s1_max, 1)
                maxima(0)
                for i in range(4):
                    if i < 3:
                        maxima(i + 1)
                    dve.wait_ge(s1_exp, i + 1)
                    c = 2 * (i % 2)
                    dve.reciprocal(ri[:, c:c + 2], rs[:, c:c + 2]).then_inc(s1_scale, 1)
                    wait(dve, s1_pv, i)
                    for g in range(3):
                        dve.wait_ge(s1_t, 3 * i + g + 1)
                        dve.tensor_copy(pt1[:, g], bank[(7, 2, 1)[g]][:, 0:384]).then_inc(s1_tr, 1)

            def rwkv():
                col = lambda a, w: a[:, w * S:(w + 1) * S]
                by_chunk = lambda a: a.rearrange("p (c n) -> p c n", c=4)
                for w in range(PAIRS):
                    last = ts(col(kk, w), col(k_t, w), PR("k_k", w, w + 1), None, ALU.mult)
                last.then_inc(kk0_ready, 1)
                dve.wait_ge(kn_full, 1)
                ts(norm_kk, psum[:, 0:3].rearrange("p b n -> p (b n)"), 1e-24, None, ALU.max).then_inc(kn_clamped, 1)
                dve.wait_ge(kn_sqrt, 1)
                dve.reciprocal(norm_kk, norm_kk).then_inc(kn_rec, 1)
                dve.wait_ge(lr_ready, PAIRS)
                for ps in range(PAIRS // 2):
                    for lp in range(2):
                        w = 2 * ps + lp
                        for c in range(4):
                            last = dve.tensor_tensor_scan(cs[:, lp, c * C:(c + 1) * C], K("ones", 0, C), sgw[:, w * S + c * C:w * S + (c + 1) * C],
                                                          0.0, ALU.mult, ALU.add)
                        last.then_inc(cs_ready, 1)
                    for lp in range(2):
                        w = 2 * ps + lp
                        v(ts(kbuf[:, lp], col(iclr, w), PR("k_a", w, w + 1), PR("k_a", w, w + 1), ALU.mult, ALU.subtract))
                        v.settle()
                        v(stt(kbuf[:, lp], kbuf[:, lp], 1.0, col(k_t, w), ALU.add, ALU.mult))
                        dve.wait_ge(e_ready, w + 1)
                        p_at = decay[:, lp, :, 1:C + 1]
                        v(tt(kr[:, lp, :, 1].rearrange("p h (c n) -> p h c n", c=2), col(r_t, w).rearrange("p (h c n) -> p h c n", h=2, c=2),
                             p_at.rearrange("p (h c) n -> p h c n", h=2), ALU.mult))
                        v.settle()
                        v(tt(kt[:, lp], kbuf[:, lp], decay_inv[:, lp], ALU.mult))
                        v(stt(cs[:, lp], col(r_t, w), PR("r_k", w, w + 1), kbuf[:, lp], ALU.mult, ALU.mult))
                        v.settle()
                        tt(by_chunk(kbuf[:, lp]), by_chunk(kt[:, lp]), decay[:, lp, :, C:C + 1].broadcast_to([P, 4, C]), ALU.mult).then_inc(dve_prep, 1)
                        dve.wait_ge(bon_full, w + 1)
                        tt(col(r_t, w), bank[3][:, 0:S], col(v_t, w), ALU.mult).then_inc(bon_ready, 1)
                        for h in range(2):
                            n = 2 * w + h
                            dve.wait_ge(tr_full, n + 1)
                            m2 = 2 * lp + h
                            v(dve.tensor_copy(vkb[:, m2].rearrange("p k n -> p (k n)"), bank[2 - h][:, 0:384]))
                            dve.tensor_copy(avk[:, 2 * m2:2 * m2 + 2, HD:P], bank[2 - h][:, 384:512].rearrange("p (e n) -> p e n", e=2)).then_inc(tr_ready, 1)
                            dve.wait_ge(sc_full, n + 1)
                            for e in range(2):
                                m = 2 * m2 + e
                                v(tt(scores[:, m].rearrange("p k n -> p (k n)"), bank[4 + e], K("score_mask"), ALU.mult))
                                v(tt(inv_x[:, m], bank[6 + e][:, 0:P], K("level1"), ALU.mult))
                            v.settle()
                            tt(inv_x[:, 2 * m2:2 * m2 + 2], inv_x[:, 2 * m2:2 * m2 + 2], ident.unsqueeze(1).broadcast_to([P, 2, P]), ALU.add).then_inc(sc_ready, 1)
                    for j in range(len(LEVELS)):
                        for lp in range(2):
                            q = (ps * len(LEVELS) + j) * 2 + lp
                            dve.wait_ge(p_full, q + 1)
                            flat = lambda a: a[:, 4 * lp:4 * lp + 4].rearrange("p m n -> p (m n)")
                            if j == 0:
                                dve.wait_ge(y0_ready, 2 * (2 * ps + lp) + 2)
                            if j < len(LEVELS) - 1:
                                v(tt(flat(inv_x), flat(inv_x), bank[2 + lp], ALU.subtract))
                            tt(flat(inv_y), flat(inv_y), bank[4 + lp], ALU.subtract).then_inc(xy_ready, 1)
                    dve.wait_ge(hg_full, ps + 1)
                    gt = kr[:, :, :, 1].rearrange("p w h n -> p (w h) n")
                    tt(gt, bank[3].rearrange("p (w n) -> p w n", w=4), gt, ALU.add).then_inc(g_ready, 1)
                    dve.wait_ge(zt_full, ps + 1)
                    dve.wait_ge(bd_zero, 1)
                    for lp in range(2):
                        o = lp * S
                        v(dve.tensor_copy(z_s[:, lp, 0], bank[7][:, o:o + HD]))
                        v(dve.tensor_copy(z_s[:, lp, 1], bank[6][:, o + 64:o + 128]))
                        for e in range(2):
                            h, hc = half(e), slice(e * HD, (e + 1) * HD)
                            v(dve.tensor_copy(state[h, lp, 0, hc], bank[6][h, o:o + HD]))
                            for step, src in ((0, bank[7][h, o + 64:o + 128]), (1, bank[6][h, o + 128:o + 192])):
                                last = stt(trans[h, lp, step, hc], K("ident_stack")[h], decay[h, lp, step + 1, C:C + 1], src, ALU.mult, ALU.add)
                                if not (lp == 1 and e == 1 and step == 1):
                                    v(last)
                    last.then_inc(zt_ready, 1)
                    for step in range(2):
                        dve.wait_ge(m_full, 2 * ps + step + 1)
                        for lp in range(2):
                            for e in range(2):
                                h, hc = half(e), slice(e * HD, (e + 1) * HD)
                                last = tt(state[h, lp, step + 1, hc], bank[step][h, lp * P + e * HD:lp * P + (e + 1) * HD], z_s[h, lp, step], ALU.add)
                        last.then_inc(m_ready, 1)
                    dve.wait_ge(yc_full, ps + 1)
                    dve.wait_ge(h_ready, ps + 1)
                    y3 = ymix[:, ps * 512:(ps + 1) * 512].rearrange("p (w n) -> p w n", w=2)[:, :, C:S]
                    tt(y3, bank[4].rearrange("p (w n) -> p w n", w=2)[:, :, C:S], y3, ALU.add).then_inc(pass_done, 1)
                dve.wait_ge(gn_mu, 1)
                stt(dev, psum[:, 0:3].rearrange("p b n -> p (b n)"), -1.0 / HD, ymix, ALU.mult, ALU.add).then_inc(gn_dev, 1)
                dve.wait_ge(gn_var, 1)
                ts(sq, psum[:, 5:8].rearrange("p b n -> p (b n)"), 1.0 / HD, GN_EPS, ALU.mult, ALU.add).then_inc(gn_ms, 1)
                dve.wait_ge(gn_sd, 1)
                dve.reciprocal(sq, sq).then_inc(gn_rs, 1)
                dve.wait_ge(gn_n, 1)
                for w in range(PAIRS):
                    v(ts(col(dev, w), col(dev, w), PR("lnx_w", w, w + 1), PR("lnx_b", w, w + 1), ALU.mult, ALU.add))
                    v.settle()
                    v(tt(col(dev, w), col(dev, w), col(r_t, w), ALU.add))
                    v.settle()
                    tt(col(ymix, w), col(dev, w), col(gate1, w), ALU.mult).then_inc(gn_ready, 1)

            def merge():
                dve.wait_ge(cm_evac, CM_G + 16)
                for n in range(16):
                    dve.wait_ge(ym_full, n + 1)
                    if n < 8:
                        tt(merged[:, n * S:(n + 1) * S], bank[4 + n % 2][:, 0:S], sig[:, (8 + n) * S:(9 + n) * S], ALU.mult).then_inc(ym_read, 1)
                    else:
                        j = n - 8
                        wait(dve, ym_ready, j - 1)
                        tt(ytmp[:, n % 2], bank[4 + n % 2][:, 0:S], sig[:, j * S:(j + 1) * S], ALU.mult).then_inc(ym_read, 1)

            def mod_columns(chunks, used):
                with dve.Fori(0, chunks // 2) as i:
                    for s in range(2):
                        dve.wait_ge(ada_used, used + s + 1 + 2 * i)
                        diag = silu[:, s].rearrange("p (n m) -> p n m", n=4)
                        tt(diag, bank[6 + s].rearrange("p (n m) -> p n m", n=4), ident.unsqueeze(1).broadcast_to([P, 4, P]), ALU.mult).then_inc(mod_part, 1)
                        dve.wait_ge(mod_part, used + s + 1 + 2 * i)
                        dve.tensor_reduce(mod_raw[:, bass.ds(8 * i + 4 * s, 4)], diag, AX.X, ALU.add).then_inc(mod_col, 1)

            def mod_layer(l):
                mod_columns(ADA2_CHUNKS, ADA1_CHUNKS + ADA2_CHUNKS * l)
                dve.wait_ge(mod_col, ADA1_CHUNKS + ADA2_CHUNKS * (l + 1))
                dve.wait_ge(s_layers, 16 * (l + 1))
                v(tt(mod[:], mod_raw[:], NOW("b_ada"), ALU.add))
                v.settle()
                v(stt(mod_scale[:], mod3[:, :, 1], 1.0, NOW("norm_g").rearrange("p (s k) -> p s k", s=3), ALU.add, ALU.mult))
                v(ts(mod_gate[:, 0:3:2], mod3[:, 0:3:2, 2], 0.5, None, ALU.mult))
                dve.tensor_copy(mod_gate[:, 1], mod3[:, 1, 2]).then_inc(mod_ready, 1)

            def mixer2(l):
                base, qbase, rbase, U = CM_2 + 16 * l, Q1 + Q2 * l, R1 + R2 * l, NU * l
                channel_major(T2, base, qbase, rbase)
                dve.wait_ge(swap_full, l + 1)
                dve.wait_ge(cm_evac, base + 16)
                dve.wait_ge(pool_zb, 1)
                for i in range(2):
                    for par in range(2):
                        h = half(par)
                        for g in range(2):
                            z = cm2[h, i * S:(i + 1) * S] if g == par else bank[i][h, 0:S]
                            pos = NOW("cmp_pos", 16 * i, 16 * i + 16)[h]
                            for jh in range(2):
                                zz = z.rearrange("p (r j q) -> p j r q", j=8, q=2)[:, :, jh:jh + 15, par]
                                last = tt(zb[h, i, 8 * jh:8 * jh + 8, g, 0:15], zz, pos[:, 8 * jh:8 * jh + 8].unsqueeze(2).broadcast_to([HD, 8, 15]), ALU.add)
                                if not (i == 1 and par == 1 and g == 1 and jh == 1):
                                    v(last)
                last.then_inc(zb_ready, 1)
                dve.wait_ge(gelu_ready, l + 1)
                for h in range(2):
                    last = dve.tensor_copy(ghrep[:, h].rearrange("p (g r c) -> p g r c", g=2, r=4),
                                           gh[:, 1, h].rearrange("p (g c) -> p g c", g=2).unsqueeze(2).broadcast_to([P, 2, 4, 16]))
                    if h == 0:
                        v(last)
                last.then_inc(ghrep_ready, 1)
                dve.wait_ge(tm_ready, 8 + 4 * l)
                xf = ftmp[:, 0:8].rearrange("p (t n) -> p t n", t=2)
                v(tt(xf, v2[:, :, 792:796], NOW("fox_bias").unsqueeze(1).broadcast_to([P, 2, 4]), ALU.add))
                v.settle()
                v(ts(ftmp[:, 32:40], ftmp[:, 0:8], -1.0, None, ALU.mult))
                v.settle()
                tt(ftmp[:, 8:16], ftmp[:, 0:8], ftmp[:, 32:40], ALU.min).then_inc(fx_neg, 1)
                v(ts(ftmp[:, 40:48], ftmp[:, 0:8], 0.0, 1 / SCALE, ALU.min, ALU.mult))
                dve.wait_ge(gate_exp, l + 1)
                v(ts(g2sig, g2sig, 1.0, None, ALU.add))
                v.settle()
                v(dve.reciprocal(g2sig, g2sig))
                dve.wait_ge(fx_ln, l + 1)
                dve.wait_ge(pool_zb, 1)
                for rep in range(2):
                    last = stt(lf8[:, :, 64 * rep:64 * rep + 4], ftmp[:, 24:32].rearrange("p (t n) -> p t n", t=2), -1 / SCALE,
                               ftmp[:, 40:48].rearrange("p (t n) -> p t n", t=2), ALU.mult, ALU.add)
                    if rep == 0:
                        v(last)
                last.then_inc(lf_ready, 1)
                dve.wait_ge(cmp2_full, l + 1)
                v(dve.tensor_copy(kcmp, bank[3][:, 0:16]))
                tt(vblk, bank[3][:, 64:128].unsqueeze(1).broadcast_to([P, 8, HD]), K("cmp_block").unsqueeze(2).broadcast_to([P, 8, HD]),
                   ALU.mult).then_inc(cmp_ready, 1)
                dve.wait_ge(f_full, l + 1)
                v(dve.tensor_copy(f_pos, bank[2][:, 0:S]))
                ts(f_neg, bank[2][:, 0:S], -1.0, None, ALU.mult).then_inc(f_ready, 1)
                dve.wait_ge(cs_full, l + 1)
                csm4 = csm.rearrange("p (t h c) -> p t h c", t=2, h=8)
                for e in range(2):
                    v(tt(csm4[:, :, 4 * e:4 * e + 4], bank[e][:, 0:128].rearrange("p (t h c) -> p t h c", t=2, h=4),
                         K("cmp_add").rearrange("p (t c) -> p t c", t=2).unsqueeze(2).broadcast_to([P, 2, 4, 16]), ALU.add))
                v.settle()
                csm3 = csm.rearrange("p (h c) -> p h c", c=16)
                v(dve.tensor_reduce(cst[:, 0:16], csm3, AX.X, ALU.max))
                v.settle()
                tt(csm3, csm3, cst[:, 0:16].unsqueeze(2).broadcast_to([P, 16, 16]), ALU.subtract).then_inc(cs_sub, 1)
                dve.wait_ge(cs_exp, l + 1)
                v(tt(csm4, csm4, K("cmp_keep").rearrange("p (t c) -> p t c", t=2).unsqueeze(2).broadcast_to([P, 2, 8, 16]), ALU.mult))
                v.settle()
                v(dve.tensor_reduce(cst[:, 16:32], csm3, AX.X, ALU.add))
                v.settle()
                v(ts(cst[:, 16:32], cst[:, 16:32], 1e-30, None, ALU.max))
                v.settle()
                v(dve.reciprocal(cst[:, 32:48], cst[:, 16:32]))
                v.settle()
                v(tt(cst[:, 48:64].rearrange("p (t h) -> p t h", t=2), cst[:, 32:48].rearrange("p (t h) -> p t h", t=2), g2sig[:, :, 0:24:3], ALU.mult))
                v.settle()
                tt(csm3, csm3, cst[:, 48:64].unsqueeze(2).broadcast_to([P, 16, 16]), ALU.mult).then_inc(cs_prob, 1)

                for i in range(NU + 2):
                    if i < NU:
                        dve.wait_ge(s_full, U + i + 1)
                        wait(dve, t_full, behind(U, i - 3))
                        dve.memset(mx[:, 16:17], 0.0)
                        c = 2 * (i % 4)
                        b = bank[S_BANK[i % 3]]
                        v(masked_max(pb[:, i % 4, 0:P], b[:, 0:P], K("causal", P, S), mx[:, c:c + 1]))
                        v(masked_max(pb[:, i % 4, P:384], b[:, P:384], K("causal"), mx[:, c + 1:c + 2]))
                        v.settle()
                        ts(nb[:, c:c + 2], mx[:, c:c + 2], -SCALE, None, ALU.mult).then_inc(s_max, 1)
                    if 1 <= i < NU + 1:
                        u = i - 1
                        c = 2 * (u % 4)
                        gate = UNITS[u][5]
                        dve.wait_ge(p_raw, U + u + 1)
                        if gate is None:
                            dve.reciprocal(ri[:, c:c + 2], rs[:, c:c + 2]).then_inc(r_scale, 1)
                        else:
                            v(dve.reciprocal(ri[:, 8 + c:10 + c], rs[:, c:c + 2]))
                            v.settle()
                            tt(ri[:, c:c + 2], ri[:, 8 + c:10 + c], g2sig[:, :, gate], ALU.mult).then_inc(r_scale, 1)
                    if i >= 2:
                        u = i - 2
                        dve.wait_ge(t_full, U + u + 1)
                        wait(dve, pv_full, behind(U, u - 1))
                        dve.tensor_copy(pt[:, u % 2], bank[T_BANK[u % 2]][:, 0:384]).then_inc(t_ready, 1)

            angles()
            dve.wait_ge(s_const, 16)
            mod_columns(ADA1_CHUNKS, 0)
            dve.wait_ge(mod_col, ADA1_CHUNKS)
            dve.wait_ge(s_params, 16)
            v(tt(mod[:, 0:48], mod_raw[:, 0:48], PR("b_ada1"), ALU.add))
            v.settle()
            v(stt(mod_scale[:, 0:2], mod3[:, 0:2, 1], 1.0, PR("g_norm").rearrange("p (s k) -> p s k", s=2), ALU.add, ALU.mult))
            tt(mod_gate[:, 0:2], mod3[:, 0:2, 2], PR("g_post").rearrange("p (s k) -> p s k", s=2), ALU.mult).then_inc(mod_ready, 1)
            norm(0, 0)
            channel_major(T1, 0, 0, 0)
            attention1()
            rwkv()
            merge()
            finish(0, out_full, 2, True)
            norm(1, 1)
            ffn(0)
            finish(1, down_done, FC, True)
            with dve.Fori(0, LAYERS) as l:
                v.enter(l, DVE_STEPS_PER_LAYER)
                mod_layer(l)
                norm(2 + 3 * l, 0)
                ffn(1 + 2 * l)
                finish(2 + 3 * l, down_done, FC * (2 + 2 * l), False)
                norm(3 + 3 * l, 1)
                mixer2(l)
                finish(3 + 3 * l, out_full, 4 + 2 * l, False)
                norm(4 + 3 * l, 2)
                ffn(2 + 2 * l)
                finish(4 + 3 * l, down_done, FC * (3 + 2 * l), False)
                v.leave(LAYERS)
            norm(8, 0, rows=False)
            dve.wait_ge(row_ready, 9)
            dve.wait_ge(xn_ready, 18)
            for t in range(NT):
                tt(xn[:, t], xn[:, t], row[:], ALU.mult).then_inc(y_ready, 1)

        @block.gpsimd
        def _(pool):
            g = Steps(pool, pool_step)
            tt, ts = pool.tensor_tensor, pool.tensor_scalar

            def channel_major(table, base, qbase):
                for j, (kind, q, _, _) in enumerate(table):
                    if q is None:
                        continue
                    pool.wait_ge(cm_evac, base + j + 1)
                    wait(pool, cm_out, since(qbase, q - 2))
                    if kind == "shift":
                        tt(pre[:, q % 3], raw[:, q % 3, 0:S], raw[:, q % 3, 1:S + 1], ALU.subtract).then_inc(cm_pre, 1)
                    else:
                        pool.wait_ge(trig_ready, 1)
                        cos = K("cos1") if kind == "rope1" else cos2[:]
                        tt(pre[:, q % 3], raw[:, q % 3, 1:S + 1], cos, ALU.mult).then_inc(cm_pre, 1)

            def add(n):
                for j in range(4):
                    pool.wait_ge(fin_read, 4 * n + j + 1)
                    dst = x[:, j // 2, (j % 2) * 512:(j % 2 + 1) * 512]
                    tt(dst, dst, fin[:, j % 2], ALU.add).then_inc(x_ready, 1)

            def attention1():
                for i in range(4):
                    pool.wait_ge(s1_scale, i + 1)
                    c = 2 * (i % 2)
                    for q, (a, b) in enumerate(((0, P), (P, 384))):
                        last = ts(p1[:, i % 2, :, a:b], p1[:, i % 2, :, a:b], ri[:, c + q:c + q + 1], None, ALU.mult)
                    last.then_inc(s1_prob, 1)

            def rwkv():
                col = lambda a, w: a[:, w * S:(w + 1) * S]
                by_chunk = lambda a: a.rearrange("p (c n) -> p c n", c=4)
                pool.wait_ge(cm_out, Q1)
                g(pool.memset(pre[:], 0.0))
                g(pool.memset(rot[:], 0.0))
                pool.memset(decay[:, :, :, 0:1], 1.0).then_inc(bd_zero, 1)
                pool.wait_ge(kk0_ready, 1)
                tt(norm_kk, kk, kk, ALU.mult).then_inc(sq_ready, 1)
                pool.wait_ge(kn_rec, 1)
                tt(kk, kk, norm_kk, ALU.mult).then_inc(kk_ready, 1)
                pool.wait_ge(kk_ready, 1)
                pool.wait_ge(lr_ready, PAIRS)
                for ps in range(PAIRS // 2):
                    wait(pool, pass_done, ps)
                    for lp in range(2):
                        w = 2 * ps + lp
                        g(tt(bbuf[:, lp], col(kk, w), col(iclr, w), ALU.mult))
                        pool.wait_ge(e_ready, w + 1)
                        g(tt(kr[:, lp, :, 0].rearrange("p h (c n) -> p h c n", c=2), col(kk, w).rearrange("p (h c n) -> p h c n", h=2, c=2),
                             decay[:, lp, :, 0:C].rearrange("p (h c) n -> p h c n", h=2), ALU.mult))
                        g.settle()
                        g(tt(bt[:, lp], bbuf[:, lp], decay_inv[:, lp], ALU.mult))
                        g.settle()
                        tt(by_chunk(bbuf[:, lp]), by_chunk(bt[:, lp]), decay[:, lp, :, C:C + 1].broadcast_to([P, 4, C]), ALU.mult).then_inc(pool_prep, 1)
                    for n in range(4):
                        pool.wait_ge(sc_ready, 4 * ps + n + 1)
                        pair = slice(2 * n, 2 * n + 2)
                        g(tt(inv_y[:, pair], scores[:, pair, 0], K("level1_t").unsqueeze(1).broadcast_to([P, 2, P]), ALU.mult))
                        g.settle()
                        tt(inv_y[:, pair], inv_y[:, pair], ident.unsqueeze(1).broadcast_to([P, 2, P]), ALU.add).then_inc(y0_ready, 1)
                    for j in range(len(LEVELS)):
                        for lp in range(2):
                            q = (ps * len(LEVELS) + j) * 2 + lp
                            wait(pool, w_full, q - 1)
                            four = slice(4 * lp, 4 * lp + 4)
                            tt(inv_n[:, four], scores[:, four, 0], K("levels_t", j * P, (j + 1) * P).unsqueeze(1).broadcast_to([P, 4, P]),
                               ALU.mult).then_inc(nl_ready, 1)
                pool.wait_ge(gn_dev, 1)
                tt(sq, dev, dev, ALU.mult).then_inc(gn_sq, 1)
                pool.wait_ge(gn_rs, 1)
                tt(dev, dev, sq, ALU.mult).then_inc(gn_n, 1)

            pool.memset(raw[:], 0.0).then_inc(raw_zero, 1)
            pool.wait_ge(raw_zero, 1)
            pool.wait_ge(s_const, 16)
            channel_major(T1, 0, 0)
            attention1()
            rwkv()
            for j in range(8):
                pool.wait_ge(ym_read, 9 + j)
                tt(merged[:, j * S:(j + 1) * S], merged[:, j * S:(j + 1) * S], ytmp[:, j % 2], ALU.add).then_inc(ym_ready, 1)
            add(0)
            add(1)
            g(pool.memset(zb, 0.0))
            pool.memset(lf8, 0.0).then_inc(pool_zb, 1)
            with pool.Fori(0, LAYERS) as l:
                add(2 + 3 * l)
                channel_major(T2, CM_2 + 16 * l, Q1 + Q2 * l)
                U = NU * l
                for u in range(NU):
                    pool.wait_ge(r_scale, U + u + 1)
                    c = 2 * (u % 4)
                    for q, (a, b) in enumerate(((0, P), (P, 384))):
                        last = tt(pb[:, u % 4, a:b], pb[:, u % 4, a:b], ri[:, c + q:c + q + 1].broadcast_to([P, b - a]), ALU.mult)
                    last.then_inc(p_ready, 1)
                add(3 + 3 * l)
                add(4 + 3 * l)


def program(nc, arrays):
    T = {n: nc.dram_tensor(f"in_{n}", a.shape, mybir.dt.from_np(a.dtype), kind="ExternalInput").ap() for n, a in arrays.items()}
    out = nc.dram_tensor("out_0", (P, NT, D), F32, kind="ExternalOutput").ap()
    build(nc, T, out)


def kernel(**inputs):
    import concourse.bacc as bacc
    from concourse.bass_utils import run_bass_kernel_spmd

    nc = bacc.Bacc("TRN2", target_bir_lowering=False, num_devices=1)
    arrays = {n: np.ascontiguousarray(a) for n, a in layout(inputs).items()}
    program(nc, arrays)
    r = run_bass_kernel_spmd(nc, [{f"in_{n}": a for n, a in arrays.items()}], core_ids=[0])
    return r.results[0]["out_0"].reshape(P, NT, D).transpose(1, 0, 2).reshape(1, NT * P, D)
```

```python
import math
from contextlib import ExitStack

import numpy as np

import concourse.bass as bass
from concourse import mybir

F32 = mybir.dt.float32
F32R = mybir.dt.float32r
I32 = mybir.dt.int32
ACT = mybir.ActivationFunctionType
ALU = mybir.AluOpType
AX = mybir.AxisListType

P = 128
D = 1024
S = 256
NT = S // P
KD = D // P
FF = 2816
FC = FF // 256
LAYERS = 2
HD = 64
SCALE = HD ** -0.5
RW = 768
PAIRS = RW // P
EPS = 1e-6
GN_EPS = 64e-5
DECAY = math.exp(-0.5)
NEG = -1e30
SLOT = 4096
SHIFT_TILES = 20
C = 64
LEVELS = (2, 4, 8, 16, 32)
DVE_STEPS_PER_LAYER = 105

CONST_WIDTHS = (
    ("ident", P), ("rope1", P), ("rope2", P), ("swap", P), ("blockones", P), ("ident_stack", HD),
    ("tri", P), ("ones", P), ("causal", S),
    ("cos1", S), ("sin1", S), ("inv_freq2", 1), ("cmp_add", 32), ("cmp_keep", 32), ("cmp_block", 8), ("fox_row", 4),
)
EARLY_WIDTHS = (("lora", 2 * RW), ("dilated", 3 * 384), ("score_mask", 512),
                ("level1", P), ("level1_t", P), ("levels_t", len(LEVELS) * P))
PARAM_WIDTHS = (
    ("b_ada1", 48), ("g_norm", 2 * KD), ("g_post", 2 * KD),
    ("final_g", KD), ("mu", SHIFT_TILES), ("w0", 6), ("a0", 6), ("k_k", 6),
    ("k_a", 6), ("r_k", 6), ("lnx_w", 6), ("lnx_b", 6),
)
LAYER_WIDTHS = (("b_ada", 72), ("norm_g", 3 * KD), ("fox_bias", 4), ("cmp_pos", 32), ("cmp_w2", 2 * 2 * HD))


def columns(widths):
    at, out = 0, {}
    for name, w in widths:
        out[name] = (at, w)
        at += w
    return out, at


CONST_AT, CONST_N = columns(CONST_WIDTHS)
EARLY_AT, EARLY_N = columns(EARLY_WIDTHS)
PARAM_AT, PARAM_N = columns(PARAM_WIDTHS)
LAYER_AT, LAYER_N = columns(LAYER_WIDTHS)

IN2_WIDTHS = (512, 512, 512, 512, 512, 284)
IN2_AT = tuple(8 * sum(IN2_WIDTHS[:i]) for i in range(len(IN2_WIDTHS)))


def constants():
    a, early = np.zeros((P, CONST_N), np.float32), np.zeros((P, EARLY_N - 2 * RW), np.float32)

    def put(name, value):
        at, w = CONST_AT[name] if name in CONST_AT else EARLY_AT[name]
        if name in EARLY_AT:
            early[:, at - 2 * RW:at - 2 * RW + w] = np.asarray(value, np.float32).reshape(P, w)
            return
        a[:, at:at + w] = np.asarray(value, np.float32).reshape(P, w)

    i = np.arange(P)
    row, col = i[:, None], i[None, :]
    put("ident", row == col)
    for name, half in (("rope1", 32), ("rope2", 8)):
        r = np.zeros((P, P))
        for m in range(P):
            d = m % HD
            if d < half:
                r[m + half, m] = -1
            elif d < 2 * half:
                r[m - half, m] = 1
        put(name, r)
    put("swap", row == (col + 64) % P)
    put("blockones", row // 64 == col // 64)
    put("ident_stack", (row % 64) == np.arange(64)[None, :])
    put("tri", row <= col)
    put("ones", np.ones((P, P)))
    q1 = P + i[:, None]
    k = np.arange(S)[None, :]
    put("causal", np.where(q1 >= k, 0, NEG))
    dil = []
    for dilation in (1, 4, 16):
        for q, keys in ((i[:, None], np.arange(P)[None, :]), (q1, k)):
            ok = (q >= keys) & (q - keys <= 128 * dilation) & ((q - keys) % dilation == 0)
            dil.append(np.where(ok, 0, NEG))
    put("dilated", np.concatenate(dil, 1))
    same = row // C == col // C
    strict, incl = same & (row < col), same & (row <= col)
    put("score_mask", np.concatenate([strict, incl, strict, incl], 1))

    def level(b):
        return (row // (2 * b) == col // (2 * b)) & (row % (2 * b) >= b) & (col % (2 * b) < b)

    put("level1", -1.0 * level(1))
    put("level1_t", -1.0 * level(1).T)
    put("levels_t", np.concatenate([level(b).T for b in LEVELS], 1))
    half = HD // 2
    inv = (10000.0 ** (-np.arange(half) / half)).astype(np.float32)
    ang = (np.arange(S, dtype=np.float32)[None, :] * inv[i % half][:, None]).astype(np.float32)
    put("cos1", np.cos(ang.astype(np.float64)))
    put("sin1", np.sin(ang.astype(np.float64)))
    inv2 = (500000.0 ** (-np.arange(0, 16, 2) / 16)).astype(np.float32)
    put("inv_freq2", np.where(i % HD < 16, inv2[i % 8], 0.0))
    cmp_ok = [(q >= 16 * np.arange(16)[None, :] + 31) & (np.arange(16)[None, :] < 15) for q in (i[:, None], q1)]
    put("cmp_add", np.concatenate([np.where(m, 0, NEG) for m in cmp_ok], 1))
    put("cmp_keep", np.concatenate(cmp_ok, 1))
    put("cmp_block", row // 16 == np.arange(8)[None, :])
    put("fox_row", row % 64 == np.arange(4)[None, :])
    return a, early


def cols(v):
    return np.asarray(v).reshape(-1, P).T


def k_tiles(w):
    kdim, n = w.shape
    return np.ascontiguousarray(np.asarray(w).reshape(kdim // P, P, n).transpose(1, 0, 2).reshape(P, -1))


def chunked(w, width=512):
    return np.stack([k_tiles(w[:, j:j + width]) for j in range(0, w.shape[1], width)])


def rows_chunked(w):
    k, n = w.shape
    return np.ascontiguousarray(w.T.reshape(n // 512, 4, P, k).transpose(0, 2, 1, 3).reshape(n // 512, P, 4 * k))


def layout(inp):
    g = {k: np.asarray(v) for k, v in inp.items()}
    params = np.concatenate([
        cols(g["b_ada"][0]),
        cols(g["g_pre_mix"][0]), cols(g["g_pre_ffn"][0]), cols(g["g_post_mix"][0]), cols(g["g_post_ffn"][0]),
        cols(g["final_g_2"]), cols(g["mu_shift"][0]), cols(g["w0"][0]),
        cols(g["a0"][0]), cols(g["k_k"][0]), cols(g["k_a"][0]), cols(g["r_k"][0].reshape(-1)),
        cols(g["lnx_w"][0]), cols(g["lnx_b"][0]),
    ], axis=1)
    assert params.shape == (P, PARAM_N)
    layers = np.stack([np.concatenate([
        cols(g["b_ada_2"][l]), cols(g["norm_g_2"][l].reshape(-1)), np.broadcast_to(g["fox_fbias_2"][l][None], (P, 4)),
        g["cmp_pos_2"][l].reshape(2, 16, 2, HD).transpose(2, 3, 0, 1).reshape(P, 32),
        k_tiles(g["cmp_w2_2"][l, 0]), k_tiles(g["cmp_w2_2"][l, 1])], 1) for l in (*range(LAYERS), LAYERS - 1)])
    const, early = constants()
    w_in = g["w_in"][0]
    at = np.cumsum([0, 2560, 768, 768, 768, 1024, 1024])
    shift, q, k, v, ga, gb = (w_in[:, at[n]:at[n + 1]] for n in range(6))
    first = np.concatenate([shift, q, k, v[:, :512]], 1)
    in2 = []
    for l in range(LAYERS):
        w = g["w_in_2"][l]
        nq = w[:, :512].reshape(D, 2, 4, HD).transpose(0, 2, 1, 3).reshape(D, 512)
        part = lambda a, b: w[:, a:b]
        chunks = [
            np.concatenate([part(512, 640), part(640, 768), part(768, 896), part(1024, 1152)], 1),
            nq,
            part(1304, 1816),
            part(2076, 2588),
            np.concatenate([part(896, 1024), part(1152, 1280), part(1816, 2072)], 1),
            np.concatenate([part(2588, 2844), part(1280, 1304), part(2072, 2076)], 1),
        ]
        in2.append(np.concatenate([k_tiles(c) for c in chunks], 1))
    w_out2 = g["w_out_2"].copy()
    w_out2[:, :512] = g["w_out_2"][:, :512].reshape(LAYERS, 2, 4, HD, D).transpose(0, 2, 1, 3, 4).reshape(LAYERS, 512, D)
    up = [g["w_ffn_in"][0]] + [g["ffn_w13_2"][l, f] for l in range(LAYERS) for f in range(2)]
    down = [g["w_ffn_out"][0]] + [g["ffn_w2_2"][l, f] for l in range(LAYERS) for f in range(2)]
    up = [w.reshape(D, 2, FC, 256).transpose(2, 0, 1, 3).reshape(FC, KD, P, 512).transpose(0, 2, 1, 3).reshape(FC, P, SLOT) for w in up]
    down = [w.reshape(FC, 2, P, D).transpose(0, 2, 1, 3).reshape(FC, P, 2 * D) for w in down]
    return {
        "const": const, "params": params, "layers": layers,
        "early": np.concatenate([np.concatenate([g["w2"][0], g["a2"][0]], 0), g["g2"][0], early], 1),
        "x": g["x"][0].reshape(NT, P, D).transpose(1, 0, 2).reshape(P, NT * D),
        "pos": g["positions_2"], "c": g["c"], "c_2": g["c_2"],
        "ada": np.concatenate([rows_chunked(g["w_ada"][0])] + [rows_chunked(g["w_ada_2"][l]) for l in range(LAYERS)]),
        "in1": chunked(first), "in1_v": k_tiles(v[:, 512:]), "gates1": chunked(np.concatenate([ga, gb], 1)),
        "w_a": chunked(g["w_a"][0]), "w_b": k_tiles(g["w_b"][0]), "w_out": chunked(g["w_out"][0]),
        "up": np.concatenate(up), "down": np.concatenate(down),
        "in2": np.stack(in2),
        "cmp1": np.stack([k_tiles(g["cmp_w1_2"][l, i]) for l in range(LAYERS) for i in range(2)]),
        "w_out2": np.concatenate([chunked(w_out2[l]) for l in range(LAYERS)]),
    }


ADA1_CHUNKS, ADA2_CHUNKS = 12, 18
FIRST = 4
G_MIX1 = FIRST
G_ADA = G_MIX1 + 10
G_GATES = G_ADA + ADA2_CHUNKS
G_FFN1 = G_GATES + 9
G_LAYER = G_FFN1 + FC
MIX2_CHUNKS = 10
PER_LAYER = 2 * FC + MIX2_CHUNKS
assert G_LAYER % 2 == 0 and PER_LAYER % 2 == 0


class Steps:

    def __init__(self, engine, sem):
        self.engine, self.sem, self.base, self.n = engine, sem, 0, 0

    def __call__(self, instruction):
        instruction.then_inc(self.sem, 1)
        self.n += 1

    def settle(self):
        self.engine.wait_ge(self.sem, self.base + self.n)

    def enter(self, turn, per_turn):
        self.outer, self.base, self.n, self.per = self.base + self.n, self.base + self.n + turn * per_turn, 0, per_turn

    def leave(self, turns):
        assert self.n == self.per, f"{self.sem}: {self.n} steps in a turn"
        self.base, self.n = self.outer + turns * self.per, 0


def wait(engine, sem, value):
    if isinstance(value, int) and value <= 0:
        return
    engine.wait_ge(sem, value)


def build(nc, T, out):
    with ExitStack() as ctx:
        def sb(name, shape, dt=F32):
            return ctx.enter_context(nc.sbuf_tensor(name, shape, dt))

        def sem(name):
            return ctx.enter_context(nc.semaphore(name))

        const = sb("const", [P, CONST_N])
        params = sb("params", [P, PARAM_N])
        x = sb("x_res", [P, NT, D])
        xn = sb("xn", [P, NT, D])
        hT = sb("hT", [P, KD, S])
        ring = sb("ring", [P, 2, SLOT])
        ring_down = sb("ring_down", [P, 2, 2 * D])
        scratch = sb("scratch", [P, 3072])
        act_t = scratch[:, 0:1024].rearrange("p (b k n) -> p b k n", b=2, k=2)
        silu = scratch[:, 1024:2048].rearrange("p (b n) -> p b n", b=2)
        fin = scratch[:, 2048:3072].rearrange("p (t n) -> p t n", t=2)
        row = sb("row", [P, D])
        mod = sb("mod", [P, 72])
        mod_raw = sb("mod_raw", [P, 3, 72])
        mod_scale = sb("mod_scale", [P, 3, KD])
        mod_gate = sb("mod_gate", [P, 3, KD])
        stat = sb("stat", [P, 48])
        cos2 = sb("cos2", [P, S])
        sin2 = sb("sin2", [P, S])
        raw = sb("raw", [P, 3, S + 2])
        pre = sb("pre", [P, 3, S])
        rot = sb("rot", [P, 2, S])
        now = sb("layer_now", [P, LAYER_N])
        mx, nb, rs, ri = (sb(n, [P, 24]) for n in ("mx", "neg_max", "row_sum", "row_scale"))
        ARENA = 24064
        with nc.sbuf_tensor("split", [P, 18432], F32R) as split:
            pass
        arena = sb("arena", [P, ARENA])
        h_hi, h_lo = (split[:, a:a + 2048].rearrange("p (k n) -> p k n", k=KD) for a in (0, 2048))
        up_hi, up_lo = (split[:, a:a + 4096].rearrange("p (h n) -> p h n", h=2) for a in (4096, 8192))
        dn_hi, dn_lo = (split[:, a:a + 2048] for a in (12288, 14336))
        act_hi, act_lo = (split[:, a:a + 1024].rearrange("p (b n) -> p b n", b=2) for a in (16384, 17408))
        psum = ctx.enter_context(nc.psum_tensor("psum", [P, 8, 512], F32))
        bank = [psum[:, b, :] for b in range(8)]

        early = ring_down[:].rearrange("p b n -> p (b n)")
        lora = early[:, 0:2 * RW]

        def K(name, a=0, b=None):
            if name in EARLY_AT:
                at, w = EARLY_AT[name]
                return early[:, at + a:at + (w if b is None else b)]
            at, w = CONST_AT[name]
            return const[:, at + a:at + (w if b is None else b)]

        def PR(name, a=0, b=None):
            at, w = PARAM_AT[name]
            return params[:, at + a:at + (w if b is None else b)]

        def NOW(name, a=0, b=None):
            at, w = LAYER_AT[name]
            return now[:, at + a:at + (w if b is None else b)]

        def places(start, *widths):
            out = []
            for w in widths:
                out.append(arena[:, start:start + w])
                start += w
            assert start <= ARENA, start
            return out

        shifted, sgw, iclr, gate1, o1 = places(0, 5120, 1536, 1536, 1536, 512)
        ymix = sgw
        r_t, k_t, v_t = shifted[:, 0:1536], shifted[:, 1536:3072], shifted[:, 3072:4608]
        Z2 = 10240
        qk1, v1, p1, pt1 = places(Z2, 3072, 1536, 2 * 1152, 1152)
        v1 = v1.rearrange("p (t n) -> p t n", t=NT)
        p1 = p1.rearrange("p (b g n) -> p b g n", b=2, g=3)
        pt1 = pt1.rearrange("p (g n) -> p g n", g=3)
        inv_x, inv_y, inv_w, inv_n, scores, avk, vkb, nw, kr, kt, bt = places(
            Z2, 1024, 1024, 1024, 1024, 4096, 1024, 1536, 1024, 1024, 512, 512)
        mats = lambda a: a.rearrange("p (m n) -> p m n", m=8)
        inv_x, inv_y, inv_w, inv_n, avk, nw = (mats(a) for a in (inv_x, inv_y, inv_w, inv_n, avk, nw))
        scores = scores.rearrange("p (m k n) -> p m k n", m=8, k=4)
        vkb = vkb.rearrange("p (m k n) -> p m k n", m=4, k=3)
        kr = kr.rearrange("p (w h k n) -> p w h k n", w=2, h=2, k=2)
        kt, bt = (a.rearrange("p (w n) -> p w n", w=2) for a in (kt, bt))
        norm_kk = arena[:, Z2 + 4608:Z2 + 6144]
        dev, sq = places(Z2 + 6656, 1536, 1536)
        sig, merged = arena[:, Z2:Z2 + 4096], arena[:, Z2 + 4096:Z2 + 6144]
        ytmp = arena[:, Z2 + 6144:Z2 + 6656].rearrange("p (b n) -> p b n", b=2)
        xn_flat = xn[:].rearrange("p t n -> p (t n)")
        kk = xn_flat[:, 0:1536]
        z_s = xn_flat[:, 1536:1792].rearrange("p (w c n) -> p w c n", w=2, c=2)
        cs = scratch[:, 0:512].rearrange("p (w n) -> p w n", w=2)
        decay = scratch[:, 512:512 + 520].rearrange("p (w c n) -> p w c n", w=2, c=4)
        decay_inv = scratch[:, 1032:1544].rearrange("p (w n) -> p w n", w=2)
        kbuf = scratch[:, 1544:2056].rearrange("p (w n) -> p w n", w=2)
        bbuf = scratch[:, 2056:2568].rearrange("p (w n) -> p w n", w=2)
        state = pre[:].rearrange("p a n -> p (a n)").rearrange("p (w c n) -> p w c n", w=2, c=3)
        trans = rot[:].rearrange("p a n -> p (a n)").rearrange("p (w c n) -> p w c n", w=2, c=2)
        ada_tile = arena[:, 18304:22400].rearrange("p (b n) -> p b n", b=4)
        c_row = arena[:, 22400:23424]
        ada_slot = arena[:, 0:4 * SLOT].rearrange("p (b n) -> p b n", b=4)
        c2_row, posf, ang, turns, pos_i = places(20000, D, S, S, S, S)
        pos_i = pos_i.bitcast(I32)
        (cm2, v2, gh, ghrep, kcmp, vblk, csm, cpt, f_pos, f_neg, pb, pt, o2, g2sig, ftmp, cst) = places(
            0, 4096, 1592, 128, 256, 16, 512, 256, 256, 256, 256, 1536, 768, 2048, 48, 48, 64)
        zb, lf8 = places(18432, 1024, 256)
        v2 = v2.rearrange("p (t n) -> p t n", t=NT)
        zb = zb.rearrange("p (i j g c) -> p i j g c", i=2, j=16, g=2)
        gh = gh.rearrange("p (i h n) -> p i h n", i=2, h=2)
        ghrep = ghrep.rearrange("p (h n) -> p h n", h=2)
        vblk = vblk.rearrange("p (h n) -> p h n", h=8)
        lf8 = lf8.rearrange("p (t n) -> p t n", t=2)
        pb = pb.rearrange("p (b n) -> p b n", b=4)
        pt = pt.rearrange("p (b n) -> p b n", b=2)
        g2sig = g2sig.rearrange("p (t n) -> p t n", t=2)
        ident = K("ident")

        s_params, s_const, s_x, s_pos, s_lora, s_layers, s_c, s_c2 = (sem(n + "_loaded") for n in ("params", "const", "x", "pos", "lora", "layers", "c", "c2"))
        slot_full = [sem("slot0_full"), sem("slot1_full")]
        down_full = [sem("down0_full"), sem("down1_full")]
        ada_used = sem("ada_used")
        apart_full = [sem(f"apart{b}_full") for b in range(4)]
        apart_used = sem("apart_used")
        sums_kept = sem("sums_kept")
        up_full = sem("up_full")
        down_done = sem("down_done")
        half_done = sem("half_done")
        h_low = sem("h_low")
        h_low_last = sem("h_low_last")
        up_high = sem("up_high")
        up_low = sem("up_low")
        dn_high = sem("dn_high")
        dn_low = sem("dn_low")
        act_high = sem("act_high")
        act_low = sem("act_low")
        cm_full = sem("cm_full")
        cm_evac = sem("cm_evac")
        cm_out = sem("cm_out")
        cm_pre = sem("cm_pre")
        rope_full = sem("rope_full")
        rope_used = sem("rope_used")
        tm_full = sem("tm_full")
        tm_ready = sem("tm_ready")
        c_ready = sem("c_ready")
        mod_ready = sem("mod_ready")
        ss_ready = sem("ss_ready")
        ms_ready = sem("ms_ready")
        sd_ready = sem("sd_ready")
        xn_ready = sem("xn_ready")
        ht_full = sem("ht_full")
        ht_act = sem("ht_act")
        ht_dve = sem("ht_dve")
        row_full = sem("row_full")
        row_ready = sem("row_ready")
        silu_ready = sem("silu_ready")
        act_ready = sem("act_ready")
        bank_full = sem("bank_full")
        fin_read = sem("fin_read")
        x_ready = sem("x_ready")
        fss_ready = sem("fss_ready")
        fms_ready = sem("fms_ready")
        fsd_ready = sem("fsd_ready")
        y_ready = sem("y_ready")
        s_out = sem("s_out")
        dve_step = sem("dve_step")
        pool_step = sem("pool_step")
        raw_zero = sem("raw_zero")
        ang_ready = sem("ang_ready")
        trig_ready = sem("trig_ready")
        ym_full = sem("ym_full")
        ym_read = sem("ym_read")
        ym_ready = sem("ym_ready")
        s1_full = sem("s1_full")
        s1_max = sem("s1_max")
        s1_exp = sem("s1_exp")
        s1_scale = sem("s1_scale")
        s1_prob = sem("s1_prob")
        s1_t = sem("s1_t")
        s1_tr = sem("s1_tr")
        s1_pv = sem("s1_pv")
        s1_o = sem("s1_o")
        lr_in = sem("lr_in")
        lr_full = sem("lr_full")
        lr_ready = sem("lr_ready")
        kk0_ready = sem("kk0_ready")
        sq_ready = sem("sq_ready")
        kn_full = sem("kn_full")
        kn_clamped = sem("kn_clamped")
        kn_sqrt = sem("kn_sqrt")
        kn_rec = sem("kn_rec")
        kk_ready = sem("kk_ready")
        bd_zero = sem("bd_zero")
        cs_ready = sem("cs_ready")
        e_ready = sem("e_ready")
        pool_prep = sem("pool_prep")
        dve_prep = sem("dve_prep")
        bon_full = sem("bon_full")
        bon_ready = sem("bon_ready")
        tr_full = sem("tr_full")
        tr_ready = sem("tr_ready")
        sc_full = sem("sc_full")
        sc_read = sem("sc_read")
        sc_ready = sem("sc_ready")
        y0_ready = sem("y0_ready")
        nl_ready = sem("nl_ready")
        w_full = sem("w_full")
        w_ready = sem("w_ready")
        p_full = sem("p_full")
        xy_ready = sem("xy_ready")
        av_full = sem("av_full")
        av_ready = sem("av_ready")
        nw_full = sem("nw_full")
        nw_ready = sem("nw_ready")
        hg_full = sem("hg_full")
        h_ready = sem("h_ready")
        g_ready = sem("g_ready")
        zt_full = sem("zt_full")
        zt_ready = sem("zt_ready")
        m_full = sem("m_full")
        m_ready = sem("m_ready")
        yc_full = sem("yc_full")
        pass_done = sem("pass_done")
        gn_mu = sem("gn_mu")
        gn_dev = sem("gn_dev")
        gn_sq = sem("gn_sq")
        gn_var = sem("gn_var")
        gn_ms = sem("gn_ms")
        gn_sd = sem("gn_sd")
        gn_rs = sem("gn_rs")
        gn_n = sem("gn_n")
        gn_ready = sem("gn_ready")
        swap_full = sem("swap_full")
        zeroed = sem("places_zeroed")
        zb_ready = sem("zb_ready")
        cmp_full = sem("cmp_full")
        gelu_ready = sem("gelu_ready")
        ghrep_ready = sem("ghrep_ready")
        cmp2_full = sem("cmp2_full")
        cmp_ready = sem("cmp_ready")
        gate_exp = sem("gate_exp")
        fx_neg = sem("fx_neg")
        fx_exp = sem("fx_exp")
        fx_ln = sem("fx_ln")
        lf_ready = sem("lf_ready")
        f_full = sem("f_full")
        f_ready = sem("f_ready")
        cs_full = sem("cs_full")
        cs_sub = sem("cs_sub")
        cs_exp = sem("cs_exp")
        cs_prob = sem("cs_prob")
        cst_full = sem("cst_full")
        cpt_ready = sem("cpt_ready")
        s_full = sem("s_full")
        s_max = sem("s_max")
        p_raw = sem("p_raw")
        r_scale = sem("r_scale")
        p_ready = sem("p_ready")
        t_full = sem("t_full")
        t_ready = sem("t_ready")
        pv_full = sem("pv_full")
        o_ready = sem("o_ready")


        def up_slot(g):
            return ring[:, g % 2, :]

        def full_count(g, more=0):
            return 16 * (g // 2 + 1) + 8 * more

        block = ctx.enter_context(nc.Block())

        def tiles(kinds, dests):
            out, q, r = [], 0, 0
            for kind, dest in zip(kinds, dests):
                out.append((kind, q if kind in ("shift", "rope1", "rope2") else None,
                            r if kind in ("rope1", "rope2") else None, dest))
                q += kind in ("shift", "rope1", "rope2")
                r += kind in ("rope1", "rope2")
            return out, q, r

        T1, Q1, R1 = tiles(["shift"] * SHIFT_TILES + ["rope1"] * 12,
                           [shifted[:, j * S:(j + 1) * S] for j in range(SHIFT_TILES)] + [qk1[:, j * S:(j + 1) * S] for j in range(12)])
        TG, _, _ = tiles(["sigmoid"] * 16, [sig[:, j * S:(j + 1) * S] for j in range(16)])
        T2, Q2, R2 = tiles(["rope2", "copy", "rope2", "rope2"] + ["rope2"] * 4 + ["copy"] * 4 + ["rope2"] * 4,
                           [cm2[:, j * S:(j + 1) * S] for j in range(16)])
        KK_SCALED, KK_SQUARED, KK_SUMMED, KK_CLAMPED, KK_ROOT, KK_INVERTED, KK_DONE = 13, 14, 17, 19, 20, (23, 25, 27), 29
        CM_G, CM_2 = len(T1), len(T1) + len(TG)

        DONE_MIX1, DONE_FFN1, DONE_A, DONE_MIX2, DONE_B, PER_LAYER_DONE = 0, 4, 7, 10, 14, 10
        BY_COLUMNS, BY_TOKENS = (0, 2, 1, 3), (0, 1, 2, 3)

        def since(base, k):
            return base + max(k, 0)

        def behind(base, k):
            return base + k if k > 0 else 0

        UNITS = []
        for t in range(4):
            for branch, ktile, v0 in ((1, 2, 0), (2, 3, 128)):
                for e in range(2):
                    UNITS.append((t, e, 4 + t, ktile, v0 + e * HD, 3 * (t + 4 * e) + branch, None))
        for t in range(2):
            for e in range(2):
                UNITS.append((4 + t, e, 8 + t, 10 + t, 256 + (2 * t + e) * HD, None, 2 * t + e))
        for t in range(2):
            for e in range(2):
                UNITS.append((6 + t, e, 12 + t, 14 + t, 512 + (2 * t + e) * HD, None, None))
        NU = len(UNITS)
        LAST_OF_PAIR = {u[0]: i for i, u in enumerate(UNITS)}
        S_BANK, T_BANK, O_BANK = (4, 5, 6), (7, 2), (1, 3)

        def half(e):
            return slice(HD * e, HD * e + HD)


        @block.sync
        def _(sp):
            sp.dma_start(params[:], T["params"]).then_inc(s_params, 16)
            released = [None, None]

            def load(g, src, release):
                if released[0]:
                    wait(sp, *released[0])
                n = src.shape[-1]
                sp.dma_start(ring[:, g % 2, 0:n], src).then_inc(slot_full[g % 2], 16)
                released[:] = [released[1], release]

            def ffn_split(g, f):
                up, dn = 2 * FC * (f - 1), FC * (f - 1)

                def step(c, i=0):
                    if c >= 2:
                        sp.wait_ge(up_low, up + 2 * (c - 1) + 2 * i)
                        sp.dma_start(ring[:, (g + c) % 2], T["up"][FC * f + c + i]).then_inc(slot_full[(g + c) % 2], 16)
                        sp.wait_ge(dn_low, dn + c - 1 + i)
                    else:
                        load(g + c, T["up"][FC * f + c], (up_low, up + 2 * (c + 1)))
                        sp.wait_ge(down_done, FC * f)
                    sp.dma_start(ring_down[:, c % 2], T["down"][FC * f + c + i]).then_inc(down_full[c % 2], 16)

                step(0)
                step(1)
                with sp.Fori(0, FC - 3, 2) as i:
                    step(2, i)
                    step(3, i)
                step(FC - 1)
                released[:] = [(up_low, up + 2 * (FC - 1)), (up_low, up + 2 * FC)]

            def ffn(g, f, with_ada=False):
                def ada(c, i=0):
                    if with_ada:
                        for s in range(2):
                            q, slot = 2 * (c - 2) + s, 2 * (c % 2) + s
                            sp.wait_ge(apart_used, 32 + q - 3 + 2 * i)
                            sp.dma_start(ada_slot[:, slot], T["ada"][ADA1_CHUNKS + q + 2 * i]).then_inc(apart_full[slot], 16)

                def down(c, i=0):
                    wait(sp, down_done, FC * f + (c + i - 1 if c >= 2 else 0))
                    sp.dma_start(ring_down[:, c % 2], T["down"][FC * f + c + i]).then_inc(down_full[c % 2], 16)

                for c in range(2):
                    load(g + c, T["up"][FC * f + c], (up_full, FC * f + c + 1))
                    down(c)
                if with_ada:
                    sp.wait_ge(bank_full, 4)
                with sp.Fori(0, FC - 3, 2) as i:
                    for c in (2, 3):
                        sp.wait_ge(up_full, FC * f + c + i - 1)
                        sp.dma_start(ring[:, (g + c) % 2], T["up"][FC * f + c + i]).then_inc(slot_full[(g + c) % 2], 16)
                        down(c, i)
                        ada(c, i)
                c = FC - 1
                sp.wait_ge(up_full, FC * f + c - 1)
                sp.dma_start(ring[:, (g + c) % 2], T["up"][FC * f + c]).then_inc(slot_full[(g + c) % 2], 16)
                down(c)
                ada(c)
                released[:] = [(up_full, FC * f + FC - 1), (up_full, FC * f + FC)]

            sp.dma_start(c_row, T["c"].broadcast_to([P, D])).then_inc(s_c, 16)
            load(0, T["ada"][0], (ada_used, 1))
            load(1, T["ada"][1], (ada_used, 2))
            sp.dma_start(x[:], T["x"].rearrange("p (t n) -> p t n", t=NT)).then_inc(s_x, 16)
            sp.dma_start(const[:], T["const"]).then_inc(s_const, 16)
            load(2, T["ada"][2], (ada_used, 3))
            load(3, T["ada"][3], (ada_used, 4))

            g = G_MIX1
            for c in range(8):
                load(g + c, T["in1"][c], (cm_full, 4 * (c + 1)))
                for s in range(4):
                    wait(sp, apart_used, 4 * c + s - 3)
                    sp.dma_start(ada_tile[:, s], T["ada"][FIRST + c, :, s * D:(s + 1) * D]).then_inc(apart_full[s], 16)
                if c == 2:
                    sp.dma_start(early, T["early"]).then_inc(s_lora, 16)
                    sp.dma_start(row[:], T["c_2"].broadcast_to([P, D])).then_inc(s_c2, 16)
            load(g + 8, T["in1"][8], (tm_full, 2))
            load(g + 9, T["in1_v"], (tm_full, 4))
            last_ada = ADA1_CHUNKS + ADA2_CHUNKS * (LAYERS - 1)
            for c in range(2):
                load(G_ADA + c, T["ada"][last_ada + c], (ada_used, FIRST + c + 1))
            with sp.Fori(1, ADA2_CHUNKS // 2) as i:
                two = T["ada"].rearrange("(c s) p n -> c s p n", s=2)
                for s in range(2):
                    sp.wait_ge(ada_used, FIRST + 2 * i + s - 1)
                    sp.dma_start(ring[:, s], two[last_ada // 2 + i, s]).then_inc(slot_full[s], 16)
            released[:] = [(ada_used, FIRST + ADA2_CHUNKS - 1), (ada_used, FIRST + ADA2_CHUNKS)]
            g = G_GATES
            for c in range(4):
                load(g + c, T["gates1"][c], (cm_full, 32 + 4 * (c + 1)))
            load(g + 4, T["w_b"], (ym_full, 8))
            for c in range(2):
                load(g + 5 + c, T["w_a"][c], (ym_full, 8 + 4 * (c + 1)))
            for c in range(2):
                load(g + 7 + c, T["w_out"][c], (bank_full, 2 * (c + 1)))
            sp.wait_ge(gn_var, 1)
            sp.dma_start(pos_i, T["pos"].broadcast_to([P, S])).then_inc(s_pos, 16)
            sp.dma_start(now[:], T["layers"][0]).then_inc(s_layers, 16)
            ffn(G_FFN1, 0, True)
            with sp.Fori(0, LAYERS) as l:
                released[:] = [(down_done, FC * (1 + 2 * l) - 1), (down_done, FC * (1 + 2 * l) - 1)]
                ffn_split(G_LAYER, 1 + 2 * l)
                g = G_LAYER + FC
                for c in range(4):
                    a, w = IN2_AT[c], 8 * IN2_WIDTHS[c]
                    load(g + c, T["in2"][l, :, a:a + w], (cm_full, 48 + 16 * l + 4 * (c + 1)))
                for c in (4, 5):
                    a, w = IN2_AT[c], 8 * IN2_WIDTHS[c]
                    load(g + c, T["in2"][l, :, a:a + w], (tm_full, 4 + 4 * l + 2 * (c - 3)))
                for c in range(2):
                    load(g + 6 + c, T["cmp1"][2 * l + c], (cmp_full, 2 * l + c + 1))
                for c in range(2):
                    load(g + 8 + c, T["w_out2"][2 * l + c], (bank_full, DONE_MIX2 + PER_LAYER_DONE * l + 2 * (c + 1)))
                sp.wait_ge(o_ready, 8 * (l + 1))
                sp.dma_start(now[:], T["layers"][l + 1]).then_inc(s_layers, 16)
                ffn_split(g + MIX2_CHUNKS, 2 + 2 * l)
            sp.wait_ge(s_layers, 16 * (LAYERS + 1))
            sp.wait_ge(y_ready, NT)
            sp.dma_start(out, xn[:]).then_inc(s_out, 16)
            sp.wait_ge(s_out, 16)
        @block.tensor
        def _(pe):
            mm = pe.matmul

            def chunk(g, more=0):
                pe.wait_ge(slot_full[g % 2], full_count(g, more))
                return up_slot(g)

            def keep_warm(times, b):
                for _ in range(times):
                    mm(bank[b][:, 0:P], ident, ident, start=True, stop=True)

            def transposes(n):
                if not (isinstance(n, int) and n == 0):
                    keep_warm(20, 7)
                for t in range(NT):
                    pe.wait_ge(xn_ready, 2 * n + t + 1)
                    for b in range(4):
                        for k in range(2):
                            last = pe.transpose(bank[4 + b][:, k * S + t * P:k * S + t * P + P],
                                                xn[:, t, (2 * b + k) * P:(2 * b + k + 1) * P], ident)
                        if t == NT - 1:
                            last.then_inc(ht_full, 1)

            def gate_row(n, column):
                if isinstance(n, int) and n == 0:
                    pe.wait_ge(mod_ready, 2)
                wait(pe, fin_read, 4 * n)
                for k in range(KD):
                    last = mm(bank[k // 4][:, (k % 4) * P:(k % 4 + 1) * P], column[:, k:k + 1].broadcast_to([P, P]), ident,
                              start=True, stop=True)
                last.then_inc(row_full, 1)

            def wait_ht(n):
                pe.wait_ge(ht_act, n + 1)
                pe.wait_ge(ht_dve, n + 1)

            def ffn(g, f, n, more=0):
                def up(c, i=0):
                    w = chunk(g + c, more + i)
                    if c >= 2:
                        pe.wait_ge(act_ready, FC * f + c + i - 1)
                    for j in range(4):
                        dst = bank[4 + 2 * (c % 2) + j // 2][:, (j % 2) * S:(j % 2 + 1) * S]
                        for k in range(KD):
                            last = mm(dst, w[:, k * 512 + j * P:k * 512 + j * P + P], hT[:, k, :],
                                      start=(k == 0), stop=(k == KD - 1))
                    last.then_inc(up_full, 1)

                def down(c, i=0):
                    pe.wait_ge(act_ready, FC * f + c + i + 1)
                    pe.wait_ge(down_full[c % 2], 16 * ((6 - c % 2) * f + c // 2 + 1) + 8 * i)
                    for t in range(NT):
                        for h in range(2):
                            for k in range(2):
                                last = mm(bank[2 * t + h], act_t[:, c % 2, k, t * P:(t + 1) * P],
                                          ring_down[:, c % 2, k * D + h * 512:k * D + h * 512 + 512],
                                          start=(c == 0 and k == 0), stop=(c == FC - 1 and k == 1), skip_group_check=True)
                            if c == FC - 1 and 2 * t + h < 3:
                                last.then_inc(bank_full, 1)
                    last.then_inc(down_done, 1)

                wait_ht(n)
                up(0)
                up(1)
                pe.wait_ge(row_ready, n + 1)
                down(0)
                with pe.Fori(0, FC - 3, 2) as i:
                    up(2, i)
                    down(1, i)
                    up(3, i)
                    down(2, i)
                up(FC - 1)
                down(FC - 2)
                down(FC - 1)

            def ffn_split(f, n):
                def up(c, i=0):
                    if c >= 2:
                        pe.wait_ge(act_ready, FC * f + c + i - 1)
                    for h in range(2):
                        pe.wait_ge(up_low, 2 * FC * (f - 1) + 2 * c + h + 1 + 2 * i)
                        if c == 0:
                            pe.wait_ge(h_low_last if h else h_low, f)
                        for j in range(4):
                            dst = bank[4 + 2 * (c % 2) + j // 2][:, (j % 2) * S:(j % 2 + 1) * S]
                            for k in range(4):
                                a, tile = slice(k * 512 + j * P, k * 512 + j * P + P), 4 * h + k
                                mm(dst, up_hi[:, h, a], h_hi[:, tile], start=(tile == 0 and j % 2 == 0), stop=False, skip_group_check=True)
                                mm(dst, up_hi[:, h, a], h_lo[:, tile], start=False, stop=False, skip_group_check=True)
                                last = mm(dst, up_lo[:, h, a], h_hi[:, tile], start=False, stop=(tile == KD - 1), skip_group_check=True)
                        last.then_inc(half_done, 1)

                def down(c, i=0):
                    pe.wait_ge(act_low, FC * (f - 1) + c + i + 1)
                    pe.wait_ge(dn_low, FC * (f - 1) + c + i + 1)
                    for t in range(NT):
                        for h in range(2):
                            for k in range(2):
                                a, w = slice(k * S + t * P, k * S + t * P + P), slice(k * D + h * 512, k * D + h * 512 + 512)
                                mm(bank[2 * t + h], act_hi[:, c % 2, a], dn_hi[:, w], start=(c == 0 and k == 0), stop=False, skip_group_check=True)
                                mm(bank[2 * t + h], act_hi[:, c % 2, a], dn_lo[:, w], start=False, stop=False, skip_group_check=True)
                                last = mm(bank[2 * t + h], act_lo[:, c % 2, a], dn_hi[:, w], start=False, stop=(c == FC - 1 and k == 1), skip_group_check=True)
                            if c == FC - 1 and 2 * t + h < 3:
                                last.then_inc(bank_full, 1)
                    last.then_inc(down_done, 1)

                up(0)
                up(1)
                pe.wait_ge(row_ready, n + 1)
                down(0)
                with pe.Fori(0, FC - 3, 2) as i:
                    up(2, i)
                    down(1, i)
                    up(3, i)
                    down(2, i)
                up(FC - 1)
                down(FC - 2)
                down(FC - 1)

            def channel_major(g, table, base, rbase, more=0):
                def rotate(j):
                    kind, q, r, _ = table[j]
                    if r is None:
                        return
                    pe.wait_ge(cm_evac, base + j + 1)
                    wait(pe, rope_used, since(rbase, r - 1))
                    mm(bank[6 + r % 2][:, 0:S], K(kind), raw[:, q % 3, 1:S + 1], start=True, stop=True).then_inc(rope_full, 1)

                for j in range(len(table)):
                    if j % 4 == 0:
                        w = chunk(g + j // 4, more)
                    wait(pe, cm_evac, since(base, j - 1))
                    n = j % 4
                    for k in range(KD):
                        last = mm(bank[4 + j % 2][:, 0:S], w[:, k * 512 + n * P:k * 512 + n * P + P], hT[:, k, :],
                                  start=(k == 0), stop=(k == KD - 1))
                    last.then_inc(cm_full, 1)
                    if j:
                        rotate(j - 1)
                    if table is T1 and j == KK_SUMMED:
                        pe.wait_ge(sq_ready, 1)
                        for n in range(3):
                            last = mm(bank[n], K("blockones"), norm_kk[:, n * 512:(n + 1) * 512], start=True, stop=True)
                        last.then_inc(kn_full, 1)
                rotate(len(table) - 1)

            def token_major(g, width, banks, more=0):
                w = chunk(g, more)
                for t in range(NT):
                    for k in range(KD):
                        last = mm(bank[banks[t]][:, 0:width], hT[:, k, t * P:(t + 1) * P], w[:, k * width:(k + 1) * width],
                                  start=(k == 0), stop=(k == KD - 1))
                    last.then_inc(tm_full, 1)

            def project(g, lhs, more=0):
                for h in range(2):
                    w = chunk(g + h, more)
                    for t in range(NT):
                        for k in range(KD):
                            last = mm(bank[2 * t + h], lhs(k, t), w[:, k * 512:(k + 1) * 512], start=(k == 0), stop=(k == KD - 1))
                        last.then_inc(bank_full, 1)

            def attention1():
                def heads(i):
                    return [((4 * g + i) // 2, half(i % 2), (4 * g + i) * HD) for g in range(3)]

                def qk(i):
                    wait(pe, s1_max, i)
                    for g, (tile, h, _) in enumerate(heads(i)):
                        q, k = qk1[h, tile * S:(tile + 1) * S], qk1[h, (6 + tile) * S:(7 + tile) * S]
                        mm(bank[4 + g][:, 0:P], q[:, 0:P], k[:, 0:P], start=True, stop=True)
                        last = mm(bank[4 + g][:, P:P + S], q[:, P:S], k, start=True, stop=True)
                    last.then_inc(s1_full, 1)

                pe.wait_ge(cm_out, Q1)
                pe.wait_ge(tm_ready, 4)
                qk(0)
                qk(1)
                for i in range(4):
                    if i < 2:
                        qk(i + 2)
                    keep_warm(20, 0)
                    pe.wait_ge(s1_prob, i + 1)
                    wait(pe, s1_tr, 3 * i)
                    for g in range(3):
                        b = bank[(7, 2, 1)[g]]
                        for n in range(3):
                            last = pe.transpose(b[:, n * P:(n + 1) * P], p1[:, i % 2, g, n * P:(n + 1) * P], ident)
                        last.then_inc(s1_t, 1)
                    keep_warm(8, 0)
                    pe.wait_ge(s1_tr, 3 * i + 3)
                    dst = bank[3][half(i % 2), (i // 2) * S:(i // 2 + 1) * S]
                    wait(pe, s1_o, i)
                    for g, (_, _, vc) in enumerate(heads(i)):
                        mm(dst, v1[:, 0, vc:vc + HD], pt1[:, g, 0:S], start=(g == 0), stop=False, skip_group_check=True)
                        last = mm(dst[:, P:S], v1[:, 1, vc:vc + HD], pt1[:, g, S:S + P], start=False, stop=(g == 2), skip_group_check=True)
                    last.then_inc(s1_pv, 1)

            def rwkv():
                pe.wait_ge(lr_in, 1)
                pe.wait_ge(s1_o, 4)
                pe.wait_ge(s_lora, 16)
                for w in range(PAIRS):
                    if w >= 2:
                        keep_warm(8, 0)
                    wait(pe, lr_ready, w - 1)
                    b0, b1 = bank[4 + 2 * (w % 2)], bank[5 + 2 * (w % 2)]
                    c = slice(w * P, (w + 1) * P)
                    mm(b0[:, 0:S], lora[0:64, c], shifted[0:64, 18 * S:19 * S], start=True, stop=True)
                    mm(b1[:, 0:S], lora[64:128, c], shifted[64:128, 18 * S:19 * S], start=True, stop=True)
                    mm(b0[:, S:2 * S], lora[:, RW + w * P:RW + (w + 1) * P], shifted[:, 19 * S:20 * S],
                       start=True, stop=True).then_inc(lr_full, 1)
                pe.wait_ge(lr_ready, PAIRS)
                for ps in range(PAIRS // 2):
                    wait(pe, pass_done, ps)
                    for lp in range(2):
                        w = 2 * ps + lp
                        keep_warm(16, 0)
                        pe.wait_ge(pool_prep, w + 1)
                        pe.wait_ge(dve_prep, w + 1)
                        wait(pe, bon_ready, w)
                        mm(bank[3][:, 0:S], K("blockones"), cs[:, lp], start=True, stop=True).then_inc(bon_full, 1)
                        for h in range(2):
                            t = slice(h * P, (h + 1) * P)
                            n = 2 * w + h
                            wait(pe, tr_ready, n - 1)
                            b = bank[2 - h]
                            for j, src in enumerate((v_t[:, w * S:(w + 1) * S][:, t], kbuf[:, lp, t], bbuf[:, lp, t], kr[:, lp, h, 0])):
                                last = pe.transpose(b[:, j * P:(j + 1) * P], src, ident)
                            last.then_inc(tr_full, 1)
                            for e in range(2):
                                wait(pe, sc_read, 2 * n + e - 1)
                                hs = half(e)
                                both = kr[hs, lp, h].rearrange("p k n -> p (k n)")
                                mm(bank[4 + e][:, 0:S], bt[hs, lp, t], both, start=True, stop=True)
                                mm(bank[4 + e][:, S:2 * S], kt[hs, lp, t], both, start=True, stop=True)
                                mm(bank[6 + e][:, 0:P], kr[hs, lp, h, 0], bt[hs, lp, t], start=True, stop=True).then_inc(sc_full, 1)
                    pe.wait_ge(sc_ready, 4 * (ps + 1))
                    pe.wait_ge(tr_ready, 4 * (ps + 1))
                    for m in range(8):
                        e = m % 2
                        last = mm(bank[6][:, m * HD:(m + 1) * HD], scores[:, m, 2], vkb[:, m // 2, 0, e * HD:(e + 1) * HD],
                                  start=True, stop=True)
                    last.then_inc(av_full, 1)
                    pe.wait_ge(y0_ready, 4 * (ps + 1))
                    pe.wait_ge(bon_ready, 2 * (ps + 1))
                    for j in range(len(LEVELS)):
                        q = (ps * len(LEVELS) + j) * 2
                        for lp in range(2):
                            pe.wait_ge(nl_ready, q + lp + 1)
                            if j:
                                pe.wait_ge(xy_ready, q + lp - 1)
                            wait(pe, w_ready, q + lp - 1)
                            for n in range(4):
                                m = 4 * lp + n
                                last = mm(bank[lp][:, n * P:(n + 1) * P], inv_n[:, m], inv_x[:, m], start=True, stop=True)
                            last.then_inc(w_full, 1)
                        for lp in range(2):
                            pe.wait_ge(w_ready, q + lp + 1)
                            for n in range(4):
                                m = 4 * lp + n
                                c = slice(n * P, (n + 1) * P)
                                if j < len(LEVELS) - 1:
                                    mm(bank[2 + lp][:, c], inv_y[:, m], inv_w[:, m], start=True, stop=True)
                                last = mm(bank[4 + lp][:, c], inv_w[:, m], inv_y[:, m], start=True, stop=True)
                            last.then_inc(p_full, 1)
                    pe.wait_ge(xy_ready, 10 * (ps + 1))
                    pe.wait_ge(av_ready, ps + 1)
                    for m in range(8):
                        last = mm(bank[m // 4][:, (m % 4) * P:(m % 4 + 1) * P], inv_y[:, m], avk[:, m], start=True, stop=True)
                    last.then_inc(nw_full, 1)
                    pe.wait_ge(nw_ready, ps + 1)
                    for m in range(8):
                        lp, h, e = m // 4, (m // 2) % 2, m % 2
                        c = slice(lp * S + h * P, lp * S + (h + 1) * P)
                        mm(bank[2][half(e), c], vkb[:, m // 2, 0, e * HD:(e + 1) * HD], scores[:, m, 3], start=True, stop=False, skip_group_check=True)
                        mm(bank[2][half(e), c], nw[:, m, 0:HD], scores[:, m, 1], start=False, stop=True, skip_group_check=True)
                        last = mm(bank[3][half(e), c], nw[:, m, HD:P], scores[:, m, 1], start=True, stop=True)
                    last.then_inc(hg_full, 1)
                    for lp in range(2):
                        for e in range(2):
                            ec = slice(e * HD, (e + 1) * HD)
                            for c, b, z, t in ((0, 6, 0, None), (2, 6, 64, 128), (1, 7, 0, 64)):
                                m = 4 * lp + 2 * (c // 2) + e
                                rows = slice(HD * (c % 2), HD * (c % 2) + HD)
                                v, kp, bp = (vkb[rows, m // 2, k, ec] for k in range(3))
                                dst = bank[b][half(e), lp * S + z:lp * S + z + HD]
                                mm(dst, kp, v, start=True, stop=False, skip_group_check=True)
                                last = mm(dst, bp, nw[rows, m, 0:HD], start=False, stop=True, skip_group_check=True)
                                if t is not None:
                                    last = mm(bank[b][half(e), lp * S + t:lp * S + t + HD], nw[rows, m, HD:P], bp, start=True, stop=True)
                    last.then_inc(zt_full, 1)
                    for step in range(2):
                        keep_warm(8, 5)
                        pe.wait_ge(zt_ready, ps + 1)
                        if step:
                            pe.wait_ge(m_ready, 2 * ps + 1)
                        for lp in range(2):
                            last = mm(bank[step][:, lp * P:(lp + 1) * P], trans[:, lp, step], state[:, lp, step], start=True, stop=True)
                        last.then_inc(m_full, 1)
                    pe.wait_ge(m_ready, 2 * ps + 2)
                    pe.wait_ge(g_ready, ps + 1)
                    for lp in range(2):
                        for c in range(1, 4):
                            last = mm(bank[4][:, lp * S + c * C:lp * S + (c + 1) * C], state[:, lp, c - 1],
                                      kr[:, lp, c // 2, 1, (c % 2) * C:(c % 2 + 1) * C], start=True, stop=True)
                    last.then_inc(yc_full, 1)
                pe.wait_ge(pass_done, PAIRS // 2)
                for n in range(3):
                    last = mm(bank[n], K("blockones"), ymix[:, n * 512:(n + 1) * 512], start=True, stop=True)
                last.then_inc(gn_mu, 1)
                pe.wait_ge(gn_sq, 1)
                for n in range(3):
                    last = mm(bank[5 + n], K("blockones"), sq[:, n * 512:(n + 1) * 512], start=True, stop=True)
                last.then_inc(gn_var, 1)

            def merge():
                w = chunk(G_GATES + 4)
                pe.wait_ge(cm_evac, CM_G + 16)
                for n in range(16):
                    if n >= 8 and n % 4 == 0:
                        w = chunk(G_GATES + 5 + (n - 8) // 4)
                    if n == 8:
                        pe.wait_ge(gn_ready, PAIRS)
                    wait(pe, ym_read, n - 1)
                    for k in range(2 if n < 8 else 6):
                        if n < 8:
                            lhs, rhs = w[:, k * D + n * P:k * D + n * P + P], o1[:, k * S:(k + 1) * S]
                        else:
                            lhs, rhs = w[:, k * 512 + (n % 4) * P:k * 512 + (n % 4) * P + P], ymix[:, k * S:(k + 1) * S]
                        last = mm(bank[4 + n % 2][:, 0:S], lhs, rhs, start=(k == 0), stop=(k == (1 if n < 8 else 5)))
                    last.then_inc(ym_full, 1)

            def mixer2(l):
                n = 3 + 3 * l
                more = PER_LAYER * l
                g = G_LAYER + FC
                base, qbase, rbase, U = CM_2 + 16 * l, Q1 + Q2 * l, R1 + R2 * l, NU * l
                wait_ht(n)
                channel_major(g, T2, base, rbase, more)
                pe.wait_ge(row_ready, n + 1)
                pe.wait_ge(cm_out, qbase + 1)
                for i in range(2):
                    last = mm(bank[i][:, 0:S], K("swap"), cm2[:, i * S:(i + 1) * S], start=True, stop=True)
                last.then_inc(swap_full, 1)
                pe.wait_ge(cm_evac, base + 16)
                pe.wait_ge(rope_used, rbase + R2)
                token_major(g + 4, 512, (4, 5), more)
                token_major(g + 5, IN2_WIDTHS[5], (6, 7), more)
                for i in range(2):
                    w = chunk(g + 6 + i, more)
                    if i == 0:
                        pe.wait_ge(zb_ready, l + 1)
                    for h in range(2):
                        for j in range(16):
                            last = mm(bank[2][:, (2 * i + h) * 32:(2 * i + h + 1) * 32], w[:, j * S + h * P:j * S + h * P + P],
                                      zb[:, i, j].rearrange("p g c -> p (g c)"), start=(j == 0), stop=(j == 15))
                    last.then_inc(cmp_full, 1)
                pe.wait_ge(gelu_ready, l + 1)
                for e in range(2):
                    for h in range(2):
                        mm(bank[3][half(e), 0:16], NOW("cmp_w2", h * HD, (h + 1) * HD), gh[:, 0, h, e * 16:(e + 1) * 16],
                           start=(h == 0), stop=(h == 1), skip_group_check=True)
                pe.wait_ge(ghrep_ready, l + 1)
                for h in range(2):
                    last = mm(bank[3][:, 64:128], ghrep[:, h], NOW("cmp_w2", (2 + h) * HD, (3 + h) * HD),
                              start=(h == 0), stop=(h == 1), skip_group_check=True)
                last.then_inc(cmp2_full, 1)
                pe.wait_ge(lf_ready, l + 1)
                mm(bank[2][:, 0:P], lf8[:, 0], K("tri"), start=True, stop=True)
                mm(bank[2][:, P:S], lf8[:, 0], K("ones"), start=True, stop=False, skip_group_check=True)
                mm(bank[2][:, P:S], lf8[:, 1], K("tri"), start=False, stop=True, skip_group_check=True).then_inc(f_full, 1)
                pe.wait_ge(cmp_ready, l + 1)
                pe.wait_ge(cm_out, qbase + Q2)
                for e in range(2):
                    for t in range(NT):
                        for j in range(4):
                            last = mm(bank[e][:, t * 64 + j * 16:t * 64 + (j + 1) * 16], cm2[half(e), (4 + j) * S + t * P:(4 + j) * S + (t + 1) * P],
                                      kcmp[half(e), 0:16], start=True, stop=True)
                last.then_inc(cs_full, 1)
                keep_warm(16, 3)
                pe.wait_ge(cs_prob, l + 1)
                for t in range(NT):
                    last = pe.transpose(bank[0][:, t * P:(t + 1) * P], csm[:, t * P:(t + 1) * P], ident)
                last.then_inc(cst_full, 1)
                pe.wait_ge(tm_ready, 8 + 4 * l)
                pe.wait_ge(f_ready, l + 1)

                def qk(u):
                    _, e, qt, ktile, _, _, fox = UNITS[u]
                    wait(pe, s_max, behind(U, u - 2))
                    b = bank[S_BANK[u % 3]]
                    q, k = cm2[half(e), qt * S:(qt + 1) * S], cm2[half(e), ktile * S:(ktile + 1) * S]
                    for qs, ks, dst in ((slice(0, P), slice(0, P), b[:, 0:P]), (slice(P, S), slice(0, S), b[:, P:P + S])):
                        last = mm(dst, q[:, qs], k[:, ks], start=True, stop=(fox is None), skip_group_check=True)
                        if fox is not None:
                            pick = K("fox_row", fox, fox + 1)[half(e)]
                            width = ks.stop - ks.start
                            mm(dst, pick.broadcast_to([HD, P]), f_neg[half(e), ks], start=False, stop=False, skip_group_check=True)
                            last = mm(dst, f_pos[half(e), qs], pick.broadcast_to([HD, width]), start=False, stop=True, skip_group_check=True)
                    last.then_inc(s_full, 1)

                def turn(u):
                    pe.wait_ge(p_ready, U + u + 1)
                    wait(pe, t_ready, behind(U, u - 1))
                    b = bank[T_BANK[u % 2]]
                    for n in range(3):
                        last = pe.transpose(b[:, n * P:(n + 1) * P], pb[:, u % 4, n * P:(n + 1) * P], ident)
                    last.then_inc(t_full, 1)

                def pv(u):
                    pair, e, _, _, vc, gate, _ = UNITS[u]
                    first = not any(x[0] == pair and x[1] == e for x in UNITS[:u])
                    final = not any(x[0] == pair and x[1] == e for x in UNITS[u + 1:])
                    dst = bank[O_BANK[pair % 2]][half(e), 0:S]
                    if first:
                        wait(pe, o_ready, behind(8 * l, pair - 1))
                        if gate is not None:
                            pe.wait_ge(cpt_ready, l + 1)
                            mm(dst, vblk[:, pair + 4 * e], cpt, start=True, stop=False, skip_group_check=True)
                    pe.wait_ge(t_ready, U + u + 1)
                    mm(dst, v2[:, 0, vc:vc + HD], pt[:, u % 2, 0:S], start=(first and gate is None), stop=False, skip_group_check=True)
                    mm(dst[:, P:S], v2[:, 1, vc:vc + HD], pt[:, u % 2, S:S + P], start=False, stop=final,
                       skip_group_check=True).then_inc(pv_full, 1)

                for i in range(NU + 4):
                    if i < NU:
                        qk(i)
                    if 3 <= i < NU + 3:
                        turn(i - 3)
                    if i >= 4:
                        pv(i - 4)
                pe.wait_ge(o_ready, 8 * (l + 1))
                project(g + 8, lambda k, t: o2[:, k * S + t * P:k * S + (t + 1) * P], more)

            pe.wait_ge(s_const, 16)
            transposes(0)
            wait_ht(0)
            channel_major(G_MIX1, T1, 0, 0)
            pe.wait_ge(kn_clamped, 1)
            token_major(G_MIX1 + 8, 512, (0, 1))
            token_major(G_MIX1 + 9, 256, (2, 3))
            attention1()
            rwkv()
            pe.wait_ge(gn_ms, 1)
            gate_row(0, mod_gate[:, 0])
            channel_major(G_GATES, TG, CM_G, 0)
            merge()
            pe.wait_ge(ym_ready, 8)
            pe.wait_ge(row_ready, 1)
            project(G_GATES + 7, lambda k, t: merged[:, k * S + t * P:k * S + (t + 1) * P])
            transposes(1)
            gate_row(1, mod_gate[:, 1])
            ffn(G_FFN1, 0, 1)
            with pe.Fori(0, LAYERS) as l:
                more = PER_LAYER * l
                transposes(2 + 3 * l)
                pe.wait_ge(mod_ready, 3 + l)
                gate_row(2 + 3 * l, mod_gate[:, 0])
                ffn_split(1 + 2 * l, 2 + 3 * l)
                transposes(3 + 3 * l)
                gate_row(3 + 3 * l, mod_gate[:, 1])
                mixer2(l)
                transposes(4 + 3 * l)
                gate_row(4 + 3 * l, mod_gate[:, 2])
                ffn_split(2 + 2 * l, 4 + 3 * l)
            gate_row(8, PR("final_g"))


        @block.scalar
        def _(act):
            f = F = act.activation

            def to_row(n):
                act.wait_ge(row_full, n + 1)
                f(row[:], psum[:, 0:2, :].rearrange("p b n -> p (b n)"), ACT.Copy).then_inc(row_ready, 1)

            def high_up(f, g, c, h, i=0, more=0):
                if h == 0:
                    act.wait_ge(slot_full[(g + c) % 2], full_count(g + c, more + i))
                wait(act, half_done, 2 * FC * (f - 1) + 2 * (c - 1) + h + 1 + 2 * i if c else 0)
                F(up_hi[:, h], ring[:, (g + c) % 2, h * 2048:(h + 1) * 2048], ACT.Copy).then_inc(up_high, 1)

            def high_down(f, c, i=0):
                act.wait_ge(down_full[c % 2], 16 * ((6 - c % 2) * f + c // 2 + 1) + 8 * i)
                if c:
                    act.wait_ge(down_done, FC * f + c + i)
                F(dn_hi, ring_down[:, c % 2], ACT.Copy).then_inc(dn_high, 1)

            def ffn_split(f, g, more):
                def one(c, i=0):
                    if c < FC - 1:
                        high_up(f, g, c + 1, 0, i, more)
                    act.wait_ge(half_done, 2 * FC * (f - 1) + 2 * (c + 1) + 2 * i)
                    wait(act, act_ready, FC * f + c + i - 1 if c >= 2 else FC * f)
                    F(silu[:, c % 2], bank[4 + 2 * (c % 2)], ACT.Silu).then_inc(silu_ready, 1)
                    if c < FC - 1:
                        high_up(f, g, c + 1, 1, i, more)
                    high_down(f, c, i)

                high_up(f, g, 0, 1, 0, more)
                one(0)
                one(1)
                with act.Fori(0, FC - 3, 2) as i:
                    one(2, i)
                    one(3, i)
                one(FC - 1)

            def norm(n, sub, mods=None, order=BY_TOKENS, rows=True, split_of=None):
                f(stat[:, 30:31], K("ones", 0, 1), ACT.Sqrt)
                for i, j in enumerate(order):
                    if isinstance(n, int) and n == 0:
                        act.wait_ge(s_x, 16)
                    else:
                        act.wait_ge(x_ready, 4 * n - 3 + i)
                    c = slice(j % 2 * 512, (j % 2 + 1) * 512)
                    f(xn[:, j // 2, c], x[:, j // 2, c], ACT.Square, accum_out=stat[:, 20 + j:21 + j]).then_inc(ss_ready, 1)
                act.wait_ge(ms_ready, n + 1)
                f(stat[:, 4:6], stat[:, 2:4], ACT.Sqrt).then_inc(sd_ready, 1)
                if not rows:
                    to_row(n)
                    return
                if split_of is not None:
                    high_up(*split_of)
                act.wait_ge(mod_ready, mods)
                for b in range(2):
                    act.wait_ge(ht_full, 4 * n + b + 1)
                    for k in (2 * b, 2 * b + 1):
                        last = f(hT[:, k], bank[4 + b][:, (k % 2) * S:(k % 2 + 1) * S], ACT.Identity,
                                 bias=mod[:, 24 * sub + k:24 * sub + k + 1], scale=mod_scale[:, sub, k:k + 1])
                        if split_of is not None:
                            last = f(h_hi[:, k], bank[4 + b][:, (k % 2) * S:(k % 2 + 1) * S], ACT.Identity,
                                     bias=mod[:, 24 * sub + k:24 * sub + k + 1], scale=mod_scale[:, sub, k:k + 1])
                last.then_inc(ht_act, 1)
                if not (isinstance(n, int) and n == 0):
                    to_row(n)

            def channel_major(table, base, qbase):
                for j, (kind, q, _, dest) in enumerate(table):
                    act.wait_ge(cm_full, base + j + 1)
                    if q is not None:
                        wait(act, cm_out, since(qbase, q - 2))
                        dest = raw[:, q % 3, 1:S + 1]
                    f(dest, bank[4 + j % 2][:, 0:S], ACT.Sigmoid if kind == "sigmoid" else ACT.Copy).then_inc(cm_evac, 1)
                    if table is T1 and j == KK_ROOT:
                        act.wait_ge(kn_clamped, 1)
                        f(norm_kk, norm_kk, ACT.Sqrt).then_inc(kn_sqrt, 1)

            def ffn(fn):
                def one(c, i=0):
                    act.wait_ge(up_full, FC * fn + c + i + 1)
                    wait(act, act_ready, FC * fn + c + i - 1 if c >= 2 else FC * fn)
                    f(silu[:, c % 2], bank[4 + 2 * (c % 2)], ACT.Silu).then_inc(silu_ready, 1)
                one(0)
                one(1)
                with act.Fori(0, FC - 3, 2) as i:
                    one(2, i)
                    one(3, i)
                one(FC - 1)

            def rms_of_output(n, done, order, downs=None):
                for i, j in enumerate(order):
                    if i == 3 and downs is not None:
                        act.wait_ge(down_done, downs)
                    else:
                        act.wait_ge(bank_full, done + i + 1)
                    f(xn_flat[:, j * 512:(j + 1) * 512], bank[j], ACT.Square, accum_out=stat[:, 8 + j:9 + j]).then_inc(fss_ready, 1)
                act.wait_ge(fms_ready, n + 1)
                f(stat[:, 14:16], stat[:, 12:14], ACT.Sqrt).then_inc(fsd_ready, 1)

            def attention1():
                def exps(i):
                    act.wait_ge(s1_max, i + 1)
                    c = 2 * (i % 2)
                    for q, (a, b) in enumerate(((0, P), (P, 384))):
                        last = f(p1[:, i % 2, :, a:b], p1[:, i % 2, :, a:b], ACT.Exp, bias=nb[:, c + q:c + q + 1], scale=SCALE,
                                 accum_out=rs[:, c + q:c + q + 1])
                    last.then_inc(s1_exp, 1)
                exps(0)
                for i in range(4):
                    if i < 3:
                        exps(i + 1)
                    act.wait_ge(s1_pv, i + 1)
                    c = slice((i // 2) * S, (i // 2 + 1) * S)
                    f(o1[half(i % 2), c], bank[3][half(i % 2), c], ACT.Copy).then_inc(s1_o, 1)

            def rwkv():
                act.wait_ge(cm_out, SHIFT_TILES)
                f(shifted[0:64, 18 * S:19 * S], shifted[0:64, 18 * S:19 * S], ACT.Tanh)
                f(shifted[:, 19 * S:20 * S], shifted[:, 19 * S:20 * S], ACT.Sigmoid).then_inc(lr_in, 1)
                for w in range(PAIRS):
                    act.wait_ge(lr_full, w + 1)
                    b0, b1 = bank[4 + 2 * (w % 2)], bank[5 + 2 * (w % 2)]
                    c = slice(w * S, (w + 1) * S)
                    f(sgw[:, c], b0[:, 0:S], ACT.Sigmoid, bias=PR("w0", w, w + 1))
                    f(iclr[:, c], b1[:, 0:S], ACT.Sigmoid, bias=PR("a0", w, w + 1))
                    f(gate1[:, c], b0[:, S:2 * S], ACT.Copy).then_inc(lr_ready, 1)
                for ps in range(PAIRS // 2):
                    wait(act, pass_done, ps)
                    for lp in range(2):
                        act.wait_ge(cs_ready, 2 * ps + lp + 1)
                        act.wait_ge(bd_zero, 1)
                        c4 = cs[:, lp].rearrange("p (c n) -> p c n", c=4)
                        f(decay[:, lp, :, 1:C + 1], c4, ACT.Exp, scale=-DECAY)
                        f(decay_inv[:, lp], cs[:, lp], ACT.Exp, scale=DECAY).then_inc(e_ready, 1)
                    act.wait_ge(av_full, ps + 1)
                    f(avk[:, :, 0:HD], bank[6].rearrange("p (m n) -> p m n", m=8), ACT.Copy).then_inc(av_ready, 1)
                    for j in range(len(LEVELS)):
                        for lp in range(2):
                            q = (ps * len(LEVELS) + j) * 2 + lp
                            act.wait_ge(w_full, q + 1)
                            wait(act, p_full, q - 1)
                            f(inv_w[:, 4 * lp:4 * lp + 4].rearrange("p m n -> p (m n)"), bank[lp], ACT.Copy).then_inc(w_ready, 1)
                    act.wait_ge(nw_full, ps + 1)
                    f(nw.rearrange("p m n -> p (m n)"), psum[:, 0:2].rearrange("p b n -> p (b n)"), ACT.Copy, scale=-1.0).then_inc(nw_ready, 1)
                    act.wait_ge(hg_full, ps + 1)
                    f(ymix[:, ps * 512:(ps + 1) * 512], bank[2], ACT.Copy).then_inc(h_ready, 1)
                act.wait_ge(gn_ms, 1)
                f(sq, sq, ACT.Sqrt).then_inc(gn_sd, 1)

            def mixer2(l):
                base, qbase, U = CM_2 + 16 * l, Q1 + Q2 * l, NU * l
                channel_major(T2, base, qbase)
                for i, (c0, c1) in enumerate(((0, 512), (512, 796))):
                    for t in range(NT):
                        act.wait_ge(tm_full, 4 + 4 * l + 2 * i + t + 1)
                        f(v2[:, t, c0:c1], bank[4 + 2 * i + t][:, 0:c1 - c0], ACT.Copy).then_inc(tm_ready, 1)
                act.wait_ge(tm_ready, 8 + 4 * l)
                f(g2sig, v2[:, :, 768:792], ACT.Exp, scale=-1.0).then_inc(gate_exp, 1)
                act.wait_ge(fx_neg, l + 1)
                f(ftmp[:, 16:24], ftmp[:, 8:16], ACT.Exp).then_inc(fx_exp, 1)
                act.wait_ge(fx_exp, l + 1)
                f(ftmp[:, 24:32], ftmp[:, 16:24], ACT.Ln, bias=1.0).then_inc(fx_ln, 1)
                act.wait_ge(cmp_full, 2 * l + 2)
                f(gh.rearrange("p i h n -> p (i h n)"), bank[2][:, 0:P], ACT.Gelu_apprx_tanh).then_inc(gelu_ready, 1)
                act.wait_ge(cs_sub, l + 1)
                f(csm, csm, ACT.Exp, scale=SCALE).then_inc(cs_exp, 1)
                act.wait_ge(cst_full, l + 1)
                f(cpt, bank[0][:, 0:S], ACT.Copy).then_inc(cpt_ready, 1)
                for i in range(NU + 5):
                    if i < NU:
                        act.wait_ge(s_max, U + i + 1)
                        c = 2 * (i % 4)
                        for q, (a, b) in enumerate(((0, P), (P, 384))):
                            last = f(pb[:, i % 4, a:b], pb[:, i % 4, a:b], ACT.Exp, bias=nb[:, c + q:c + q + 1], scale=SCALE,
                                     accum_out=rs[:, c + q:c + q + 1])
                        last.then_inc(p_raw, 1)
                    for pair, u in LAST_OF_PAIR.items():
                        if u + 5 == i:
                            act.wait_ge(pv_full, U + u + 1)
                            f(o2[:, pair * S:(pair + 1) * S], bank[O_BANK[pair % 2]][:, 0:S], ACT.Copy).then_inc(o_ready, 1)

            act.wait_ge(s_c, 16)
            f(c_row, c_row, ACT.Silu).then_inc(c_ready, 1)
            act.wait_ge(s_const, 16)
            norm(0, 0, 1)
            act.wait_ge(raw_zero, 1)
            channel_major(T1, 0, 0)
            for i in range(4):
                act.wait_ge(tm_full, i + 1)
                a, b = ((0, 512), (512, 768))[i // 2]
                f(v1[:, i % 2, a:b], bank[i][:, 0:b - a], ACT.Copy).then_inc(tm_ready, 1)
            act.wait_ge(s_c2, 16)
            f(row[:], row[:], ACT.Silu).then_inc(c_ready, 1)
            attention1()
            rwkv()
            f(c2_row, row[:], ACT.Copy).then_inc(c_ready, 1)
            act.wait_ge(ada_used, FIRST + ADA2_CHUNKS)
            act.wait_ge(c_ready, 3)
            to_row(0)
            channel_major(TG, CM_G, 0)
            rms_of_output(0, DONE_MIX1, BY_COLUMNS)
            norm(1, 1, 2, BY_COLUMNS)
            act.wait_ge(ang_ready, 1)
            f(sin2[:], sin2[:], ACT.Sin)
            f(cos2[:], cos2[:], ACT.Sin).then_inc(trig_ready, 1)
            ffn(0)
            rms_of_output(1, DONE_FFN1, BY_TOKENS, FC)
            with act.Fori(0, LAYERS) as l:
                more = PER_LAYER * l
                norm(2 + 3 * l, 0, 3 + l, split_of=(1 + 2 * l, G_LAYER, 0, 0, 0, more))
                ffn_split(1 + 2 * l, G_LAYER, more)
                norm(3 + 3 * l, 1, 3 + l)
                mixer2(l)
                G_B = G_LAYER + FC + MIX2_CHUNKS
                norm(4 + 3 * l, 2, 3 + l, BY_COLUMNS, split_of=(2 + 2 * l, G_B, 0, 0, 0, more))
                ffn_split(2 + 2 * l, G_B, more)
            norm(8, 0, rows=False)

        @block.vector
        def _(dve):
            v = Steps(dve, dve_step)
            tt, ts, stt = dve.tensor_tensor, dve.tensor_scalar, dve.scalar_tensor_tensor
            mod3 = mod[:].rearrange("p (s j k) -> p s j k", s=3, j=3)

            def angles():
                turn_hi = 6.28125
                turn_lo = 2 * math.pi - turn_hi
                magic = 1.5 * 2.0 ** 23
                dve.wait_ge(s_pos, 16)
                m = turns
                v(dve.tensor_copy(posf, pos_i))
                v.settle()
                v(ts(ang, posf, K("inv_freq2"), None, ALU.mult))
                v.settle()
                for dst, quarter in ((sin2, 0.0), (cos2, 0.25)):
                    v(ts(m, ang, 1 / (2 * math.pi), quarter, ALU.mult, ALU.add))
                    v.settle()
                    v(ts(m, m, magic, None, ALU.add))
                    v.settle()
                    v(ts(m, m, magic, None, ALU.subtract))
                    v.settle()
                    v(stt(posf, m, -turn_hi, ang, ALU.mult, ALU.add))
                    v.settle()
                    v(stt(posf, m, -turn_lo, posf, ALU.mult, ALU.add))
                    v.settle()
                    v(ts(posf, posf, quarter * 2 * math.pi, None, ALU.add))
                    v.settle()
                    last = ts(dst[:], posf, math.pi, -math.pi, ALU.min, ALU.max)
                    v(last)
                    v.settle()
                dve.nop().then_inc(ang_ready, 1)

            def dot(weights, c_of, out):
                return dve.tensor_tensor_reduce(out=weights, in0=weights, in1=c_of, scale=1.0, scalar=0.0, op0=ALU.mult, op1=ALU.add, accum_out=out)

            def ada_first(j):
                if j % 4 == 0:
                    dve.wait_ge(slot_full[j // 4 % 2], full_count(j // 4))
                last = dot(ring[:, j // 4 % 2, (j % 4) * D:(j % 4 + 1) * D], c_row, mod_raw[:, 0, j:j + 1])
                if j % 4 == 3:
                    last.then_inc(ada_used, 1)

            def ada_beside(j):
                dve.wait_ge(apart_full[j % 4], 16 * (j // 4 + 1))
                dot(ada_tile[:, j % 4], c_row, mod_raw[:, 0, 4 * FIRST + j:4 * FIRST + j + 1]).then_inc(apart_used, 1)

            def ada_last(tiles):
                for j in tiles:
                    if j % 4 == 0:
                        dve.wait_ge(slot_full[j // 4 % 2], full_count(G_ADA + j // 4))
                    last = dot(ring[:, j // 4 % 2, (j % 4) * D:(j % 4 + 1) * D], row[:], mod_raw[:, LAYERS, j:j + 1])
                    if j % 4 == 3:
                        last.then_inc(ada_used, 1)

            def ada_next(c, i=0):
                sums = pre[:, c % 2, 0:8]
                for s in range(2):
                    slot = 2 * (c % 2) + s
                    dve.wait_ge(apart_full[slot], 128 + 16 * ((c - 2) // 2 + 1) + 8 * i)
                    for j in range(4):
                        last = dot(ada_slot[:, slot, j * D:(j + 1) * D], c2_row, sums[:, 4 * s + j:4 * s + j + 1])
                    last.then_inc(apart_used, 1)
                dve.wait_ge(apart_used, 32 + 2 * (c - 1) + 2 * i)
                dve.tensor_copy(mod_raw[:, 1, bass.ds(8 * (c - 2) + 8 * i, 8)], sums).then_inc(sums_kept, 1)

            def low_up(f, g, c, h, i=0):
                dve.wait_ge(up_high, 2 * FC * (f - 1) + 2 * c + h + 1 + 2 * i)
                tt(up_lo[:, h], ring[:, (g + c) % 2, h * 2048:(h + 1) * 2048], up_hi[:, h].bitcast(F32), ALU.subtract).then_inc(up_low, 1)

            def ffn_split(f, g, n):
                def one(c, i=0):
                    if c < FC - 1:
                        low_up(f, g, c + 1, 0, i)
                    dve.wait_ge(silu_ready, FC * f + c + i + 1)
                    whole = act_t[:, c % 2].rearrange("p k n -> p (k n)")
                    tt(whole, silu[:, c % 2], bank[5 + 2 * (c % 2)], ALU.mult).then_inc(act_ready, 1)
                    dve.wait_ge(act_ready, FC * f + c + i + 1)
                    if c >= 2:
                        dve.wait_ge(down_done, FC * f + c + i - 1)
                    dve.tensor_copy(act_hi[:, c % 2], whole).then_inc(act_high, 1)
                    dve.wait_ge(act_high, FC * (f - 1) + c + i + 1)
                    tt(act_lo[:, c % 2], whole, act_hi[:, c % 2].bitcast(F32), ALU.subtract).then_inc(act_low, 1)
                    if c < FC - 1:
                        low_up(f, g, c + 1, 1, i)
                    dve.wait_ge(dn_high, FC * (f - 1) + c + i + 1)
                    tt(dn_lo, ring_down[:, c % 2], dn_hi.bitcast(F32), ALU.subtract).then_inc(dn_low, 1)

                dve.wait_ge(ht_dve, n + 1)
                tt(h_lo[:, 4:8], hT[:, 4:8], h_hi[:, 4:8].bitcast(F32), ALU.subtract).then_inc(h_low_last, 1)
                low_up(f, g, 0, 1)
                one(0)
                one(1)
                with dve.Fori(0, FC - 3, 2) as i:
                    one(2, i)
                    one(3, i)
                one(FC - 1)

            def norm(n, sub, rows=True, ahead=None, split_of=None):
                dve.wait_ge(ss_ready, 4 * n + 4)
                quarters = stat[:, 20:24].rearrange("p (t h) -> p t h", t=2)
                v(tt(stat[:, 0:2], quarters[:, :, 0], quarters[:, :, 1], ALU.add))
                v.settle()
                ts(stat[:, 2:4], stat[:, 0:2], 1.0 / D, EPS, ALU.mult, ALU.add).then_inc(ms_ready, 1)
                dve.wait_ge(sd_ready, n + 1)
                v(dve.reciprocal(stat[:, 6:8], stat[:, 4:6]))
                v.settle()
                for t in range(NT):
                    ts(xn[:, t], x[:, t], stat[:, 6 + t:7 + t], None, ALU.mult).then_inc(xn_ready, 1)
                if not rows:
                    return
                if split_of is not None:
                    low_up(*split_of)
                if ahead:
                    ahead()
                for b in range(2, 4):
                    dve.wait_ge(ht_full, 4 * n + b + 1)
                    for k in (2 * b, 2 * b + 1):
                        last = ts(hT[:, k], bank[4 + b][:, (k % 2) * S:(k % 2 + 1) * S], mod_scale[:, sub, k:k + 1],
                                  mod[:, 24 * sub + k:24 * sub + k + 1], ALU.mult, ALU.add)
                        if split_of is not None:
                            last = ts(h_hi[:, k], bank[4 + b][:, (k % 2) * S:(k % 2 + 1) * S], mod_scale[:, sub, k:k + 1],
                                      mod[:, 24 * sub + k:24 * sub + k + 1], ALU.mult, ALU.add)
                last.then_inc(ht_dve, 1)

            def finish(n, done, order, rms, downs=None):
                dve.wait_ge(row_ready, n + 1)
                if rms:
                    dve.wait_ge(fss_ready, 4 * n + 4)
                    s4 = stat[:, 8:12].rearrange("p (t h) -> p t h", t=2)
                    v(tt(stat[:, 12:14], s4[:, :, 0], s4[:, :, 1], ALU.add))
                    v.settle()
                    ts(stat[:, 12:14], stat[:, 12:14], 1.0 / D, EPS, ALU.mult, ALU.add).then_inc(fms_ready, 1)
                    dve.wait_ge(fsd_ready, n + 1)
                    v(dve.reciprocal(stat[:, 16:18], stat[:, 14:16]))
                    v.settle()
                for i, j in enumerate(order):
                    if i == 3 and downs is not None:
                        dve.wait_ge(down_done, downs)
                    else:
                        dve.wait_ge(bank_full, done + i + 1)
                    wait(dve, x_ready, 4 * n + i - 1)
                    r = row[:, (j % 2) * 512:(j % 2 + 1) * 512]
                    if rms:
                        last = stt(fin[:, i % 2], bank[j], stat[:, 16 + j // 2:17 + j // 2], r, ALU.mult, ALU.mult)
                    else:
                        last = tt(fin[:, i % 2], bank[j], r, ALU.mult)
                    last.then_inc(fin_read, 1)

            def kk_norms(j):
                if j == KK_SCALED:
                    dve.wait_ge(cm_out, 12)
                    for w in range(PAIRS):
                        last = ts(kk[:, w * S:(w + 1) * S], k_t[:, w * S:(w + 1) * S], PR("k_k", w, w + 1), None, ALU.mult)
                    last.then_inc(kk0_ready, 1)
                if j == KK_CLAMPED:
                    dve.wait_ge(kn_full, 1)
                    ts(norm_kk, psum[:, 0:3].rearrange("p b n -> p (b n)"), 1e-24, None, ALU.max).then_inc(kn_clamped, 1)
                if j in KK_INVERTED:
                    dve.wait_ge(kn_sqrt, 1)
                    part = norm_kk[:, KK_INVERTED.index(j) * 512:KK_INVERTED.index(j) * 512 + 512]
                    dve.reciprocal(part, part).then_inc(kn_rec, 1)

            def channel_major(table, base, qbase, rbase):
                for j, (kind, q, r, dest) in enumerate(table):
                    if kind == "shift":
                        dve.wait_ge(cm_pre, q + 1)
                        stt(dest, pre[:, q % 3], PR("mu", j, j + 1), raw[:, q % 3, 1:S + 1], ALU.mult, ALU.add).then_inc(cm_out, 1)
                    elif r is not None:
                        sin = K("sin1") if kind == "rope1" else sin2[:]
                        if kind == "rope2":
                            dve.wait_ge(trig_ready, 1)
                        dve.wait_ge(rope_full, rbase + r + 1)
                        tt(rot[:, r % 2], bank[6 + r % 2][:, 0:S], sin, ALU.mult).then_inc(rope_used, 1)
                        dve.wait_ge(rope_used, rbase + r + 1)
                        dve.wait_ge(cm_pre, qbase + q + 1)
                        tt(dest, rot[:, r % 2], pre[:, q % 3], ALU.add).then_inc(cm_out, 1)
                    if table is T1:
                        ada_beside(j)
                        kk_norms(j)

            def ffn(fn, with_ada=False):
                def one(c, i=0):
                    dve.wait_ge(silu_ready, FC * fn + c + i + 1)
                    wait(dve, down_done, FC * fn + c + i - 1 if c >= 2 else FC * fn)
                    tt(act_t[:, c % 2].rearrange("p k n -> p (k n)"), silu[:, c % 2], bank[5 + 2 * (c % 2)], ALU.mult).then_inc(act_ready, 1)
                    if with_ada and c >= 2:
                        ada_next(c, i)

                one(0)
                one(1)
                with dve.Fori(0, FC - 3, 2) as i:
                    one(2, i)
                    one(3, i)
                one(FC - 1)

            def masked_max(dst, scores, mask, out):
                return dve.tensor_tensor_reduce(out=dst, in0=scores, in1=mask, scale=1.0, scalar=-3e38, op0=ALU.add, op1=ALU.max, accum_out=out)

            def attention1():
                def maxima(i):
                    dve.wait_ge(s1_full, i + 1)
                    wait(dve, s1_t, 3 * (i - 1))
                    c = 8 * (i % 2)
                    for g in range(3):
                        for q, (a, b) in enumerate(((0, P), (P, 384))):
                            v(masked_max(p1[:, i % 2, g, a:b], bank[4 + g][:, a:b], K("dilated", 384 * g + a, 384 * g + b),
                                         mx[:, c + 3 * q + g:c + 3 * q + g + 1]))
                    v.settle()
                    v(dve.tensor_reduce(mx[:, c + 6:c + 8], mx[:, c:c + 6].rearrange("p (q g) -> p q g", q=2), AX.X, ALU.max))
                    v.settle()
                    ts(nb[:, 2 * (i % 2):2 * (i % 2) + 2], mx[:, c + 6:c + 8], -SCALE, None, ALU.mult).then_inc(s1_max, 1)
                dve.wait_ge(c_ready, 2)
                dve.wait_ge(kk_ready, 1)
                maxima(0)
                for i in range(4):
                    ada_last(range(6 * i, 6 * i + 2))
                    dve.wait_ge(s1_exp, i + 1)
                    c = 2 * (i % 2)
                    dve.reciprocal(ri[:, c:c + 2], rs[:, c:c + 2]).then_inc(s1_scale, 1)
                    if i < 3:
                        maxima(i + 1)
                    ada_last(range(6 * i + 2, 6 * i + 6))
                    wait(dve, s1_pv, i)
                    for g in range(3):
                        dve.wait_ge(s1_t, 3 * i + g + 1)
                        dve.tensor_copy(pt1[:, g], bank[(7, 2, 1)[g]][:, 0:384]).then_inc(s1_tr, 1)

            def rwkv():
                col = lambda a, w: a[:, w * S:(w + 1) * S]
                by_chunk = lambda a: a.rearrange("p (c n) -> p c n", c=4)
                for ps in range(PAIRS // 2):
                    for lp in range(2):
                        w = 2 * ps + lp
                        dve.wait_ge(lr_ready, w + 1)
                        for c in range(4):
                            last = dve.tensor_tensor_scan(cs[:, lp, c * C:(c + 1) * C], K("ones", 0, C), sgw[:, w * S + c * C:w * S + (c + 1) * C],
                                                          0.0, ALU.mult, ALU.add)
                        last.then_inc(cs_ready, 1)
                    for lp in range(2):
                        w = 2 * ps + lp
                        v(ts(kbuf[:, lp], col(iclr, w), PR("k_a", w, w + 1), PR("k_a", w, w + 1), ALU.mult, ALU.subtract))
                        v.settle()
                        v(stt(kbuf[:, lp], kbuf[:, lp], 1.0, col(k_t, w), ALU.add, ALU.mult))
                        dve.wait_ge(e_ready, w + 1)
                        p_at = decay[:, lp, :, 1:C + 1]
                        v(tt(kr[:, lp, :, 1].rearrange("p h (c n) -> p h c n", c=2), col(r_t, w).rearrange("p (h c n) -> p h c n", h=2, c=2),
                             p_at.rearrange("p (h c) n -> p h c n", h=2), ALU.mult))
                        v.settle()
                        v(tt(kt[:, lp], kbuf[:, lp], decay_inv[:, lp], ALU.mult))
                        v(stt(cs[:, lp], col(r_t, w), PR("r_k", w, w + 1), kbuf[:, lp], ALU.mult, ALU.mult))
                        v.settle()
                        tt(by_chunk(kbuf[:, lp]), by_chunk(kt[:, lp]), decay[:, lp, :, C:C + 1].broadcast_to([P, 4, C]), ALU.mult).then_inc(dve_prep, 1)
                        dve.wait_ge(bon_full, w + 1)
                        tt(col(r_t, w), bank[3][:, 0:S], col(v_t, w), ALU.mult).then_inc(bon_ready, 1)
                        for h in range(2):
                            n = 2 * w + h
                            dve.wait_ge(tr_full, n + 1)
                            m2 = 2 * lp + h
                            v(dve.tensor_copy(vkb[:, m2].rearrange("p k n -> p (k n)"), bank[2 - h][:, 0:384]))
                            dve.tensor_copy(avk[:, 2 * m2:2 * m2 + 2, HD:P], bank[2 - h][:, 384:512].rearrange("p (e n) -> p e n", e=2)).then_inc(tr_ready, 1)
                            for e in range(2):
                                dve.wait_ge(sc_full, 2 * n + e + 1)
                                m = 2 * m2 + e
                                v(tt(scores[:, m].rearrange("p k n -> p (k n)"), bank[4 + e], K("score_mask"), ALU.mult))
                                tt(inv_x[:, m], bank[6 + e][:, 0:P], K("level1"), ALU.mult).then_inc(sc_read, 1)
                            v.settle()
                            dve.wait_ge(sc_read, 2 * n + 2)
                            tt(inv_x[:, 2 * m2:2 * m2 + 2], inv_x[:, 2 * m2:2 * m2 + 2], ident.unsqueeze(1).broadcast_to([P, 2, P]), ALU.add).then_inc(sc_ready, 1)
                    for j in range(len(LEVELS)):
                        for lp in range(2):
                            q = (ps * len(LEVELS) + j) * 2 + lp
                            dve.wait_ge(p_full, q + 1)
                            flat = lambda a: a[:, 4 * lp:4 * lp + 4].rearrange("p m n -> p (m n)")
                            if j == 0:
                                dve.wait_ge(y0_ready, 2 * (2 * ps + lp) + 2)
                            if j < len(LEVELS) - 1:
                                v(tt(flat(inv_x), flat(inv_x), bank[2 + lp], ALU.subtract))
                            tt(flat(inv_y), flat(inv_y), bank[4 + lp], ALU.subtract).then_inc(xy_ready, 1)
                        ada_last(range(24 + 16 * ps + 3 * j, 24 + 16 * ps + 3 * j + 3))
                    ada_last(range(24 + 16 * ps + 15, 24 + 16 * ps + 16))
                    dve.wait_ge(hg_full, ps + 1)
                    gt = kr[:, :, :, 1].rearrange("p w h n -> p (w h) n")
                    tt(gt, bank[3].rearrange("p (w n) -> p w n", w=4), gt, ALU.add).then_inc(g_ready, 1)
                    dve.wait_ge(zt_full, ps + 1)
                    dve.wait_ge(bd_zero, 1)
                    for lp in range(2):
                        o = lp * S
                        v(dve.tensor_copy(z_s[:, lp, 0], bank[7][:, o:o + HD]))
                        v(dve.tensor_copy(z_s[:, lp, 1], bank[6][:, o + 64:o + 128]))
                        for e in range(2):
                            h, hc = half(e), slice(e * HD, (e + 1) * HD)
                            v(dve.tensor_copy(state[h, lp, 0, hc], bank[6][h, o:o + HD]))
                            for step, src in ((0, bank[7][h, o + 64:o + 128]), (1, bank[6][h, o + 128:o + 192])):
                                last = stt(trans[h, lp, step, hc], K("ident_stack")[h], decay[h, lp, step + 1, C:C + 1], src, ALU.mult, ALU.add)
                                if not (lp == 1 and e == 1 and step == 1):
                                    v(last)
                    last.then_inc(zt_ready, 1)
                    for step in range(2):
                        dve.wait_ge(m_full, 2 * ps + step + 1)
                        for lp in range(2):
                            for e in range(2):
                                h, hc = half(e), slice(e * HD, (e + 1) * HD)
                                last = tt(state[h, lp, step + 1, hc], bank[step][h, lp * P + e * HD:lp * P + (e + 1) * HD], z_s[h, lp, step], ALU.add)
                        last.then_inc(m_ready, 1)
                    dve.wait_ge(yc_full, ps + 1)
                    dve.wait_ge(h_ready, ps + 1)
                    y3 = ymix[:, ps * 512:(ps + 1) * 512].rearrange("p (w n) -> p w n", w=2)[:, :, C:S]
                    tt(y3, bank[4].rearrange("p (w n) -> p w n", w=2)[:, :, C:S], y3, ALU.add).then_inc(pass_done, 1)
                dve.wait_ge(gn_mu, 1)
                stt(dev, psum[:, 0:3].rearrange("p b n -> p (b n)"), -1.0 / HD, ymix, ALU.mult, ALU.add).then_inc(gn_dev, 1)
                dve.wait_ge(gn_var, 1)
                ts(sq, psum[:, 5:8].rearrange("p b n -> p (b n)"), 1.0 / HD, GN_EPS, ALU.mult, ALU.add).then_inc(gn_ms, 1)
                dve.wait_ge(gn_sd, 1)
                dve.reciprocal(sq, sq).then_inc(gn_rs, 1)
                dve.wait_ge(gn_n, 1)
                for w in range(PAIRS):
                    v(ts(col(dev, w), col(dev, w), PR("lnx_w", w, w + 1), PR("lnx_b", w, w + 1), ALU.mult, ALU.add))
                    v.settle()
                    v(tt(col(dev, w), col(dev, w), col(r_t, w), ALU.add))
                    v.settle()
                    tt(col(ymix, w), col(dev, w), col(gate1, w), ALU.mult).then_inc(gn_ready, 1)

            def merge():
                dve.wait_ge(cm_evac, CM_G + 16)
                for n in range(16):
                    dve.wait_ge(ym_full, n + 1)
                    if n < 8:
                        tt(merged[:, n * S:(n + 1) * S], bank[4 + n % 2][:, 0:S], sig[:, (8 + n) * S:(9 + n) * S], ALU.mult).then_inc(ym_read, 1)
                    else:
                        j = n - 8
                        wait(dve, ym_ready, j - 1)
                        tt(ytmp[:, n % 2], bank[4 + n % 2][:, 0:S], sig[:, j * S:(j + 1) * S], ALU.mult).then_inc(ym_read, 1)

            def mod_layer(l):
                dve.wait_ge(s_layers, 16 * (l + 1))
                v(tt(mod[:], mod_raw[:, bass.ds(l + 1, 1)].rearrange("p o n -> p (o n)"), NOW("b_ada"), ALU.add))
                v.settle()
                v(stt(mod_scale[:], mod3[:, :, 1], 1.0, NOW("norm_g").rearrange("p (s k) -> p s k", s=3), ALU.add, ALU.mult))
                v(ts(mod_gate[:, 0:3:2], mod3[:, 0:3:2, 2], 0.5, None, ALU.mult))
                dve.tensor_copy(mod_gate[:, 1], mod3[:, 1, 2]).then_inc(mod_ready, 1)
                dve.wait_ge(mod_ready, 3 + l)

            def mixer2(l):
                base, qbase, rbase, U = CM_2 + 16 * l, Q1 + Q2 * l, R1 + R2 * l, NU * l
                channel_major(T2, base, qbase, rbase)
                dve.wait_ge(swap_full, l + 1)
                dve.wait_ge(cm_evac, base + 16)
                dve.wait_ge(zeroed, 1)
                for i in range(2):
                    for par in range(2):
                        h = half(par)
                        for g in range(2):
                            z = cm2[h, i * S:(i + 1) * S] if g == par else bank[i][h, 0:S]
                            pos = NOW("cmp_pos", 16 * i, 16 * i + 16)[h]
                            for jh in range(2):
                                zz = z.rearrange("p (r j q) -> p j r q", j=8, q=2)[:, :, jh:jh + 15, par]
                                last = tt(zb[h, i, 8 * jh:8 * jh + 8, g, 0:15], zz, pos[:, 8 * jh:8 * jh + 8].unsqueeze(2).broadcast_to([HD, 8, 15]), ALU.add)
                                if not (i == 1 and par == 1 and g == 1 and jh == 1):
                                    v(last)
                last.then_inc(zb_ready, 1)
                dve.wait_ge(tm_ready, 8 + 4 * l)
                xf = ftmp[:, 0:8].rearrange("p (t n) -> p t n", t=2)
                v(tt(xf, v2[:, :, 792:796], NOW("fox_bias").unsqueeze(1).broadcast_to([P, 2, 4]), ALU.add))
                v.settle()
                v(ts(ftmp[:, 32:40], ftmp[:, 0:8], -1.0, None, ALU.mult))
                v.settle()
                tt(ftmp[:, 8:16], ftmp[:, 0:8], ftmp[:, 32:40], ALU.min).then_inc(fx_neg, 1)
                v(ts(ftmp[:, 40:48], ftmp[:, 0:8], 0.0, 1 / SCALE, ALU.min, ALU.mult))
                dve.wait_ge(gate_exp, l + 1)
                v(ts(g2sig, g2sig, 1.0, None, ALU.add))
                v.settle()
                v(dve.reciprocal(g2sig, g2sig))
                dve.wait_ge(fx_ln, l + 1)
                dve.wait_ge(zeroed, 1)
                for rep in range(2):
                    last = stt(lf8[:, :, 64 * rep:64 * rep + 4], ftmp[:, 24:32].rearrange("p (t n) -> p t n", t=2), -1 / SCALE,
                               ftmp[:, 40:48].rearrange("p (t n) -> p t n", t=2), ALU.mult, ALU.add)
                    if rep == 0:
                        v(last)
                last.then_inc(lf_ready, 1)
                dve.wait_ge(gelu_ready, l + 1)
                for h in range(2):
                    last = dve.tensor_copy(ghrep[:, h].rearrange("p (g r c) -> p g r c", g=2, r=4),
                                           gh[:, 1, h].rearrange("p (g c) -> p g c", g=2).unsqueeze(2).broadcast_to([P, 2, 4, 16]))
                    if h == 0:
                        v(last)
                last.then_inc(ghrep_ready, 1)
                dve.wait_ge(cmp2_full, l + 1)
                v(dve.tensor_copy(kcmp, bank[3][:, 0:16]))
                tt(vblk, bank[3][:, 64:128].unsqueeze(1).broadcast_to([P, 8, HD]), K("cmp_block").unsqueeze(2).broadcast_to([P, 8, HD]),
                   ALU.mult).then_inc(cmp_ready, 1)
                dve.wait_ge(f_full, l + 1)
                v(dve.tensor_copy(f_pos, bank[2][:, 0:S]))
                ts(f_neg, bank[2][:, 0:S], -1.0, None, ALU.mult).then_inc(f_ready, 1)
                dve.wait_ge(cs_full, l + 1)
                csm4 = csm.rearrange("p (t h c) -> p t h c", t=2, h=8)
                for e in range(2):
                    v(tt(csm4[:, :, 4 * e:4 * e + 4], bank[e][:, 0:128].rearrange("p (t h c) -> p t h c", t=2, h=4),
                         K("cmp_add").rearrange("p (t c) -> p t c", t=2).unsqueeze(2).broadcast_to([P, 2, 4, 16]), ALU.add))
                v.settle()
                csm3 = csm.rearrange("p (h c) -> p h c", c=16)
                v(dve.tensor_reduce(cst[:, 0:16], csm3, AX.X, ALU.max))
                v.settle()
                tt(csm3, csm3, cst[:, 0:16].unsqueeze(2).broadcast_to([P, 16, 16]), ALU.subtract).then_inc(cs_sub, 1)
                dve.wait_ge(cs_exp, l + 1)
                v(tt(csm4, csm4, K("cmp_keep").rearrange("p (t c) -> p t c", t=2).unsqueeze(2).broadcast_to([P, 2, 8, 16]), ALU.mult))
                v.settle()
                v(dve.tensor_reduce(cst[:, 16:32], csm3, AX.X, ALU.add))
                v.settle()
                v(ts(cst[:, 16:32], cst[:, 16:32], 1e-30, None, ALU.max))
                v.settle()
                v(dve.reciprocal(cst[:, 32:48], cst[:, 16:32]))
                v.settle()
                v(tt(cst[:, 48:64].rearrange("p (t h) -> p t h", t=2), cst[:, 32:48].rearrange("p (t h) -> p t h", t=2), g2sig[:, :, 0:24:3], ALU.mult))
                v.settle()
                tt(csm3, csm3, cst[:, 48:64].unsqueeze(2).broadcast_to([P, 16, 16]), ALU.mult).then_inc(cs_prob, 1)

                for i in range(NU + 3):
                    if i < NU:
                        dve.wait_ge(s_full, U + i + 1)
                        wait(dve, t_full, behind(U, i - 3))
                        dve.memset(mx[:, 16:17], 0.0)
                        c = 2 * (i % 4)
                        b = bank[S_BANK[i % 3]]
                        v(masked_max(pb[:, i % 4, 0:P], b[:, 0:P], K("causal", P, S), mx[:, c:c + 1]))
                        v(masked_max(pb[:, i % 4, P:384], b[:, P:384], K("causal"), mx[:, c + 1:c + 2]))
                        v.settle()
                        ts(nb[:, c:c + 2], mx[:, c:c + 2], -SCALE, None, ALU.mult).then_inc(s_max, 1)
                    if 1 <= i < NU + 1:
                        u = i - 1
                        c = 2 * (u % 4)
                        gate = UNITS[u][5]
                        dve.wait_ge(p_raw, U + u + 1)
                        if gate is None:
                            dve.reciprocal(ri[:, c:c + 2], rs[:, c:c + 2]).then_inc(r_scale, 1)
                        else:
                            v(dve.reciprocal(ri[:, 8 + c:10 + c], rs[:, c:c + 2]))
                            v.settle()
                            tt(ri[:, c:c + 2], ri[:, 8 + c:10 + c], g2sig[:, :, gate], ALU.mult).then_inc(r_scale, 1)
                    if i >= 3:
                        u = i - 3
                        dve.wait_ge(t_full, U + u + 1)
                        wait(dve, pv_full, behind(U, u - 1))
                        dve.tensor_copy(pt[:, u % 2], bank[T_BANK[u % 2]][:, 0:384]).then_inc(t_ready, 1)

            dve.wait_ge(c_ready, 1)
            for j in range(4 * FIRST):
                ada_first(j)
            dve.wait_ge(s_params, 16)
            dve.wait_ge(ada_used, FIRST)
            v(tt(mod[:, 0:16], mod_raw[:, 0, 0:16], PR("b_ada1", 0, 16), ALU.add))
            v.settle()
            stt(mod_scale[:, 0], mod3[:, 0, 1], 1.0, PR("g_norm", 0, KD), ALU.add, ALU.mult).then_inc(mod_ready, 1)
            dve.wait_ge(s_const, 16)
            norm(0, 0)
            channel_major(T1, 0, 0, 0)
            dve.wait_ge(apart_used, 4 * 8)
            v(tt(mod[:, 16:48], mod_raw[:, 0, 16:48], PR("b_ada1", 16, 48), ALU.add))
            v.settle()
            v(stt(mod_scale[:, 1], mod3[:, 1, 1], 1.0, PR("g_norm", KD, 2 * KD), ALU.add, ALU.mult))
            tt(mod_gate[:, 0:2], mod3[:, 0:2, 2], PR("g_post").rearrange("p (s k) -> p s k", s=2), ALU.mult).then_inc(mod_ready, 1)
            attention1()
            rwkv()
            merge()
            finish(0, DONE_MIX1, BY_COLUMNS, True)
            norm(1, 1)
            angles()
            ffn(0, True)
            dve.wait_ge(sums_kept, ADA2_CHUNKS // 2)
            finish(1, DONE_FFN1, BY_TOKENS, True, FC)
            with dve.Fori(0, LAYERS) as l:
                v.enter(l, DVE_STEPS_PER_LAYER)
                G_B = G_LAYER + FC + MIX2_CHUNKS
                norm(2 + 3 * l, 0, ahead=lambda: mod_layer(l), split_of=(1 + 2 * l, G_LAYER, 0, 0))
                ffn_split(1 + 2 * l, G_LAYER, 2 + 3 * l)
                finish(2 + 3 * l, DONE_A + PER_LAYER_DONE * l, BY_TOKENS, False, FC * (2 + 2 * l))
                norm(3 + 3 * l, 1)
                mixer2(l)
                finish(3 + 3 * l, DONE_MIX2 + PER_LAYER_DONE * l, BY_COLUMNS, False)
                norm(4 + 3 * l, 2, split_of=(2 + 2 * l, G_B, 0, 0))
                ffn_split(2 + 2 * l, G_B, 4 + 3 * l)
                finish(4 + 3 * l, DONE_B + PER_LAYER_DONE * l, BY_TOKENS, False, FC * (3 + 2 * l))
                v.leave(LAYERS)
            norm(8, 0, rows=False)
            dve.wait_ge(row_ready, 9)
            dve.wait_ge(xn_ready, 18)
            for t in range(NT):
                tt(xn[:, t], xn[:, t], row[:], ALU.mult).then_inc(y_ready, 1)

        @block.gpsimd
        def _(pool):
            g = Steps(pool, pool_step)
            tt, ts = pool.tensor_tensor, pool.tensor_scalar

            def channel_major(table, base, qbase):
                for j, (kind, q, _, _) in enumerate(table):
                    if q is None:
                        continue
                    pool.wait_ge(cm_evac, base + j + 1)
                    wait(pool, cm_out, since(qbase, q - 2))
                    if kind == "shift":
                        tt(pre[:, q % 3], raw[:, q % 3, 0:S], raw[:, q % 3, 1:S + 1], ALU.subtract).then_inc(cm_pre, 1)
                    else:
                        if kind == "rope2":
                            pool.wait_ge(trig_ready, 1)
                        cos = K("cos1") if kind == "rope1" else cos2[:]
                        tt(pre[:, q % 3], raw[:, q % 3, 1:S + 1], cos, ALU.mult).then_inc(cm_pre, 1)
                    if table is T1 and j == KK_SQUARED:
                        pool.wait_ge(kk0_ready, 1)
                        tt(norm_kk, kk, kk, ALU.mult).then_inc(sq_ready, 1)
                    if table is T1 and j == KK_DONE:
                        pool.wait_ge(kn_rec, 3)
                        tt(kk, kk, norm_kk, ALU.mult).then_inc(kk_ready, 1)

            def add(n, order):
                for i, j in enumerate(order):
                    pool.wait_ge(fin_read, 4 * n + i + 1)
                    dst = x[:, j // 2, (j % 2) * 512:(j % 2 + 1) * 512]
                    tt(dst, dst, fin[:, i % 2], ALU.add).then_inc(x_ready, 1)

            def attention1():
                for i in range(4):
                    pool.wait_ge(s1_scale, i + 1)
                    c = 2 * (i % 2)
                    for q, (a, b) in enumerate(((0, P), (P, 384))):
                        last = ts(p1[:, i % 2, :, a:b], p1[:, i % 2, :, a:b], ri[:, c + q:c + q + 1], None, ALU.mult)
                    last.then_inc(s1_prob, 1)

            def rwkv():
                col = lambda a, w: a[:, w * S:(w + 1) * S]
                by_chunk = lambda a: a.rearrange("p (c n) -> p c n", c=4)
                pool.wait_ge(cm_out, Q1)
                g(pool.memset(pre[:], 0.0))
                g(pool.memset(rot[:], 0.0))
                pool.memset(decay[:, :, :, 0:1], 1.0).then_inc(bd_zero, 1)
                for ps in range(PAIRS // 2):
                    wait(pool, pass_done, ps)
                    for lp in range(2):
                        w = 2 * ps + lp
                        pool.wait_ge(lr_ready, w + 1)
                        g(tt(bbuf[:, lp], col(kk, w), col(iclr, w), ALU.mult))
                        pool.wait_ge(e_ready, w + 1)
                        g(tt(kr[:, lp, :, 0].rearrange("p h (c n) -> p h c n", c=2), col(kk, w).rearrange("p (h c n) -> p h c n", h=2, c=2),
                             decay[:, lp, :, 0:C].rearrange("p (h c) n -> p h c n", h=2), ALU.mult))
                        g.settle()
                        g(tt(bt[:, lp], bbuf[:, lp], decay_inv[:, lp], ALU.mult))
                        g.settle()
                        tt(by_chunk(bbuf[:, lp]), by_chunk(bt[:, lp]), decay[:, lp, :, C:C + 1].broadcast_to([P, 4, C]), ALU.mult).then_inc(pool_prep, 1)
                    for n in range(4):
                        pool.wait_ge(sc_ready, 4 * ps + n + 1)
                        pair = slice(2 * n, 2 * n + 2)
                        g(tt(inv_y[:, pair], scores[:, pair, 0], K("level1_t").unsqueeze(1).broadcast_to([P, 2, P]), ALU.mult))
                        g.settle()
                        tt(inv_y[:, pair], inv_y[:, pair], ident.unsqueeze(1).broadcast_to([P, 2, P]), ALU.add).then_inc(y0_ready, 1)
                    for j in range(len(LEVELS)):
                        for lp in range(2):
                            q = (ps * len(LEVELS) + j) * 2 + lp
                            wait(pool, w_full, q - 1)
                            four = slice(4 * lp, 4 * lp + 4)
                            tt(inv_n[:, four], scores[:, four, 0], K("levels_t", j * P, (j + 1) * P).unsqueeze(1).broadcast_to([P, 4, P]),
                               ALU.mult).then_inc(nl_ready, 1)
                pool.wait_ge(gn_dev, 1)
                tt(sq, dev, dev, ALU.mult).then_inc(gn_sq, 1)
                pool.wait_ge(gn_rs, 1)
                tt(dev, dev, sq, ALU.mult).then_inc(gn_n, 1)

            pool.memset(raw[:], 0.0).then_inc(raw_zero, 1)
            pool.wait_ge(raw_zero, 1)
            pool.wait_ge(s_const, 16)
            channel_major(T1, 0, 0)
            attention1()
            rwkv()
            for j in range(8):
                pool.wait_ge(ym_read, 9 + j)
                tt(merged[:, j * S:(j + 1) * S], merged[:, j * S:(j + 1) * S], ytmp[:, j % 2], ALU.add).then_inc(ym_ready, 1)
            add(0, BY_COLUMNS)
            add(1, BY_TOKENS)
            g(pool.memset(zb, 0.0))
            pool.memset(lf8, 0.0).then_inc(zeroed, 1)
            def low_h(f, n):
                pool.wait_ge(ht_act, n + 1)
                tt(h_lo[:, 0:4], hT[:, 0:4], h_hi[:, 0:4].bitcast(F32), ALU.subtract).then_inc(h_low, 1)

            with pool.Fori(0, LAYERS) as l:
                low_h(1 + 2 * l, 2 + 3 * l)
                add(2 + 3 * l, BY_TOKENS)
                channel_major(T2, CM_2 + 16 * l, Q1 + Q2 * l)
                U = NU * l
                for u in range(NU):
                    pool.wait_ge(r_scale, U + u + 1)
                    c = 2 * (u % 4)
                    for q, (a, b) in enumerate(((0, P), (P, 384))):
                        last = tt(pb[:, u % 4, a:b], pb[:, u % 4, a:b], ri[:, c + q:c + q + 1].broadcast_to([P, b - a]), ALU.mult)
                    last.then_inc(p_ready, 1)
                add(3 + 3 * l, BY_COLUMNS)
                low_h(2 + 2 * l, 4 + 3 * l)
                add(4 + 3 * l, BY_TOKENS)


def program(nc, arrays):
    T = {n: nc.dram_tensor(f"in_{n}", a.shape, mybir.dt.from_np(a.dtype), kind="ExternalInput").ap() for n, a in arrays.items()}
    out = nc.dram_tensor("out_0", (P, NT, D), F32, kind="ExternalOutput").ap()
    build(nc, T, out)


def kernel(**inputs):
    import concourse.bacc as bacc
    from concourse.bass_utils import run_bass_kernel_spmd

    nc = bacc.Bacc("TRN2", target_bir_lowering=False, num_devices=1)
    arrays = {n: np.ascontiguousarray(a) for n, a in layout(inputs).items()}
    program(nc, arrays)
    r = run_bass_kernel_spmd(nc, [{f"in_{n}": a for n, a in arrays.items()}], core_ids=[0])
    return r.results[0]["out_0"].reshape(P, NT, D).transpose(1, 0, 2).reshape(1, NT * P, D)
```
